# Optimizing a Trainium2 kernel written in Bass

```python
import math
import jax
import jax.numpy as jnp
from jax import lax
import numpy as np
import jax, jax.numpy as jnp

D_MODEL = 2048
BATCH = 1
SEQ = 256
DEPTH = 1

D_ATTN = D_MODEL // 2
D_SSM = D_MODEL // 2

NSA_HEADS = 16
NSA_KV_HEADS = 2
NSA_GROUP = NSA_HEADS // NSA_KV_HEADS
HEAD_DIM = D_ATTN // NSA_HEADS
CMP_BLOCK = 32
CMP_STRIDE = 16
CMP_HIDDEN = 4 * HEAD_DIM
SLC_BLOCK = 64
SLC_TOPN = 16
WINDOW = 512
Q_BLOCK = 128
FORCE_SCORE = 1e4
NEG_INF = -1e30

REL_BUCKETS = 32
REL_MAX_DIST = 2048

SSM_HEAD_DIM = 64
SSM_HEADS = D_SSM // SSM_HEAD_DIM
SSM_GROUPS = 2
SSM_STATE = 128
CONV_WIDTH = 4
CONV_CH = D_SSM + 2 * SSM_GROUPS * SSM_STATE
SSM_CHUNK = 256

PEER_HEADS = 8
PEER_NKEYS = 128
PEER_EXPERTS = PEER_NKEYS * PEER_NKEYS
PEER_KEY_DIM = 256
PEER_TOPK = 16
PEER_TOKEN_BLOCK = 128

N_Q = NSA_HEADS * HEAD_DIM
N_KV = 6 * NSA_KV_HEADS * HEAD_DIM
N_GATE = 3 * NSA_HEADS
N_Z = D_SSM
N_XBC = CONV_CH
N_DT = SSM_HEADS
N_IN = N_Q + N_KV + N_GATE + N_Z + N_XBC + N_DT

RMS_EPS = 1e-6


def rms_norm(x, w):
    xf = x.astype(jnp.float32)
    y = xf * lax.rsqrt(jnp.mean(xf * xf, axis=-1, keepdims=True) + RMS_EPS)
    return (y * w.astype(jnp.float32)).astype(x.dtype)

def masked_softmax(s, mask):
    p = jax.nn.softmax(jnp.where(mask, s.astype(jnp.float32), NEG_INF), axis=-1)
    return jnp.where(mask, p, 0.0)

def rel_bucket(diff):
    dist = jnp.maximum(diff, 0)
    max_exact = REL_BUCKETS // 2
    log_ratio = jnp.log(jnp.maximum(dist, max_exact).astype(jnp.float32) / max_exact) / math.log(REL_MAX_DIST / max_exact)
    large = max_exact + (log_ratio * (REL_BUCKETS - max_exact)).astype(jnp.int32)
    return jnp.where(dist < max_exact, dist, jnp.minimum(large, REL_BUCKETS - 1))

def compress_blocks(k, pe, w1, w2):
    bsz, s = k.shape[0], k.shape[1]
    n_cmp = (s - CMP_BLOCK) // CMP_STRIDE + 1
    idx = np.arange(n_cmp)[:, None] * CMP_STRIDE + np.arange(CMP_BLOCK)[None, :]
    blocks = k[:, idx] + pe[None, None, :, None, :]
    flat = blocks.transpose(0, 1, 3, 2, 4).reshape(bsz, n_cmp, NSA_KV_HEADS, CMP_BLOCK * HEAD_DIM)
    return jax.nn.gelu(flat @ w1) @ w2

def nsa_attention(q, kv, gate_logits, cmp_pe, cmp_w1, cmp_w2, rel_bias):
    bsz, s, _ = q.shape
    f32 = jnp.float32
    q = q.reshape(bsz, s, NSA_KV_HEADS, NSA_GROUP, HEAD_DIM)
    kv = kv.reshape(bsz, s, 6, NSA_KV_HEADS, HEAD_DIM)
    k_cmp_raw, v_cmp_raw, k_slc, v_slc, k_win, v_win = [kv[:, :, i] for i in range(6)]
    gates = jax.nn.sigmoid(gate_logits.astype(f32)).reshape(bsz, s, NSA_KV_HEADS, NSA_GROUP, 3).astype(q.dtype)

    n_cmp = (s - CMP_BLOCK) // CMP_STRIDE + 1
    k_cmp = compress_blocks(k_cmp_raw, cmp_pe[0], cmp_w1[0], cmp_w2[0])
    v_cmp = compress_blocks(v_cmp_raw, cmp_pe[1], cmp_w1[1], cmp_w2[1])
    cmp_end = jnp.arange(n_cmp) * CMP_STRIDE + CMP_BLOCK - 1

    n_slc = s // SLC_BLOCK
    n_sel = min(SLC_TOPN, n_slc)
    k_blocks = k_slc.reshape(bsz, n_slc, SLC_BLOCK, NSA_KV_HEADS, HEAD_DIM).transpose(0, 3, 1, 2, 4)
    v_blocks = v_slc.reshape(bsz, n_slc, SLC_BLOCK, NSA_KV_HEADS, HEAD_DIM).transpose(0, 3, 1, 2, 4)
    j = np.arange(n_slc)
    lo = np.clip((j * SLC_BLOCK - CMP_BLOCK) // CMP_STRIDE + 1, 0, n_cmp)
    hi = np.clip(-((-(j * SLC_BLOCK + SLC_BLOCK)) // CMP_STRIDE), 0, n_cmp)
    blk = jnp.arange(n_slc)

    pad = ((0, 0), (WINDOW, 0), (0, 0), (0, 0))
    k_win_p = jnp.pad(k_win, pad)
    v_win_p = jnp.pad(v_win, pad)

    rel_kg = rel_bias.reshape(REL_BUCKETS, NSA_KV_HEADS, NSA_GROUP)
    b_idx = jnp.arange(bsz)[:, None, None, None]
    h_idx = jnp.arange(NSA_KV_HEADS)[None, :, None, None]
    kv_idx = jnp.arange(NSA_KV_HEADS)[None, :, None, None, None, None]
    g_idx = jnp.arange(NSA_GROUP)[None, None, :, None, None, None]
    scale = HEAD_DIM ** -0.5

    def head_bias(diff):
        return rel_kg[rel_bucket(diff)].transpose(2, 3, 0, 1)

    def query_block(i):
        qs = i * Q_BLOCK
        t = qs + jnp.arange(Q_BLOCK)
        qb = lax.dynamic_slice_in_dim(q, qs, Q_BLOCK, axis=1)
        gb = lax.dynamic_slice_in_dim(gates, qs, Q_BLOCK, axis=1)

        s_c = jnp.einsum('bqkgd,bnkd->bkgqn', qb, k_cmp).astype(f32) * scale + head_bias(t[:, None] - cmp_end[None, :])
        p_c = masked_softmax(s_c, cmp_end[None, :] <= t[:, None])
        o_c = jnp.einsum('bkgqn,bnkd->bqkgd', p_c.astype(qb.dtype), v_cmp)

        cs = jnp.pad(jnp.cumsum(p_c.sum(axis=2), axis=-1), ((0, 0), (0, 0), (0, 0), (1, 0)))
        imp = cs[..., hi] - cs[..., lo]
        cur = (t // SLC_BLOCK)[:, None]
        forced = (blk == 0) | (blk == cur) | (blk == cur - 1)
        imp = jnp.where(forced, FORCE_SCORE, jnp.where(blk <= cur, imp, -FORCE_SCORE))
        _, sel = lax.top_k(imp, n_sel)

        k_sel = k_blocks[b_idx, h_idx, sel]
        v_sel = v_blocks[b_idx, h_idx, sel]
        pos_s = sel[..., None] * SLC_BLOCK + jnp.arange(SLC_BLOCK)
        diff_s = t[:, None, None] - pos_s
        bias_s = rel_kg[rel_bucket(diff_s)[:, :, None], kv_idx, g_idx]
        s_s = jnp.einsum('bqkgd,bkqnld->bkgqnl', qb, k_sel).astype(f32) * scale + bias_s
        s_s = s_s.reshape(bsz, NSA_KV_HEADS, NSA_GROUP, Q_BLOCK, n_sel * SLC_BLOCK)
        mask_s = (diff_s >= 0).reshape(bsz, NSA_KV_HEADS, Q_BLOCK, n_sel * SLC_BLOCK)[:, :, None]
        p_s = masked_softmax(s_s, mask_s)
        o_s = jnp.einsum('bkgqm,bkqmd->bqkgd', p_s.astype(qb.dtype),
                         v_sel.reshape(bsz, NSA_KV_HEADS, Q_BLOCK, n_sel * SLC_BLOCK, HEAD_DIM))

        kw = lax.dynamic_slice_in_dim(k_win_p, qs, WINDOW + Q_BLOCK, axis=1)
        vw = lax.dynamic_slice_in_dim(v_win_p, qs, WINDOW + Q_BLOCK, axis=1)
        pos_w = qs - WINDOW + jnp.arange(WINDOW + Q_BLOCK)
        diff_w = t[:, None] - pos_w[None, :]
        mask_w = (diff_w >= 0) & (diff_w < WINDOW) & (pos_w[None, :] >= 0)
        s_w = jnp.einsum('bqkgd,bmkd->bkgqm', qb, kw).astype(f32) * scale + head_bias(diff_w)
        p_w = masked_softmax(s_w, mask_w)
        o_w = jnp.einsum('bkgqm,bmkd->bqkgd', p_w.astype(qb.dtype), vw)

        return gb[..., 0:1] * o_c + gb[..., 1:2] * o_s + gb[..., 2:3] * o_w

    out = lax.map(query_block, jnp.arange(s // Q_BLOCK))
    return out.transpose(1, 0, 2, 3, 4, 5).reshape(bsz, s, NSA_HEADS * HEAD_DIM)

def causal_depthwise_conv(u, w, b):
    ch = u.shape[-1]
    out = lax.conv_general_dilated(u, w[:, None, :].astype(u.dtype), window_strides=(1,),
                                   padding=[(CONV_WIDTH - 1, 0)],
                                   dimension_numbers=('NWC', 'WIO', 'NWC'),
                                   feature_group_count=ch)
    return out + b

def ssd_chunked_scan(x, dt, a, bmat, cmat):
    f32 = jnp.float32
    bsz, s, nh, p = x.shape
    ng, ns = bmat.shape[2], bmat.shape[3]
    nj = nh // ng
    pad = (-s) % SSM_CHUNK
    sp = s + pad
    nc = sp // SSM_CHUNK
    ln = SSM_CHUNK

    def padc(u):
        return jnp.pad(u, [(0, 0), (0, pad)] + [(0, 0)] * (u.ndim - 2))

    def chunks(u):
        return jnp.moveaxis(u.reshape((bsz, nc, ln) + u.shape[2:]), 1, 0)

    xc = chunks(padc(x.astype(f32)).reshape(bsz, sp, ng, nj, p))
    dtc = chunks(padc(dt).reshape(bsz, sp, ng, nj))
    bc = chunks(padc(bmat.astype(f32)))
    cc = chunks(padc(cmat.astype(f32)))
    a_gj = a.reshape(ng, nj)
    causal = jnp.tril(jnp.ones((ln, ln), bool))[None, :, :, None, None]

    def step(state, inp):
        xk, dtk, bk, ck = inp
        acs = jnp.cumsum(dtk * a_gj, axis=1)
        seg = acs[:, :, None] - acs[:, None, :]
        decay = jnp.exp(jnp.where(causal, seg, -jnp.inf))
        cb = jnp.einsum('blgn,bsgn->blsg', ck, bk)
        m = cb[..., None] * decay * dtk[:, None]
        y = jnp.einsum('blsgj,bsgjp->blgjp', m, xk)
        y = y + jnp.einsum('blgn,bgjpn->blgjp', ck, state) * jnp.exp(acs)[..., None]
        last = acs[:, -1]
        w = jnp.exp(last[:, None] - acs) * dtk
        state = state * jnp.exp(last)[..., None, None] + jnp.einsum('bsgj,bsgn,bsgjp->bgjpn', w, bk, xk)
        return state, y

    state0 = jnp.zeros((bsz, ng, nj, p, ns), f32)
    _, ys = lax.scan(step, state0, (xc, dtc, bc, cc))
    ys = jnp.moveaxis(ys, 0, 1).reshape(bsz, sp, nh, p)
    return ys[:, :s]

def mamba2_ssd(z, xbc, dt_raw, conv_w, conv_b, dt_bias, a_log, d_skip, norm_w):
    bsz, s, _ = z.shape
    f32 = jnp.float32
    xbc = jax.nn.silu(causal_depthwise_conv(xbc, conv_w, conv_b))
    xs, bm, cm = jnp.split(xbc, [D_SSM, D_SSM + SSM_GROUPS * SSM_STATE], axis=-1)
    xs = xs.reshape(bsz, s, SSM_HEADS, SSM_HEAD_DIM)
    bm = bm.reshape(bsz, s, SSM_GROUPS, SSM_STATE)
    cm = cm.reshape(bsz, s, SSM_GROUPS, SSM_STATE)
    dt = jax.nn.softplus(dt_raw.astype(f32) + dt_bias.astype(f32))
    a = -jnp.exp(a_log.astype(f32))
    y = ssd_chunked_scan(xs, dt, a, bm, cm)
    y = y + d_skip.astype(f32)[:, None] * xs.astype(f32)
    gw = D_SSM // SSM_GROUPS
    y = y.reshape(bsz, s, SSM_GROUPS, gw) * jax.nn.silu(z.astype(f32)).reshape(bsz, s, SSM_GROUPS, gw)
    y = y * lax.rsqrt(jnp.mean(y * y, axis=-1, keepdims=True) + RMS_EPS)
    return (y.reshape(bsz, s, D_SSM) * norm_w.astype(f32)).astype(z.dtype)

def hybrid_mixer(h, w_in, cmp_pe, cmp_w1, cmp_w2, rel_bias, attn_out_norm,
                 conv_w, conv_b, dt_bias, a_log, d_skip, ssm_norm, w_out):
    proj = h @ w_in
    cuts = [int(v) for v in np.cumsum([N_Q, N_KV, N_GATE, N_Z, N_XBC])]
    q, kv, gate_logits, z, xbc, dt_raw = jnp.split(proj, cuts, axis=-1)
    attn = rms_norm(nsa_attention(q, kv, gate_logits, cmp_pe, cmp_w1, cmp_w2, rel_bias), attn_out_norm)
    ssm = mamba2_ssd(z, xbc, dt_raw, conv_w, conv_b, dt_bias, a_log, d_skip, ssm_norm)
    return jnp.concatenate([attn, ssm], axis=-1) @ w_out

def peer_ffn(h, wq, subkeys, u_tab, v_tab):
    bsz, s, d = h.shape
    f32 = jnp.float32
    q = (h @ wq).reshape(bsz, s, PEER_HEADS, 2, PEER_KEY_DIM // 2)
    s1 = jnp.einsum('bshd,kd->bshk', q[:, :, :, 0], subkeys[0]).astype(f32)
    s2 = jnp.einsum('bshd,kd->bshk', q[:, :, :, 1], subkeys[1]).astype(f32)
    v1, i1 = lax.top_k(s1, PEER_TOPK)
    v2, i2 = lax.top_k(s2, PEER_TOPK)
    n_cand = PEER_TOPK * PEER_TOPK
    cand = (v1[..., :, None] + v2[..., None, :]).reshape(bsz, s, PEER_HEADS, n_cand)
    cidx = (i1[..., :, None] * PEER_NKEYS + i2[..., None, :]).reshape(bsz, s, PEER_HEADS, n_cand)
    best, pos = lax.top_k(cand, PEER_TOPK)
    eidx = jnp.take_along_axis(cidx, pos, axis=-1)
    gate = jax.nn.softmax(best, axis=-1).astype(h.dtype)
    n_blk = bsz * s // PEER_TOKEN_BLOCK
    hb = h.reshape(n_blk, PEER_TOKEN_BLOCK, d)
    eb = eidx.reshape(n_blk, PEER_TOKEN_BLOCK, PEER_HEADS * PEER_TOPK)
    gb = gate.reshape(n_blk, PEER_TOKEN_BLOCK, PEER_HEADS * PEER_TOPK)

    def expert_block(args):
        hx, ex, gx = args
        act = jax.nn.gelu(jnp.einsum('td,tkd->tk', hx, u_tab[ex]))
        return jnp.einsum('tk,tkd->td', act * gx, v_tab[ex])

    return lax.map(expert_block, (hb, eb, gb)).reshape(bsz, s, d)

def first_inputs(seed: int = 0) -> dict:
    key = jax.random.key(seed)
    ks = jax.random.split(key, 24)
    f32 = jnp.float32

    def nrm(k, shape, sd):
        return jax.random.normal(k, shape, f32) * sd

    dt0 = jnp.exp(jax.random.uniform(ks[14], (DEPTH, SSM_HEADS), f32) * (math.log(0.1) - math.log(0.001)) + math.log(0.001))
    return {
        'x': nrm(ks[0], (BATCH, SEQ, D_MODEL), 1.0),
        'c': nrm(ks[1], (BATCH, D_MODEL), 1.0),
        'ada_w': nrm(ks[2], (DEPTH, D_MODEL, 6 * D_MODEL), 0.5 * D_MODEL ** -0.5),
        'ada_b': nrm(ks[3], (DEPTH, 6 * D_MODEL), 0.01),
        'norm_mix': 1.0 + nrm(ks[4], (DEPTH, D_MODEL), 0.05),
        'norm_ffn': 1.0 + nrm(ks[5], (DEPTH, D_MODEL), 0.05),
        'w_in': nrm(ks[6], (DEPTH, D_MODEL, N_IN), D_MODEL ** -0.5),
        'cmp_pe': nrm(ks[7], (DEPTH, 2, CMP_BLOCK, HEAD_DIM), 0.1),
        'cmp_w1': nrm(ks[8], (DEPTH, 2, CMP_BLOCK * HEAD_DIM, CMP_HIDDEN), (CMP_BLOCK * HEAD_DIM) ** -0.5),
        'cmp_w2': nrm(ks[9], (DEPTH, 2, CMP_HIDDEN, HEAD_DIM), CMP_HIDDEN ** -0.5),
        'rel_bias': nrm(ks[10], (REL_BUCKETS, NSA_HEADS), 0.5),
        'attn_out_norm': 1.0 + nrm(ks[11], (DEPTH, D_ATTN), 0.05),
        'conv_w': nrm(ks[12], (DEPTH, CONV_WIDTH, CONV_CH), CONV_WIDTH ** -0.5),
        'conv_b': nrm(ks[13], (DEPTH, CONV_CH), 0.01),
        'dt_bias': dt0 + jnp.log(-jnp.expm1(-dt0)),
        'a_log': jnp.log(jax.random.uniform(ks[15], (DEPTH, SSM_HEADS), f32, 1.0, 16.0)),
        'd_skip': 1.0 + nrm(ks[16], (DEPTH, SSM_HEADS), 0.1),
        'ssm_norm': 1.0 + nrm(ks[17], (DEPTH, D_SSM), 0.05),
        'w_out': nrm(ks[18], (DEPTH, D_MODEL, D_MODEL), D_MODEL ** -0.5),
        'peer_wq': nrm(ks[19], (DEPTH, D_MODEL, PEER_HEADS * PEER_KEY_DIM), D_MODEL ** -0.5),
        'peer_subkeys': nrm(ks[20], (DEPTH, 2, PEER_NKEYS, PEER_KEY_DIM // 2), (PEER_KEY_DIM // 2) ** -0.5),
        'peer_u': nrm(ks[21], (DEPTH, PEER_EXPERTS, D_MODEL), D_MODEL ** -0.5),
        'peer_v': nrm(ks[22], (DEPTH, PEER_EXPERTS, D_MODEL), PEER_HEADS ** -0.5),
        'norm_final': 1.0 + nrm(ks[23], (D_MODEL,), 0.05),
    }

def first_block(x, c, ada_w, ada_b, norm_mix, norm_ffn, w_in, cmp_pe, cmp_w1, cmp_w2, rel_bias,
              attn_out_norm, conv_w, conv_b, dt_bias, a_log, d_skip, ssm_norm, w_out,
              peer_wq, peer_subkeys, peer_u, peer_v, norm_final):
    cond = jax.nn.silu(c)
    for l in range(DEPTH):
        mod = (cond @ ada_w[l] + ada_b[l])[:, None, :]
        sh1, sc1, g1, sh2, sc2, g2 = jnp.split(mod, 6, axis=-1)
        h = rms_norm(x, norm_mix[l]) * (1.0 + sc1) + sh1
        x = x + g1 * hybrid_mixer(h, w_in[l], cmp_pe[l], cmp_w1[l], cmp_w2[l], rel_bias, attn_out_norm[l],
                                  conv_w[l], conv_b[l], dt_bias[l], a_log[l], d_skip[l], ssm_norm[l], w_out[l])
        h = rms_norm(x, norm_ffn[l]) * (1.0 + sc2) + sh2
        x = x + g2 * peer_ffn(h, peer_wq[l], peer_subkeys[l], peer_u[l], peer_v[l])
    return rms_norm(x, norm_final)


GDN_HEADS = 8
GDN_HEAD_DIM = 128
GDN_WIDTH = GDN_HEADS * GDN_HEAD_DIM
GDN_CONV = 4
GDN_CHUNK = 64
RWKV_HEAD_DIM = 64
RWKV_HEADS = 16
RWKV_WIDTH = RWKV_HEADS * RWKV_HEAD_DIM
RWKV_DECAY_LORA = 96
RWKV_ICLR_LORA = 96
RWKV_SHIFT_COLS = 3 * RWKV_WIDTH + RWKV_DECAY_LORA + RWKV_ICLR_LORA
RWKV_LN_EPS = 64e-5
S5_GROUP = 16
S5_WIDTH = 1024
S5_GROUPS = S5_WIDTH // S5_GROUP
S5_STATE = 64
N_BRANCH = 3
BRANCH_WIDTH = 1024
NORM_EPS = 1e-6

SPLIT_SIZES = (3 * GDN_WIDTH, GDN_WIDTH, GDN_HEADS, GDN_HEADS,
               RWKV_SHIFT_COLS, RWKV_WIDTH,
               S5_WIDTH, S5_WIDTH,
               N_BRANCH * D_MODEL)
IN_COLS = sum(SPLIT_SIZES)


def _split_cols(t, sizes):
    out, start = [], 0
    for s in sizes:
        out.append(t[..., start:start + s])
        start += s
    return out

def rms_norm_2(x, w, eps=NORM_EPS):
    xf = x.astype(jnp.float32)
    y = xf * lax.rsqrt(jnp.mean(xf * xf, axis=-1, keepdims=True) + eps)
    return (y * w.astype(jnp.float32)).astype(x.dtype)

def l2_normalize(x, eps=1e-6):
    return x * lax.rsqrt(jnp.sum(x * x, axis=-1, keepdims=True) + eps)

def causal_depthwise_conv_2(x, w):
    k_width, ch = w.shape
    return lax.conv_general_dilated(x, w[:, None, :].astype(x.dtype), window_strides=(1,),
                                    padding=[(k_width - 1, 0)],
                                    dimension_numbers=('NWC', 'WIO', 'NWC'),
                                    feature_group_count=ch)

def _to_chunks(t, n):
    bsz, _, h = t.shape[:3]
    t = t.reshape((bsz, n, GDN_CHUNK, h) + t.shape[3:])
    return t.transpose((1, 0, 3, 2) + tuple(range(4, t.ndim)))

def gated_delta_rule_chunked(q, k, v, beta, g):
    bsz, seq, h, dk = q.shape
    dv = v.shape[-1]
    n = seq // GDN_CHUNK
    q, k, v, beta, g = (_to_chunks(t, n) for t in (q, k, v, beta, g))
    g_cum = jnp.cumsum(g, axis=-1)
    idx = jnp.arange(GDN_CHUNK)
    strict = idx[:, None] > idx[None, :]
    incl = idx[:, None] >= idx[None, :]
    diff = g_cum[..., :, None] - g_cum[..., None, :]
    decay_strict = jnp.exp(jnp.where(strict, diff, -jnp.inf))
    decay_incl = jnp.exp(jnp.where(incl, diff, -jnp.inf))
    k_beta = k * beta[..., None]
    lower = jnp.einsum('nbhcd,nbhsd->nbhcs', k_beta, k) * decay_strict
    eye = jnp.eye(GDN_CHUNK, dtype=q.dtype)
    t_mat = lax.linalg.triangular_solve(eye + lower, jnp.broadcast_to(eye, lower.shape),
                                        left_side=True, lower=True)
    u = jnp.einsum('nbhcs,nbhse->nbhce', t_mat, v * beta[..., None])
    w = jnp.einsum('nbhcs,nbhsd->nbhcd', t_mat, k_beta * jnp.exp(g_cum)[..., None])
    attn = jnp.einsum('nbhcd,nbhsd->nbhcs', q, k) * decay_incl
    q_dec = q * jnp.exp(g_cum)[..., None]
    g_last = g_cum[..., -1]
    k_dec = k * jnp.exp(g_last[..., None] - g_cum)[..., None]

    def step(state, xs):
        q_i, k_i, u_i, w_i, a_i, gl_i = xs
        v_new = u_i - jnp.einsum('bhcd,bhde->bhce', w_i, state)
        o_i = (jnp.einsum('bhcd,bhde->bhce', q_i, state)
               + jnp.einsum('bhcs,bhse->bhce', a_i, v_new))
        state = state * jnp.exp(gl_i)[..., None, None] + jnp.einsum('bhcd,bhce->bhde', k_i, v_new)
        return state, o_i

    s0 = jnp.zeros((bsz, h, dk, dv), jnp.float32)
    _, o = lax.scan(step, s0, (q_dec, k_dec, u, w, attn, g_last))
    return o.transpose(1, 0, 3, 2, 4).reshape(bsz, seq, h, dv)

def gdn_branch(qkv, z, b_logit, a_logit, conv_w, a_log, dt_bias, norm_w):
    bsz, seq, _ = qkv.shape
    qkv = jax.nn.silu(causal_depthwise_conv_2(qkv, conv_w)).astype(jnp.float32)
    q, k, v = jnp.split(qkv, 3, axis=-1)
    hs = (bsz, seq, GDN_HEADS, GDN_HEAD_DIM)
    q = l2_normalize(q.reshape(hs)) * (GDN_HEAD_DIM ** -0.5)
    k = l2_normalize(k.reshape(hs))
    v = v.reshape(hs)
    beta = jax.nn.sigmoid(b_logit.astype(jnp.float32))
    g = -jnp.exp(a_log.astype(jnp.float32)) * jax.nn.softplus(
        a_logit.astype(jnp.float32) + dt_bias.astype(jnp.float32))
    o = gated_delta_rule_chunked(q, k, v, beta, g)
    o = rms_norm_2(o, norm_w) * jax.nn.silu(z.astype(jnp.float32).reshape(hs))
    return o.reshape(bsz, seq, GDN_WIDTH)

def rwkv7_scan(r, w, k, v, kk, a):
    bsz, seq, h, n = r.shape

    def step(state, xs):
        r_t, w_t, k_t, v_t, kk_t, a_t = xs
        sa = jnp.einsum('bhvk,bhk->bhv', state, -kk_t)
        state = (state * w_t[:, :, None, :] + sa[..., None] * (kk_t * a_t)[:, :, None, :]
                 + v_t[..., None] * k_t[:, :, None, :])
        return state, jnp.einsum('bhvk,bhk->bhv', state, r_t)

    xs = tuple(t.transpose(1, 0, 2, 3) for t in (r, w, k, v, kk, a))
    s0 = jnp.zeros((bsz, h, n, n), jnp.float32)
    _, y = lax.scan(step, s0, xs)
    return y.transpose(1, 0, 2, 3)

def rwkv7_branch(feat, z, mu, w0, w_up, a0, a_up, k_k, k_a, r_k, lnx_w, lnx_b):
    bsz, seq, _ = feat.shape
    f32 = jnp.float32
    feat = feat.astype(f32)
    prev = jnp.pad(feat[:, :-1], ((0, 0), (1, 0), (0, 0)))
    feat = feat + (prev - feat) * mu.astype(f32)
    r, k, v, wl, al = _split_cols(feat, (RWKV_WIDTH,) * 3 + (RWKV_DECAY_LORA, RWKV_ICLR_LORA))
    w_pre = w0.astype(f32) + jnp.tanh(wl) @ w_up.astype(f32)
    decay = jnp.exp(-jnp.exp(-jax.nn.softplus(-w_pre) - 0.5))
    a = jax.nn.sigmoid(a0.astype(f32) + al @ a_up.astype(f32))
    hs = (bsz, seq, RWKV_HEADS, RWKV_HEAD_DIM)
    kk = l2_normalize((k * k_k.astype(f32)).reshape(hs))
    k = k * (1.0 + (a - 1.0) * k_a.astype(f32))
    r, k, v, a, decay = (t.reshape(hs) for t in (r, k, v, a, decay))
    y = rwkv7_scan(r, decay, k, v, kk, a)
    mean = jnp.mean(y, axis=-1, keepdims=True)
    var = jnp.mean(jnp.square(y - mean), axis=-1, keepdims=True)
    y = ((y - mean) * lax.rsqrt(var + RWKV_LN_EPS) * lnx_w.astype(f32).reshape(RWKV_HEADS, RWKV_HEAD_DIM)
         + lnx_b.astype(f32).reshape(RWKV_HEADS, RWKV_HEAD_DIM))
    y = y + jnp.sum(r * k * r_k.astype(f32), axis=-1, keepdims=True) * v
    y = y * jax.nn.silu(z.astype(f32).reshape(hs))
    return y.reshape(bsz, seq, RWKV_WIDTH)

def s5_branch(u, z, a_re, a_im, log_dt, b_re, b_im, c_re, c_im, d_skip, glu_w, glu_b):
    bsz, seq, _ = u.shape
    f32 = jnp.float32
    u = u.astype(f32)
    ug = u.reshape(bsz, seq, S5_GROUPS, S5_GROUP)
    a_re, a_im, b_re, b_im, c_re, c_im = (t.astype(f32) for t in (a_re, a_im, b_re, b_im, c_re, c_im))
    dt = jnp.exp(log_dt.astype(f32))[:, None]
    mag = jnp.exp(a_re * dt)
    ab_re, ab_im = mag * jnp.cos(a_im * dt), mag * jnp.sin(a_im * dt)
    den = a_re * a_re + a_im * a_im
    coef_re = ((ab_re - 1.0) * a_re + ab_im * a_im) / den
    coef_im = (ab_im * a_re - (ab_re - 1.0) * a_im) / den
    bb_re = coef_re[..., None] * b_re - coef_im[..., None] * b_im
    bb_im = coef_re[..., None] * b_im + coef_im[..., None] * b_re
    bu_re = jnp.einsum('gpc,blgc->blgp', bb_re, ug)
    bu_im = jnp.einsum('gpc,blgc->blgp', bb_im, ug)
    shp = (1, seq, S5_GROUPS, S5_STATE)
    a_re_t = jnp.broadcast_to(ab_re, shp)
    a_im_t = jnp.broadcast_to(ab_im, shp)

    def combine(e1, e2):
        a1r, a1i, b1r, b1i = e1
        a2r, a2i, b2r, b2i = e2
        return (a1r * a2r - a1i * a2i, a1r * a2i + a1i * a2r,
                a2r * b1r - a2i * b1i + b2r, a2r * b1i + a2i * b1r + b2i)

    _, _, s_re, s_im = lax.associative_scan(combine, (a_re_t, a_im_t, bu_re, bu_im), axis=1)
    y = jnp.einsum('gcp,blgp->blgc', c_re, s_re) - jnp.einsum('gcp,blgp->blgc', c_im, s_im)
    y = y.reshape(bsz, seq, S5_WIDTH) + d_skip.astype(f32) * u
    y = jax.nn.gelu(y)
    y = y * jax.nn.sigmoid(y @ glu_w.astype(f32) + glu_b.astype(f32))
    return y * jax.nn.silu(z.astype(f32))

def second_inputs(seed: int = 0) -> dict:
    key = jax.random.key(seed)
    ks = iter(jax.random.split(key, 40))
    f32 = jnp.float32

    def nrm(shape, s):
        return s * jax.random.normal(next(ks), shape, f32)

    def unif(shape, lo, hi):
        return jax.random.uniform(next(ks), shape, f32, lo, hi)

    gdn_dt = jnp.exp(unif((DEPTH, GDN_HEADS), math.log(1e-3), math.log(1e-1)))
    return {
        "x": nrm((BATCH, SEQ, D_MODEL), 1.0),
        "norm_w": 1.0 + nrm((DEPTH, D_MODEL), 0.02),
        "w_in": nrm((DEPTH, D_MODEL, IN_COLS), D_MODEL ** -0.5),
        "gdn_conv_w": nrm((DEPTH, GDN_CONV, 3 * GDN_WIDTH), GDN_CONV ** -0.5),
        "gdn_a_log": jnp.log(unif((DEPTH, GDN_HEADS), 1.0, 16.0)),
        "gdn_dt_bias": jnp.log(jnp.expm1(gdn_dt)),
        "gdn_norm_w": 1.0 + nrm((DEPTH, GDN_HEAD_DIM), 0.02),
        "rwkv_mu": unif((DEPTH, RWKV_SHIFT_COLS), 0.0, 1.0),
        "rwkv_w0": unif((DEPTH, RWKV_WIDTH), -6.5, -1.5),
        "rwkv_w_up": nrm((DEPTH, RWKV_DECAY_LORA, RWKV_WIDTH), 0.5 * RWKV_DECAY_LORA ** -0.5),
        "rwkv_a0": nrm((DEPTH, RWKV_WIDTH), 0.1),
        "rwkv_a_up": nrm((DEPTH, RWKV_ICLR_LORA, RWKV_WIDTH), 0.5 * RWKV_ICLR_LORA ** -0.5),
        "rwkv_k_k": 0.85 + nrm((DEPTH, RWKV_WIDTH), 0.05),
        "rwkv_k_a": 1.0 + nrm((DEPTH, RWKV_WIDTH), 0.05),
        "rwkv_r_k": nrm((DEPTH, RWKV_HEADS, RWKV_HEAD_DIM), 0.1),
        "rwkv_lnx_w": 1.0 + nrm((DEPTH, RWKV_WIDTH), 0.02),
        "rwkv_lnx_b": nrm((DEPTH, RWKV_WIDTH), 0.02),
        "s5_a_re": -0.5 + nrm((DEPTH, S5_GROUPS, S5_STATE), 0.01),
        "s5_a_im": jnp.pi * jnp.arange(S5_STATE, dtype=f32)[None, None, :] + nrm((DEPTH, S5_GROUPS, S5_STATE), 0.01),
        "s5_log_dt": unif((DEPTH, S5_GROUPS), math.log(1e-3), math.log(1e-1)),
        "s5_b_re": nrm((DEPTH, S5_GROUPS, S5_STATE, S5_GROUP), (2 * S5_GROUP) ** -0.5),
        "s5_b_im": nrm((DEPTH, S5_GROUPS, S5_STATE, S5_GROUP), (2 * S5_GROUP) ** -0.5),
        "s5_c_re": nrm((DEPTH, S5_GROUPS, S5_GROUP, S5_STATE), (2 * S5_STATE) ** -0.5),
        "s5_c_im": nrm((DEPTH, S5_GROUPS, S5_GROUP, S5_STATE), (2 * S5_STATE) ** -0.5),
        "s5_d": nrm((DEPTH, S5_WIDTH), 1.0),
        "s5_glu_w": nrm((DEPTH, S5_WIDTH, S5_WIDTH), S5_WIDTH ** -0.5),
        "s5_glu_b": nrm((DEPTH, S5_WIDTH), 0.02),
        "gate_b": nrm((DEPTH, N_BRANCH, D_MODEL), 0.02),
        "w_branch": nrm((DEPTH, N_BRANCH, BRANCH_WIDTH, D_MODEL), BRANCH_WIDTH ** -0.5),
        "w_out": nrm((DEPTH, D_MODEL, D_MODEL), D_MODEL ** -0.5),
        "final_norm_w": 1.0 + nrm((D_MODEL,), 0.02),
    }

def second_block(x, norm_w, w_in, gdn_conv_w, gdn_a_log, gdn_dt_bias, gdn_norm_w,
              rwkv_mu, rwkv_w0, rwkv_w_up, rwkv_a0, rwkv_a_up, rwkv_k_k, rwkv_k_a, rwkv_r_k,
              rwkv_lnx_w, rwkv_lnx_b,
              s5_a_re, s5_a_im, s5_log_dt, s5_b_re, s5_b_im, s5_c_re, s5_c_im, s5_d,
              s5_glu_w, s5_glu_b,
              gate_b, w_branch, w_out, final_norm_w):
    bsz, seq, _ = x.shape
    for i in range(DEPTH):
        h = rms_norm_2(x, norm_w[i])
        proj = h @ w_in[i]
        (g_qkv, g_z, g_b, g_a, r_feat, r_z, s_u, s_z, gate_logits) = _split_cols(proj, SPLIT_SIZES)
        o_a = gdn_branch(g_qkv, g_z, g_b, g_a, gdn_conv_w[i], gdn_a_log[i], gdn_dt_bias[i], gdn_norm_w[i])
        o_b = rwkv7_branch(r_feat, r_z, rwkv_mu[i], rwkv_w0[i], rwkv_w_up[i], rwkv_a0[i], rwkv_a_up[i],
                           rwkv_k_k[i], rwkv_k_a[i], rwkv_r_k[i], rwkv_lnx_w[i], rwkv_lnx_b[i])
        o_c = s5_branch(s_u, s_z, s5_a_re[i], s5_a_im[i], s5_log_dt[i], s5_b_re[i], s5_b_im[i],
                        s5_c_re[i], s5_c_im[i], s5_d[i], s5_glu_w[i], s5_glu_b[i])
        branches = jnp.stack([o_a, o_b, o_c], axis=2)
        branch_proj = jnp.einsum('blnc,ncd->blnd', branches, w_branch[i].astype(jnp.float32))
        gates = jax.nn.sigmoid(gate_logits.astype(jnp.float32).reshape(bsz, seq, N_BRANCH, D_MODEL)
                               + gate_b[i].astype(jnp.float32))
        merged = jnp.sum(gates * branch_proj, axis=2)
        x = x + (merged @ w_out[i].astype(jnp.float32)).astype(x.dtype)
    return rms_norm_2(x, final_norm_w)


_first_inputs = second_inputs


def second_inputs(seed=0):
    import zlib

    import numpy as np

    out = dict(_first_inputs(seed))
    spreads = {}
    factors = {'norm_w': 3.342,
     'gdn_norm_w': 53.831,
     'rwkv_w_up': 8.0,
     'rwkv_a0': 4.667,
     'rwkv_k_k': 35.556,
     'rwkv_k_a': 3.541,
     'rwkv_lnx_w': 58.75,
     'rwkv_lnx_b': 59.231,
     's5_a_re': 64.0,
     's5_a_im': 64.0,
     's5_log_dt': 64.0,
     's5_b_re': 64.0,
     's5_b_im': 64.0,
     's5_c_re': 64.0,
     's5_c_im': 64.0,
     's5_glu_b': 64.0,
     'gate_b': 8.0,
     'final_norm_w': 7.639}
    for name, (base, spread) in spreads.items():
        noise = np.random.default_rng([zlib.crc32(name.encode()), seed]).standard_normal(out[name].shape)
        drawn = base * np.exp(spread * noise) if base else spread * noise
        out[name] = __import__('jax').numpy.asarray(drawn.astype(out[name].dtype))
    for name, factor in factors.items():
        out[name] = (out[name] * factor).astype(out[name].dtype)
    return out


_narrow_inputs = second_inputs


def second_inputs(seed=0):
    out = dict(_narrow_inputs(seed))
    wider = {'gdn_norm_w': 4.51,
     'rwkv_k_k': 4.43,
     'rwkv_lnx_w': 4.48,
     'rwkv_lnx_b': 4.46,
     's5_d': 4.14,
     's5_glu_w': 7.09,
     's5_glu_b': 12.0,
     'final_norm_w': 3.11}
    for name, times in wider.items():
        mean = out[name].mean()
        out[name] = (mean + times * (out[name] - mean)).astype(out[name].dtype)
    return out


def setup_inputs(seed=0):
    out = dict(first_inputs(seed))
    for name, value in second_inputs(seed + 1).items():
        if name != "x":
            out[name + "_2"] = value
    return out


def reference(
    x, c, ada_w, ada_b, norm_mix, norm_ffn, w_in, cmp_pe, cmp_w1, cmp_w2, rel_bias,
    attn_out_norm, conv_w, conv_b, dt_bias, a_log, d_skip, ssm_norm, w_out, peer_wq,
    peer_subkeys, peer_u, peer_v, norm_final, norm_w_2, w_in_2, gdn_conv_w_2, gdn_a_log_2,
    gdn_dt_bias_2, gdn_norm_w_2, rwkv_mu_2, rwkv_w0_2, rwkv_w_up_2, rwkv_a0_2, rwkv_a_up_2,
    rwkv_k_k_2, rwkv_k_a_2, rwkv_r_k_2, rwkv_lnx_w_2, rwkv_lnx_b_2, s5_a_re_2, s5_a_im_2,
    s5_log_dt_2, s5_b_re_2, s5_b_im_2, s5_c_re_2, s5_c_im_2, s5_d_2, s5_glu_w_2, s5_glu_b_2,
    gate_b_2, w_branch_2, w_out_2, final_norm_w_2,
):
    x = first_block(
        x, c, ada_w, ada_b, norm_mix, norm_ffn, w_in, cmp_pe, cmp_w1, cmp_w2, rel_bias,
        attn_out_norm, conv_w, conv_b, dt_bias, a_log, d_skip, ssm_norm, w_out, peer_wq,
        peer_subkeys, peer_u, peer_v, norm_final,
    )
    return second_block(
        x, norm_w_2, w_in_2, gdn_conv_w_2, gdn_a_log_2, gdn_dt_bias_2, gdn_norm_w_2, rwkv_mu_2,
        rwkv_w0_2, rwkv_w_up_2, rwkv_a0_2, rwkv_a_up_2, rwkv_k_k_2, rwkv_k_a_2, rwkv_r_k_2,
        rwkv_lnx_w_2, rwkv_lnx_b_2, s5_a_re_2, s5_a_im_2, s5_log_dt_2, s5_b_re_2, s5_b_im_2,
        s5_c_re_2, s5_c_im_2, s5_d_2, s5_glu_w_2, s5_glu_b_2, gate_b_2, w_branch_2, w_out_2,
        final_norm_w_2,
    )


_drawn_inputs = setup_inputs


def setup_inputs(seed=0):
    import zlib

    import numpy as np

    out = dict(_drawn_inputs(seed))
    spreads = {}
    factors = {'conv_b': 6.405}
    for name, (base, spread) in spreads.items():
        noise = np.random.default_rng([zlib.crc32(name.encode()), seed]).standard_normal(out[name].shape)
        drawn = base * np.exp(spread * noise) if base else spread * noise
        out[name] = jnp.asarray(drawn.astype(out[name].dtype))
    for name, factor in factors.items():
        out[name] = (out[name] * factor).astype(out[name].dtype)
    return out
```

```python
from contextlib import ExitStack

import numpy as np

import concourse.bass as bass
from concourse import mybir

ALU = mybir.AluOpType
ACT = mybir.ActivationFunctionType
F32 = mybir.dt.float32
I32 = mybir.dt.int32
U32 = mybir.dt.uint32
AX_X = mybir.AxisListType.X

P = 128
T = 256
TT = T // P
D = 2048
KD = D // P
CHUNK = 512
HALF = 1024
EPS = 1e-6
NEG = -1e30
HEADS, KV_HEADS, GROUP, DH = 16, 2, 8, 64
N_IN = 4416
CONV_TAPS = 4
EXPERTS_SIDE = 128
PEER_HEADS, TOPK = 8, 16

Q0, KV0, GATE0, Z0, XBC0, DT0 = 0, 1024, 1792, 1840, 2864, 4400
GQKV0, GZ0, GB0, GA0, RF0, RZ0, SU0, SZ0, MG0 = 0, 3072, 4096, 4104, 4112, 7376, 8400, 9424, 10448


class Chain:

    def __init__(self, sem):
        self.sem, self.n = sem, 0

    def __call__(self, ins):
        ins.then_inc(self.sem, 1)
        self.n = self.n + 1
        self.eng.wait_ge(self.sem, self.n)

    def on(self, eng):
        self.eng = eng
        return self

    def enter(self, i, per):
        self.base, self.per = self.n, per
        self.n = self.n + i * per

    def leave(self, steps):
        self.n = self.base + steps * self.per


class BankRing:

    def __init__(self, banks, filled, emptied):
        self.banks, self.filled, self.emptied = banks, filled, emptied
        self.nf = self.ne = self.of = self.oe = 0

    def take(self, pe):
        if self.of + self.nf >= len(self.banks):
            pe.wait_ge(self.emptied, self.wf + self.nf + self.of - len(self.banks) + 1)
        return self.banks[(self.of + self.nf) % len(self.banks)]

    wf = we = 0

    def put(self, ins):
        ins.then_inc(self.filled, 1)
        self.nf += 1

    def get(self, eng):
        eng.wait_ge(self.filled, self.we + self.ne + self.oe + 1)
        return self.banks[(self.oe + self.ne) % len(self.banks)]

    def free(self, ins):
        ins.then_inc(self.emptied, 1)
        self.ne += 1

    def enter_fill(self, i, per):
        self.of, self.nf, self.wf = self.of + self.nf, 0, i * per

    def leave_fill(self, steps, per):
        assert self.nf == per and per % len(self.banks) == 0 and self.of >= len(self.banks)
        self.of, self.nf, self.wf = self.of + steps * per, 0, 0

    def enter_empty(self, i, per):
        self.oe, self.ne, self.we = self.oe + self.ne, 0, i * per

    def leave_empty(self, steps, per):
        assert self.ne == per and per % len(self.banks) == 0
        self.oe, self.ne, self.we = self.oe + steps * per, 0, 0


class Machine:

    def __init__(self, nc, ctx):
        self.nc, self.ctx, self.sems, self.uses = nc, ctx, {}, {}
        banks = [ctx.enter_context(nc.psum_tensor(f"bank{i}", [P, CHUNK], F32)) for i in range(8)]
        self.to_dve = BankRing(banks[:4], self.sem("dve_banks_filled"), self.sem("dve_banks_emptied"))
        self.to_act = BankRing(banks[4:], self.sem("act_banks_filled"), self.sem("act_banks_emptied"))
        self.banks = banks
        self.dve_chain = Chain(self.sem("dve_done"))
        self.act_chain = Chain(self.sem("act_done"))
        self.pool_chain = Chain(self.sem("pool_done"))
        self.weights = WeightStream(self)
        self.shared = set(self.sems) | {"residual_gain_loaded"}

    def sem(self, name):
        if name not in self.sems:
            self.sems[name] = self.nc.alloc_semaphore(name=name)
        return self.sems[name]

    def clear_stage_semaphores(self):
        stage = [name for name in self.sems if name not in self.shared]
        self.nc.clear_and_free_semaphores([self.sems.pop(name) for name in stage])
        self.nc.all_engine_barrier()

    def sb(self, ctx, name, shape, dt=F32):
        self.uses[name] = self.uses.get(name, 0) + 1
        unique = name if self.uses[name] == 1 else f"{name}_{self.uses[name]}"
        return ctx.enter_context(self.nc.sbuf_tensor(unique, shape, dt))

    def dram(self, name, shape):
        return self.nc.dram_tensor(name, shape, F32, kind="Internal").ap()


class WeightStream:

    def __init__(self, m):
        self.m = m
        self.buf = [m.sb(m.ctx, f"weights{b}", [P, KD, CHUNK]) for b in range(2)]
        self.loaded = [m.sem(f"weights_loaded{b}") for b in range(2)]
        self.used = [m.sem(f"weights_used{b}") for b in range(2)]
        self.n_load = self.n_use = 0

    def load(self, sp, w, c0, n):
        b, turn = self.n_load % 2, self.n_load // 2
        if turn:
            sp.wait_ge(self.used[b], turn)
        kt = w.shape[0] // P
        src = w.rearrange("(k p) n -> p k n", p=P)[:, :, c0:c0 + n]
        sp.dma_start(self.buf[b][:, 0:kt, 0:n], src).then_inc(self.loaded[b], 16)
        self.n_load += 1

    def multiply(self, pe, acts, kt, n, ring):
        b, turn = self.n_use % 2, self.n_use // 2
        pe.wait_ge(self.loaded[b], 16 * (turn + 1))
        for tt in range(TT):
            bank = ring.take(pe)
            for k in range(kt):
                mm = pe.matmul(bank[:, 0:n], acts[:, k, tt * P:(tt + 1) * P], self.buf[b][:, k, 0:n],
                               start=(k == 0), stop=(k == kt - 1))
            ring.put(mm)
        pe.drain().then_inc(self.used[b], 1)
        self.n_use += 1


def chunks(n, size=CHUNK):
    return [(c, min(size, n - c)) for c in range(0, n, size)]


class Vectors:

    LISTS = [
        [("c", 16), ("norm_mix", 16), ("norm_ffn", 16), ("norm_w_2", 16), ("ssm_norm", 8), ("attn_out_norm", 8),
         ("conv_w", 48)],
        [("ada_b", 96), ("conv_b", 12), ("s5_d_2", 8)],
        [("gdn_conv_w_2", 96), ("cmp_pe", 32)],
    ]

    def __init__(self, m):
        self.cols = m.sb(m.ctx, "vector_columns", [P, len(self.LISTS), P])
        self.at = {}
        for g, names in enumerate(self.LISTS):
            c = 0
            for name, n in names:
                self.at[name] = (g, c, n)
                c += n

    def col(self, name, k, n=1):
        g, c, _ = self.at[name]
        return self.cols[:, g, c + k:c + k + n]


def turn_to_columns(pe, ring, ident, src, kt):
    for j in range(kt // 2):
        bank = ring.take(pe)
        for u in range(2):
            for tt in range(TT):
                mm = pe.transpose(bank[:, (u * TT + tt) * P:(u * TT + tt + 1) * P], src(2 * j + u, tt), ident)
        ring.put(mm)



def stage_modulation(nc, m, io, st):
    NM = 6 * D
    PIECE = NM // 4
    with ExitStack() as ctx:
        rows = m.sb(ctx, "vector_rows", [P, 3, P])
        ring = m.sb(ctx, "ada_ring", [P, 4, PIECE])
        acc = m.sb(ctx, "ada_acc", [P, NM])
        cond = m.sb(ctx, "cond", [P, KD])
        ones = m.sb(ctx, "ones_col", [P, 1])
        mod_rows = m.sb(ctx, "mod_rows", [NM // P, P])
        xor = m.sb(ctx, "xor_bits", [P, P], I32)
        s_idx = m.sb(ctx, "s_idx", [P, P], I32)
        t_idx = m.sb(ctx, "t_idx", [P, P], I32)
        xorf = m.sb(ctx, "xor_f", [P, P])
        tmp = m.sb(ctx, "mask_tmp", [P, P])
        vec_loaded, vec_zero = m.sem("vectors_loaded"), m.sem("vector_rows_zeroed")
        piece_loaded = [m.sem(f"ada_piece_loaded{b}") for b in range(4)]
        piece_used = [m.sem(f"ada_piece_used{b}") for b in range(4)]
        iotas_ready, ident_ready = m.sem("iotas_ready"), m.sem("identity_ready")
        cond_ready, acc_ready, ones_ready = m.sem("cond_ready"), m.sem("ada_sum_ready"), m.sem("ones_ready")
        cols_ready = m.sem("vector_columns_ready")
        mod_cols_ready, mod_rows_ready, mod_stored = m.sem("mod_columns_ready"), m.sem("mod_rows_ready"), m.sem("mod_stored")
        ident0 = m.sem("identity_zeroed")
        n_vec = sum(len(names) for names in Vectors.LISTS)

        with nc.Block() as block:
            @block.sync
            def _(sp):
                sp.wait_ge(vec_zero, 1)
                for g, names in enumerate(Vectors.LISTS):
                    for name, n in names:
                        _, c, _ = st.vec.at[name]
                        sp.dma_start(rows[c:c + n, g, :], flat(io[name]).rearrange("(r p) -> r p", p=P))\
                          .then_inc(vec_loaded, 16)
                for t in range(TT):
                    sp.dma_start(st.x[:, t, :], io["x"][0, t * P:(t + 1) * P, :]).then_inc(m.sem("x_loaded"), 16)
                with sp.Fori(0, KD) as k:
                    for b in range(4):
                        sp.wait_ge(piece_used[b], k)
                        sp.dma_start(ring[:, b, :], io["ada_w"][0, bass.ds(k * P, P), b * PIECE:(b + 1) * PIECE])\
                          .then_inc(piece_loaded[b], 16)
                sp.wait_ge(mod_rows_ready, 1)
                sp.dma_start(st.mod_dram.rearrange("(r p) -> r p", p=P), mod_rows[:, :]).then_inc(mod_stored, 16)
                sp.wait_ge(mod_stored, 16)

            @block.gpsimd
            def _(pool):
                pool.memset(rows[:, :, :], 0.0).then_inc(vec_zero, 1)
                pool.memset(st.ident[:, :], 0.0).then_inc(ident0, 1)
                pool.wait_ge(ident0, 1)
                pool.affine_select(out=st.ident[:, :], in_=st.ident[:, :], compare_op=ALU.not_equal, fill=1.0,
                                   base=0, pattern=[[-1, P]], channel_multiplier=1).then_inc(ident_ready, 1)
                pool.iota(s_idx[:, :], pattern=[[0, P]], base=0, channel_multiplier=1)
                pool.iota(t_idx[:, :], pattern=[[1, P]], base=0, channel_multiplier=0).then_inc(iotas_ready, 1)

            @block.vector
            def _(dve):
                V = m.dve_chain.on(dve)
                dve.memset(ones[:, :], 1.0).then_inc(ones_ready, 1)
                V(dve.memset(acc[:, :], 0.0))
                dve.wait_ge(iotas_ready, 1)
                V(dve.tensor_tensor(xor[:, :], s_idx[:, :], t_idx[:, :], ALU.bitwise_xor))
                V(dve.tensor_tensor(st.strict[:, :], s_idx[:, :], t_idx[:, :], ALU.is_lt))
                V(dve.tensor_tensor(st.incl[:, :], s_idx[:, :], t_idx[:, :], ALU.is_le))
                V(dve.tensor_copy(xorf[:, :], xor[:, :]))
                V(dve.tensor_copy(st.iota_row[:, :], t_idx[:, :]))
                V(dve.tensor_scalar(st.same64[:, :], xorf[:, :], 64.0, None, ALU.is_lt))
                for lv in range(7):
                    V(dve.tensor_scalar(tmp[:, :], xorf[:, :], float(2 ** lv), None, ALU.is_ge))
                    V(dve.scalar_tensor_tensor(out=tmp[:, :], in0=xorf[:, :], scalar=float(2 ** (lv + 1)),
                                               in1=tmp[:, :], op0=ALU.is_lt, op1=ALU.mult))
                    V(dve.tensor_tensor(st.level[:, lv, :], tmp[:, :], st.strict[:, :], ALU.mult))
                for g in range(3):
                    bank = m.to_dve.get(dve)
                    m.to_dve.free(dve.tensor_copy(st.vec.cols[:, g, :], bank[:, 0:P]))
                dve.engine_nop()
                dve.drain().then_inc(cols_ready, 1)
                dve.wait_ge(cond_ready, 1)
                with dve.Fori(0, KD) as k:
                    for b in range(4):
                        dve.wait_ge(piece_loaded[b], 16 * (k + 1))
                        part = acc[:, b * PIECE:(b + 1) * PIECE]
                        dve.scalar_tensor_tensor(out=part, in0=ring[:, b, :], scalar=cond[:, bass.ds(k, 1)],
                                                 in1=part, op0=ALU.mult, op1=ALU.add).then_inc(piece_used[b], 1)
                        dve.wait_ge(piece_used[b], k + 1)
                dve.drain().then_inc(acc_ready, 1)
                bank = m.to_dve.get(dve)
                m.to_dve.free(dve.tensor_tensor(st.mod_cols[:, :], bank[:, 0:NM // P], st.vec.col("ada_b", 0, 96), ALU.add))
                dve.drain().then_inc(mod_cols_ready, 1)
                dve.wait_ge(mod_cols_ready, 1)
                for name, part, dst in (("norm_mix", 1, st.gain1), ("norm_ffn", 4, st.gain2)):
                    dve.scalar_tensor_tensor(out=dst[:, :], in0=st.mod_cols[:, part * KD:(part + 1) * KD], scalar=1.0,
                                             in1=st.vec.col(name, 0, KD), op0=ALU.add, op1=ALU.mult)
                bank = m.to_dve.get(dve)
                m.to_dve.free(dve.tensor_copy(mod_rows[:, :], bank[0:NM // P, 0:P]))
                dve.drain().then_inc(mod_rows_ready, 1)

            @block.scalar
            def _(act):
                act.wait_ge(cols_ready, 1)
                act.activation(cond[:, :], st.vec.col("c", 0, KD), ACT.Silu).then_inc(cond_ready, 1)

            @block.tensor
            def _(pe):
                pe.wait_ge(ident_ready, 1)
                pe.wait_ge(vec_loaded, 16 * n_vec)
                for g in range(3):
                    bank = m.to_dve.take(pe)
                    m.to_dve.put(pe.transpose(bank[:, 0:P], rows[:, g, :], st.ident[:, :]))
                pe.wait_ge(acc_ready, 1)
                pe.wait_ge(ones_ready, 1)
                bank = m.to_dve.take(pe)
                for j in range(NM // P):
                    mm = pe.matmul(bank[:, j:j + 1], acc[:, j * P:(j + 1) * P], ones[:, :], start=True, stop=True)
                m.to_dve.put(mm)
                pe.wait_ge(mod_cols_ready, 1)
                bank = m.to_dve.take(pe)
                m.to_dve.put(pe.transpose(bank[0:NM // P, 0:P], st.mod_cols[:, :], st.ident[:, :]))


def flat(ap):
    names = "abcdefg"[:len(ap.shape)]
    return ap.rearrange(f"{' '.join(names)} -> ({' '.join(names)})") if len(names) > 1 else ap



def norm_to_columns(nc, m, st, name, x, width, dst, gain, shift, before_sync=None, x_sem=None, groups=1):
    kt = width // P
    with ExitStack() as ctx:
        squares = m.sb(ctx, f"{name}_squares", [P, width // groups])
        scaled = m.sb(ctx, f"{name}_scaled", [P, TT, width])
        ms = m.sb(ctx, f"{name}_ms", [P, TT * groups])
        rms = m.sb(ctx, f"{name}_rms", [P, TT * groups])
        rinv = m.sb(ctx, f"{name}_rinv", [P, TT * groups])
        squared, mean_ready = m.sem(f"{name}_squared"), m.sem(f"{name}_mean_ready")
        root_ready, scaled_ready = m.sem(f"{name}_root_ready"), m.sem(f"{name}_scaled_ready")
        w = width // groups
        with nc.Block() as block:
            if before_sync:
                @block.sync
                def _(sp):
                    before_sync(sp)

            @block.scalar
            def _(act):
                A = m.act_chain.on(act)
                if x_sem:
                    act.wait_ge(*x_sem)
                for tt in range(TT):
                    for g in range(groups):
                        A(act.activation(squares[:, :], x[:, tt, g * w:(g + 1) * w], ACT.Square,
                                         accum_out=ms[:, tt * groups + g:tt * groups + g + 1]))
                act.drain().then_inc(squared, 1)
                act.wait_ge(mean_ready, 1)
                act.activation(rms[:, :], ms[:, :], ACT.Sqrt).then_inc(root_ready, 1)

            @block.vector
            def _(dve):
                V = m.dve_chain.on(dve)
                dve.wait_ge(squared, 1)
                dve.tensor_scalar(ms[:, :], ms[:, :], 1.0 / w, EPS, ALU.mult, ALU.add).then_inc(mean_ready, 1)
                dve.wait_ge(root_ready, 1)
                V(dve.reciprocal(rinv[:, :], rms[:, :]))
                for tt in range(TT):
                    for g in range(groups):
                        dve.tensor_scalar(scaled[:, tt, g * w:(g + 1) * w], x[:, tt, g * w:(g + 1) * w],
                                          rinv[:, tt * groups + g:tt * groups + g + 1], None, ALU.mult)
                dve.drain().then_inc(scaled_ready, 1)
                for j in range(kt // 2):
                    bank = m.to_dve.get(dve)
                    for u in range(2):
                        k = 2 * j + u
                        src = bank[:, u * T:(u + 1) * T]
                        if shift:
                            ins = dve.tensor_scalar(dst(k), src, gain(k), shift(k), ALU.mult, ALU.add)
                        elif gain:
                            ins = dve.tensor_scalar(dst(k), src, gain(k), None, ALU.mult)
                        else:
                            ins = dve.tensor_copy(dst(k), src)
                    m.to_dve.free(ins)

            @block.tensor
            def _(pe):
                pe.wait_ge(scaled_ready, 1)
                turn_to_columns(pe, m.to_dve, st.ident[:, :], lambda k, tt: scaled[:, tt, k * P:(k + 1) * P], kt)


def project(nc, m, st, acts, kt, w, c0, n, out, act_share=True):
    with nc.Block() as block:
        @block.sync
        def _(sp):
            for c, size in chunks(n):
                m.weights.load(sp, w, c0 + c, size)

        @block.tensor
        def _(pe):
            for i, (c, size) in enumerate(chunks(n)):
                m.weights.multiply(pe, acts, kt, size, m.to_act if i % 2 else m.to_dve)

        @block.scalar
        def _(act):
            for i, (c, size) in enumerate(chunks(n)):
                if i % 2:
                    for tt in range(TT):
                        bank = m.to_act.get(act)
                        m.to_act.free(act.activation(out(tt, c, size), bank[:, 0:size], ACT.Copy))

        @block.vector
        def _(dve):
            for i, (c, size) in enumerate(chunks(n)):
                if i % 2 == 0:
                    for tt in range(TT):
                        bank = m.to_dve.get(dve)
                        m.to_dve.free(dve.tensor_copy(out(tt, c, size), bank[:, 0:size]))


class State:
    pass


def shared_state(m):
    st = State()
    st.vec = Vectors(m)
    st.x = m.sb(m.ctx, "x_rows", [P, TT, D])
    st.acts = m.sb(m.ctx, "act_columns", [P, KD, T])
    st.ident = m.sb(m.ctx, "ident", [P, P])
    st.strict = m.sb(m.ctx, "strict_mask", [P, P])
    st.incl = m.sb(m.ctx, "incl_mask", [P, P])
    st.same64 = m.sb(m.ctx, "same64_mask", [P, P])
    st.level = m.sb(m.ctx, "level_masks", [P, 7, P])
    st.iota_row = m.sb(m.ctx, "iota_row", [P, P])
    st.mod_cols = m.sb(m.ctx, "mod_cols", [P, 6 * KD])
    st.gain1 = m.sb(m.ctx, "gain1", [P, KD])
    st.gain2 = m.sb(m.ctx, "gain2", [P, KD])
    st.gain_count = 0
    st.mod_dram = m.dram("mod_row", [6 * D])
    return st


def view(ap, dims, offset=0):
    return bass.AP(tensor=ap.tensor, offset=ap.offset + offset, ap=[list(ap.ap[0])] + [list(d) for d in dims])


def spread(ap, n):
    return bass.AP(tensor=ap.tensor, offset=ap.offset, ap=[list(d) for d in ap.ap] + [[0, n]])



BUCKETS, MAX_DIST = 32, 2048
CMP_BLOCK, CMP_STRIDE = 32, 16
N_CMP = (T - CMP_BLOCK) // CMP_STRIDE + 1
BIAS_W = T + P


def bucket_starts():
    exact = BUCKETS // 2
    d = np.arange(4 * MAX_DIST)
    ratio = np.log(np.maximum(d, exact).astype(np.float32) / np.float32(exact)) / np.float32(np.log(MAX_DIST / exact))
    large = exact + (ratio * np.float32(BUCKETS - exact)).astype(np.int32)
    b = np.where(d < exact, d, np.minimum(large, BUCKETS - 1))
    return [int(np.argmax(b >= i)) for i in range(BUCKETS)]


def stage_attention(nc, m, io, st, proj, attn):
    starts = bucket_starts()
    MASKED = BUCKETS
    bias_dram = m.dram("bias_rows", [HEADS, P, 2 * T])
    with ExitStack() as ctx:
        bias = m.sb(ctx, "bias", [P, HEADS, BIAS_W])
        qT = st.acts[:, KD // 2:KD, :]
        kvT = m.sb(ctx, "kvT", [P, 4, T])
        gates = m.sb(ctx, "gates", [P, TT, 3 * HEADS])
        kcT = m.sb(ctx, "kcT", [P, N_CMP])
        vblk = m.sb(ctx, "v_cmp_blocks", [8 * N_CMP, KV_HEADS, GROUP * DH])
        with ExitStack() as c1:
            table = m.sb(c1, "bias_table", [BUCKETS + 1, HEADS])
            lo = m.sb(c1, "bucket_lo", [BUCKETS + 1, 1])
            hi = m.sb(c1, "bucket_hi", [BUCKETS + 1, 1])
            dist = m.sb(c1, "dist_row", [BUCKETS + 1, 2 * T])
            dge = m.sb(c1, "dist_ge", [BUCKETS + 1, 2 * T])
            onehot = m.sb(c1, "bucket_onehot", [BUCKETS + 1, 2 * T])
            vec = m.sb(c1, "bias_vec", [HEADS, 2 * T])
            pairs = m.sb(c1, "token_pairs", [P, 2, KV_HEADS, T])
            blocks = m.sb(c1, "cmp_inputs", [P, 2, CMP_BLOCK // 2, KV_HEADS, N_CMP])
            hid = m.sb(c1, "cmp_hidden", [P, 2, 2, KV_HEADS * N_CMP])
            w2 = m.sb(c1, "cmp_w2_sb", [P, 2, 2, DH])
            qpair = attn[:, :, :].rearrange("p t (j g d) -> p t j g d", g=KV_HEADS, d=DH)
            qpair_ready = m.sem("query_pairs_ready")
            vc = m.sb(c1, "v_cmp", [N_CMP, KV_HEADS, DH])
            lo_ready, hi_ready, table_loaded = m.sem("bucket_lo_ready"), m.sem("bucket_hi_ready"), m.sem("bias_table_loaded")
            onehot_ready, vec_ready, vec_stored = m.sem("onehot_ready"), m.sem("bias_vec_ready"), m.sem("bias_vec_stored")
            kv_turned, pairs_zero, pairs_loaded = m.sem("kv_turned"), m.sem("pairs_zeroed"), m.sem("pairs_loaded")
            blocks_ready, hid_ready, w2_loaded = m.sem("cmp_inputs_ready"), m.sem("cmp_hidden_ready"), m.sem("cmp_w2_loaded")
            vc_ready, bias_loaded = m.sem("v_cmp_ready"), m.sem("bias_loaded")
            with nc.Block() as block:
                @block.gpsimd
                def _(pool):
                    L = m.pool_chain.on(pool)
                    L(pool.iota(dist[:, :], pattern=[[-1, 2 * T]], base=T - 1, channel_multiplier=0,
                                allow_small_or_imprecise_dtypes=True))
                    L(pool.memset(lo[:, :], -4.0 * T))
                    L(pool.memset(hi[:, :], 0.0))
                    for b in range(BUCKETS):
                        last = b == BUCKETS - 1
                        for t, v in ((lo, starts[b]), (hi, 8 * MAX_DIST if last else starts[b + 1])):
                            L(pool.affine_select(out=t[:, :], in_=t[:, :], compare_op=ALU.not_equal, fill=float(v),
                                                 base=-b, pattern=[[0, 1]], channel_multiplier=1))
                    pool.drain().then_inc(lo_ready, 1)
                    L(pool.memset(pairs[:, :, :, :], 0.0))
                    pool.memset(vblk[:, :, :], 0.0).then_inc(pairs_zero, 1)

                @block.sync
                def _(sp):
                    sp.dma_start(table[0:BUCKETS, :], io["rel_bias"]).then_inc(table_loaded, 16)
                    for kv in range(2):
                        m.weights.load(sp, io["cmp_w1"][0, kv], 0, 4 * DH)
                        sp.dma_start(w2[:, kv, :, :], io["cmp_w2"][0, kv].rearrange("(h p) d -> p h d", p=P)).then_inc(w2_loaded, 16)
                    sp.wait_ge(kv_turned, 1)
                    sp.wait_ge(pairs_zero, 1)
                    for kv in range(2):
                        for g in range(KV_HEADS):
                            src = kvT[g * DH:(g + 1) * DH, kv, :]
                            sp.dma_start(pairs[0:DH, kv, g, :], src).then_inc(pairs_loaded, 16)
                            sp.dma_start(pairs[DH:P, kv, g, 0:T - 1], src[:, 1:T]).then_inc(pairs_loaded, 16)
                    sp.wait_ge(vec_ready, 1)
                    sp.dma_start(bias_dram, view(vec[:, 0:1], [[0, P], [1, 2 * T]])).then_inc(vec_stored, 16)
                    sp.wait_ge(vec_stored, 16)
                    for h in range(HEADS):
                        src = bass.AP(tensor=bias_dram.tensor, offset=h * P * 2 * T + T - 1 - P, ap=[[2 * T - 1, P], [1, BIAS_W]])
                        sp.dma_start(bias[:, h, :], src).then_inc(bias_loaded, 16)
                    sp.wait_ge(vc_ready, 1)
                    for g in range(KV_HEADS):
                        for h in range(GROUP):
                            sp.dma_start(vblk[h * N_CMP:(h + 1) * N_CMP, g, h * DH:(h + 1) * DH], vc[:, g, :])\
                              .then_inc(bias_loaded, 16)
                    sp.wait_ge(bias_loaded, 16 * 2 * HEADS)

                @block.tensor
                def _(pe):
                    pe.wait_ge(qpair_ready, 1)
                    for j in range(2):
                        bank = m.to_dve.take(pe)
                        for u in range(2):
                            c = KV0 + (0, 1, 2, 4)[2 * j + u] * P
                            for tt in range(TT):
                                mm = pe.transpose(bank[:, (u * TT + tt) * P:(u * TT + tt + 1) * P],
                                                  proj[:, tt, c:c + P], st.ident[:, :])
                        m.to_dve.put(mm)
                    turn_to_columns(pe, m.to_dve, st.ident[:, :],
                                    lambda j, tt: qpair[:, tt, j, :, :].rearrange("p g d -> p (g d)"), 8)
                    pe.wait_ge(onehot_ready, 1)
                    bank = m.to_dve.take(pe)
                    m.to_dve.put(pe.matmul(bank[0:HEADS, :], table[:, :], onehot[:, :], start=True, stop=True))
                    pe.wait_ge(blocks_ready, 1)
                    for kv in range(2):
                        b, turn = m.weights.n_use % 2, m.weights.n_use // 2
                        pe.wait_ge(m.weights.loaded[b], 16 * (turn + 1))
                        bank = m.to_act.take(pe)
                        for hh in range(2):
                            for jj in range(KD):
                                mm = pe.matmul(bank[:, hh * 32:hh * 32 + KV_HEADS * N_CMP],
                                               m.weights.buf[b][:, jj, hh * P:(hh + 1) * P],
                                               blocks[:, kv, jj, :, :], start=(jj == 0), stop=(jj == KD - 1))
                        m.to_act.put(mm)
                        pe.drain().then_inc(m.weights.used[b], 1)
                        m.weights.n_use += 1
                    pe.wait_ge(hid_ready, 1)
                    pe.wait_ge(w2_loaded, 32)
                    bank = m.to_dve.take(pe)
                    for g in range(KV_HEADS):
                        for hh in range(2):
                            mm = pe.matmul(bank[g * DH:(g + 1) * DH, 0:N_CMP], w2[:, 0, hh, :],
                                           hid[:, 0, hh, g * N_CMP:(g + 1) * N_CMP], start=(hh == 0), stop=(hh == 1))
                    m.to_dve.put(mm)
                    bank = m.to_dve.take(pe)
                    for g in range(KV_HEADS):
                        for hh in range(2):
                            mm = pe.matmul(bank[0:N_CMP, g * DH:(g + 1) * DH], hid[:, 1, hh, g * N_CMP:(g + 1) * N_CMP],
                                           w2[:, 1, hh, :], start=(hh == 0), stop=(hh == 1))
                    m.to_dve.put(mm)

                @block.scalar
                def _(act):
                    act.activation(gates[:, :, :], proj[:, :, GATE0:GATE0 + 3 * HEADS], ACT.Sigmoid)
                    for kv in range(2):
                        bank = m.to_act.get(act)
                        m.to_act.free(act.activation(hid[:, kv, :, :], view(bank[:, 0:1], [[32, 2], [1, KV_HEADS * N_CMP]]),
                                                     ACT.Gelu_apprx_tanh))
                    act.drain().then_inc(hid_ready, 1)

                @block.vector
                def _(dve):
                    V = m.dve_chain.on(dve)
                    for tt in range(TT):
                        for g in range(KV_HEADS):
                            src = proj[:, tt, Q0 + g * HALF // 2:Q0 + (g + 1) * HALF // 2].rearrange("p (j d) -> p j d", d=DH)
                            dve.tensor_scalar(qpair[:, tt, :, g, :], src, DH ** -0.5, None, ALU.mult)
                    dve.drain().then_inc(qpair_ready, 1)
                    for j in range(2):
                        bank = m.to_dve.get(dve)
                        m.to_dve.free(dve.tensor_copy(kvT[:, 2 * j:2 * j + 2, :], bank[:, :]))
                    dve.drain().then_inc(kv_turned, 1)
                    for j in range(4):
                        bank = m.to_dve.get(dve)
                        m.to_dve.free(dve.tensor_copy(qT[:, 2 * j:2 * j + 2, :], bank[:, :]))
                    V(dve.memset(table[BUCKETS:BUCKETS + 1, :], NEG))
                    dve.wait_ge(lo_ready, 1)
                    V(dve.tensor_scalar(dge[:, :], dist[:, :], lo[:, 0:1], None, ALU.is_ge))
                    V(dve.scalar_tensor_tensor(out=onehot[:, :], in0=dist[:, :], scalar=hi[:, 0:1], in1=dge[:, :],
                                               op0=ALU.is_lt, op1=ALU.mult))
                    dve.wait_ge(table_loaded, 16)
                    dve.drain().then_inc(onehot_ready, 1)
                    bank = m.to_dve.get(dve)
                    m.to_dve.free(dve.tensor_copy(vec[:, :], bank[0:HEADS, :]))
                    dve.drain().then_inc(vec_ready, 1)
                    dve.wait_ge(pairs_loaded, 8 * 16)
                    for kv in range(2):
                        for g in range(KV_HEADS):
                            dve.tensor_tensor(blocks[:, kv, :, g, :],
                                              view(pairs[:, kv, g, 0:1], [[2, CMP_BLOCK // 2], [CMP_STRIDE, N_CMP]]),
                                              spread(st.vec.col("cmp_pe", kv * 16, 16), N_CMP), ALU.add)
                    dve.drain().then_inc(blocks_ready, 1)
                    bank = m.to_dve.get(dve)
                    m.to_dve.free(dve.tensor_copy(kcT[:, :], bank[:, 0:N_CMP]))
                    bank = m.to_dve.get(dve)
                    m.to_dve.free(dve.tensor_copy(vc[:, :, :], bank[0:N_CMP, 0:P]))
                    dve.drain().then_inc(vc_ready, 1)

        units = [(qt, g, br) for qt in range(TT) for g in range(KV_HEADS) for br in range(3)]
        with ExitStack() as c2:
            S = m.sb(c2, "scores", [P, 2, GROUP, T])
            PT = st.acts[:, 0:KD // 2, :].rearrange("p k (e q) -> p (k e) q", q=P)\
                        .rearrange("p (t h) q -> p t h q", h=GROUP)
            nmax = m.sb(c2, "neg_max", [P, len(units), GROUP])
            sums = m.sb(c2, "prob_sums", [P, len(units), GROUP])
            coef = m.sb(c2, "branch_coef", [P, len(units), GROUP])
            part = m.sb(c2, "branch_part", [P, GROUP, DH])
            rowok = m.sb(c2, "cmp_row_ok", [P, 1])
            shifted, probs, turned = m.sem("scores_shifted"), m.sem("probs_ready"), m.sem("probs_turned")
            pv_done, rowok_ready = m.sem("pv_done"), m.sem("row_ok_ready")
            with nc.Block() as block:
                def keys(qt, br):
                    return N_CMP if br == 0 else (qt + 1) * P

                @block.gpsimd
                def _(pool):
                    L = m.pool_chain.on(pool)
                    L(pool.memset(rowok[:, :], 1.0))
                    pool.affine_select(out=rowok[:, :], in_=rowok[:, :], compare_op=ALU.is_ge, fill=0.0,
                                       base=-(CMP_BLOCK - 1), pattern=[[0, 1]], channel_multiplier=1).then_inc(rowok_ready, 1)

                @block.tensor
                def _(pe):
                    def scores(u):
                        qt, g, br = units[u]
                        gp = slice(g * DH, (g + 1) * DH)
                        if br == 0:
                            bank = m.to_dve.take(pe)
                            for h in range(GROUP):
                                mm = pe.matmul(bank[:, h * N_CMP:(h + 1) * N_CMP], qT[gp, h, qt * P:(qt + 1) * P],
                                               kcT[gp, :], start=True, stop=True)
                            m.to_dve.put(mm)
                            return
                        n = keys(qt, br)
                        for h in range(0, GROUP, 2):
                            bank = m.to_dve.take(pe)
                            for e in range(2):
                                mm = pe.matmul(bank[:, e * T:e * T + n], qT[gp, h + e, qt * P:(qt + 1) * P],
                                               kvT[gp, 1 + br, 0:n], start=True, stop=True)
                            m.to_dve.put(mm)

                    def values(u):
                        qt, g, br = units[u]
                        pe.wait_ge(probs, u + 1)
                        if br == 0:
                            bank = m.to_act.take(pe)
                            m.to_act.put(pe.transpose(bank[0:GROUP * N_CMP, 0:P], view(S[:, u % 2, 0, 0:1], [[1, GROUP * N_CMP]]),
                                                      st.ident[:, :]))
                            pe.wait_ge(turned, u + 1)
                            bank = m.to_dve.take(pe)
                            mm = pe.matmul(bank[:, :], PT[0:GROUP * N_CMP, 0, 0, :], vblk[:, g, :], start=True, stop=True)
                            m.to_dve.put(mm)
                        else:
                            for kt in range(qt + 1):
                                for q4 in range(2):
                                    bank = m.to_act.take(pe)
                                    for e in range(4):
                                        mm = pe.transpose(bank[:, e * P:(e + 1) * P],
                                                          S[:, u % 2, q4 * 4 + e, kt * P:(kt + 1) * P], st.ident[:, :])
                                    m.to_act.put(mm)
                            pe.wait_ge(turned, u + 1)
                            bank = m.to_dve.take(pe)
                            for h in range(GROUP):
                                for kt in range(qt + 1):
                                    c = KV0 + (2 * br + 1) * P + g * DH
                                    mm = pe.matmul(bank[:, h * DH:(h + 1) * DH], PT[:, kt, h, :], proj[:, kt, c:c + DH],
                                                   start=(kt == 0), stop=(kt == qt))
                            m.to_dve.put(mm)
                        pe.drain().then_inc(pv_done, 1)

                    for u in range(len(units) + 1):
                        if u < len(units):
                            scores(u)
                        if u:
                            values(u - 1)

                @block.scalar
                def _(act):
                    for u, (qt, g, br) in enumerate(units):
                        act.wait_ge(shifted, u + 1)
                        if br == 0:
                            flat_s = view(S[:, u % 2, 0, 0:1], [[1, GROUP * N_CMP]])
                            act.activation(flat_s, flat_s, ACT.Exp)
                        else:
                            for h in range(GROUP):
                                row = S[:, u % 2, h, 0:keys(qt, br)]
                                act.activation(row, row, ACT.Exp, bias=nmax[:, u, h:h + 1],
                                               accum_out=sums[:, u, h:h + 1])
                        act.drain().then_inc(probs, 1)
                        if u:
                            act.wait_ge(pv_done, u)
                        if br == 0:
                            bank = m.to_act.get(act)
                            m.to_act.free(act.activation(PT[0:GROUP * N_CMP, 0, 0, :], bank[0:GROUP * N_CMP, 0:P], ACT.Copy))
                        else:
                            for kt in range(qt + 1):
                                for q4 in range(2):
                                    bank = m.to_act.get(act)
                                    m.to_act.free(act.activation(PT[:, kt, q4 * 4:q4 * 4 + 4, :], bank[:, :], ACT.Copy))
                        act.drain().then_inc(turned, 1)

                @block.vector
                def _(dve):
                    V = m.dve_chain.on(dve)

                    def shift(u):
                        qt, g, br = units[u]
                        n = keys(qt, br)
                        off = (TT - 1 - qt) * P
                        if u >= 2:
                            dve.wait_ge(pv_done, u - 1)
                        if br == 0:
                            s = view(S[:, u % 2, 0, 0:1], [[N_CMP, GROUP], [1, N_CMP]])
                            bank = m.to_dve.get(dve)
                            b = view(bias[:, g * GROUP, 0:1], [[BIAS_W, GROUP], [CMP_STRIDE, N_CMP]], off + CMP_BLOCK - 1)
                            m.to_dve.free(dve.tensor_tensor(s, view(bank[:, 0:1], [[N_CMP, GROUP], [1, N_CMP]]), b, ALU.add))
                            V(dve.engine_nop())
                            V(dve.tensor_reduce(nmax[:, u, :], s, AX_X, ALU.max))
                            V(dve.tensor_tensor(s, s, spread(nmax[:, u, :], N_CMP), ALU.subtract))
                        else:
                            for h in range(0, GROUP, 2):
                                bank = m.to_dve.get(dve)
                                m.to_dve.free(dve.tensor_tensor(
                                    S[:, u % 2, h:h + 2, 0:n], view(bank[:, 0:1], [[T, 2], [1, n]]),
                                    bias[:, g * GROUP + h:g * GROUP + h + 2, off:off + n], ALU.add))
                            V(dve.engine_nop())
                            V(dve.tensor_reduce(nmax[:, u, :], S[:, u % 2, :, 0:n], AX_X, ALU.max, negate=True))
                        dve.drain().then_inc(shifted, 1)

                    def combine(u):
                        qt, g, br = units[u]
                        dve.wait_ge(probs, u + 1)
                        if br == 0:
                            V(dve.tensor_reduce(sums[:, u, :], view(S[:, u % 2, 0, 0:1], [[N_CMP, GROUP], [1, N_CMP]]),
                                                AX_X, ALU.add))
                        V(dve.reciprocal(coef[:, u, :], sums[:, u, :]))
                        gate = view(gates[:, qt, 0:1], [[3, GROUP]], g * GROUP * 3 + br)
                        V(dve.tensor_tensor(coef[:, u, :], coef[:, u, :], gate, ALU.mult))
                        if br == 0 and qt == 0:
                            dve.wait_ge(rowok_ready, 1)
                            V(dve.tensor_scalar(coef[:, u, :], coef[:, u, :], rowok[:, 0:1], None, ALU.mult))
                        bank = m.to_dve.get(dve)
                        src = view(bank[:, 0:1], [[DH, GROUP], [1, DH]])
                        out = view(attn[:, qt, g * GROUP * DH:g * GROUP * DH + 1], [[DH, GROUP], [1, DH]])
                        if br == 0:
                            m.to_dve.free(dve.tensor_tensor(out, src, spread(coef[:, u, :], DH), ALU.mult))
                        else:
                            m.to_dve.free(dve.tensor_tensor(part[:, :, :], src, spread(coef[:, u, :], DH), ALU.mult))
                            V(dve.engine_nop())
                            V(dve.tensor_tensor(out, out, part[:, :, :], ALU.add))
                        V(dve.engine_nop())

                    for u in range(len(units) + 1):
                        if u < len(units):
                            shift(u)
                        if u:
                            combine(u - 1)


def turn_to_rows(pe, ring, ident, src, kt, per=4):
    for tt in range(TT):
        for k0 in range(0, kt, per):
            bank = ring.take(pe)
            for e in range(per):
                mm = pe.transpose(bank[:, e * P:(e + 1) * P], src(k0 + e, tt), ident)
            ring.put(mm)


def everywhere(ap, n):
    return bass.AP(tensor=ap.tensor, offset=ap.offset, ap=[[0, P], [1, n]])


def causal_conv(dve, V, src, dst, tiles, tap, first):
    for j in range(CONV_TAPS - 1, -1, -1):
        for k in range(tiles):
            u = src[:, k, j:j + T]
            if j == CONV_TAPS - 1:
                ins = first(k, u)
            else:
                ins = dve.scalar_tensor_tensor(out=dst[:, k, :], in0=u, scalar=tap(j, k), in1=dst[:, k, :],
                                               op0=ALU.mult, op1=ALU.add)
        V(ins)


class Softplus:

    TERMS = 10

    def __init__(self, m, ctx, name, n):
        self.x, self.e, self.z, self.w, self.s = (m.sb(ctx, f"{name}_sp_{s}", [n, T]) for s in "xezws")
        self.abs_ready, self.e_ready = m.sem(f"{name}_abs_ready"), m.sem(f"{name}_exp_ready")

    def on_dve(self, dve, V, out):
        x, e, z, w, s = (a[:, :] for a in (self.x, self.e, self.z, self.w, self.s))
        V(dve.scalar_tensor_tensor(out=e, in0=x, scalar=-1.0, in1=x, op0=ALU.mult, op1=ALU.max))
        dve.drain().then_inc(self.abs_ready, 1)
        dve.wait_ge(self.e_ready, 1)
        V(dve.tensor_scalar(z, e, 2.0, None, ALU.add))
        V(dve.reciprocal(z, z))
        V(dve.tensor_tensor(z, z, e, ALU.mult))
        V(dve.tensor_tensor(w, z, z, ALU.mult))
        V(dve.tensor_scalar(s, w, 1.0 / (2 * self.TERMS - 1), None, ALU.mult))
        for k in range(self.TERMS - 2, 0, -1):
            V(dve.scalar_tensor_tensor(out=s, in0=s, scalar=1.0 / (2 * k + 1), in1=w, op0=ALU.add, op1=ALU.mult))
        V(dve.scalar_tensor_tensor(out=s, in0=s, scalar=1.0, in1=z, op0=ALU.add, op1=ALU.mult))
        V(dve.tensor_scalar(s, s, 2.0, None, ALU.mult))
        V(dve.scalar_tensor_tensor(out=out, in0=x, scalar=0.0, in1=s, op0=ALU.max, op1=ALU.add))

    def on_act(self, act):
        act.wait_ge(self.abs_ready, 1)
        act.activation(self.e[:, :], self.e[:, :], ACT.Exp, scale=-1.0).then_inc(self.e_ready, 1)



SSM_HEADS, SSM_GROUPS = 16, 2
XBC_TILES, X_TILES = 12, 8


def stage_mamba(nc, m, io, st, proj, y):
    with ExitStack() as ctx:
        conv = m.sb(ctx, "xbc_conv", [P, XBC_TILES, T])
        xr = m.sb(ctx, "ssm_x_rows", [P, TT, HALF])
        dtc = m.sb(ctx, "dt_cols", [P, TT, SSM_HEADS])
        acsc = m.sb(ctx, "acs_cols", [P, TT, SSM_HEADS])
        cb = m.sb(ctx, "cb_masked", [P, SSM_GROUPS, TT, T])
        acs = m.sb(ctx, "acs", [SSM_HEADS, T])
        dsk = m.sb(ctx, "d_skip_rows", [P, SSM_HEADS])
        with ExitStack() as c1:
            u = m.sb(c1, "xbc_padded", [P, XBC_TILES, T + CONV_TAPS - 1])
            sp_ = Softplus(m, c1, "ssm", SSM_HEADS)
            dt = m.sb(c1, "dt", [SSM_HEADS, T])
            dta = m.sb(c1, "dt_a", [SSM_HEADS, T])
            ones = m.sb(c1, "ssm_ones", [SSM_HEADS, T])
            bias = m.sb(c1, "dt_bias_col", [SSM_HEADS, 1])
            alog = m.sb(c1, "a_log_col", [SSM_HEADS, 1])
            loaded, exp_a, conv_sum, conv_done = m.sem("ssm_small_loaded"), m.sem("ssm_exp_a"), m.sem("ssm_conv_summed"), m.sem("ssm_conv_done")
            acs_ready = m.sem("acs_ready")
            with nc.Block() as block:
                @block.sync
                def _(sp):
                    sp.dma_start(bias[:, :], io["dt_bias"].rearrange("a h -> h a")).then_inc(loaded, 16)
                    sp.dma_start(alog[:, :], io["a_log"].rearrange("a h -> h a")).then_inc(loaded, 16)
                    sp.dma_start(dsk[:, :], everywhere(io["d_skip"], SSM_HEADS)).then_inc(loaded, 16)
                    sp.wait_ge(loaded, 48)

                @block.scalar
                def _(act):
                    sp_.on_act(act)
                    act.wait_ge(loaded, 48)
                    act.activation(alog[:, :], alog[:, :], ACT.Exp).then_inc(exp_a, 1)
                    act.activation(proj[:, :, Z0:Z0 + HALF], proj[:, :, Z0:Z0 + HALF], ACT.Silu)
                    for k in range(XBC_TILES // 4):
                        act.wait_ge(conv_sum, k + 1)
                        act.activation(conv[:, 4 * k:4 * k + 4, :], conv[:, 4 * k:4 * k + 4, :], ACT.Silu)
                        act.drain().then_inc(conv_done, 1)

                @block.tensor
                def _(pe):
                    bank = m.to_dve.take(pe)
                    for tt in range(TT):
                        mm = pe.transpose(bank[0:SSM_HEADS, tt * P:(tt + 1) * P], proj[:, tt, DT0:DT0 + SSM_HEADS], st.ident[:, :])
                    m.to_dve.put(mm)
                    turn_to_columns(pe, m.to_dve, st.ident[:, :],
                                    lambda k, tt: proj[:, tt, XBC0 + k * P:XBC0 + (k + 1) * P], XBC_TILES)
                    pe.wait_ge(acs_ready, 1)
                    bank = m.to_dve.take(pe)
                    for i, src in enumerate((dt, acs)):
                        for tt in range(TT):
                            c = (i * TT + tt) * SSM_HEADS
                            mm = pe.transpose(bank[:, c:c + SSM_HEADS], src[:, tt * P:(tt + 1) * P],
                                              st.ident[0:SSM_HEADS, 0:SSM_HEADS])
                    m.to_dve.put(mm)
                    pe.wait_ge(conv_done, 3)
                    for g in range(SSM_GROUPS):
                        bank = m.to_dve.take(pe)
                        for tt in range(TT):
                            mm = pe.matmul(bank[:, tt * T:(tt + 1) * T], conv[:, X_TILES + g, tt * P:(tt + 1) * P],
                                           conv[:, X_TILES + SSM_GROUPS + g, :], start=True, stop=True)
                        m.to_dve.put(mm)
                    turn_to_rows(pe, m.to_dve, st.ident[:, :], lambda k, tt: conv[:, k, tt * P:(tt + 1) * P], X_TILES)

                @block.vector
                def _(dve):
                    V = m.dve_chain.on(dve)
                    V(dve.memset(u[:, :, 0:CONV_TAPS - 1], 0.0))
                    V(dve.memset(ones[:, :], 1.0))
                    dve.wait_ge(loaded, 48)
                    bank = m.to_dve.get(dve)
                    m.to_dve.free(dve.tensor_scalar(sp_.x[:, :], bank[0:SSM_HEADS, 0:T], bias[:, 0:1], None, ALU.add))
                    V(dve.engine_nop())
                    for j in range(XBC_TILES // 2):
                        bank = m.to_dve.get(dve)
                        m.to_dve.free(dve.tensor_copy(u[:, 2 * j:2 * j + 2, CONV_TAPS - 1:], view(bank[:, 0:1], [[T, 2], [1, T]])))
                    sp_.on_dve(dve, V, dt[:, :])
                    dve.wait_ge(exp_a, 1)
                    V(dve.tensor_scalar(dta[:, :], dt[:, :], alog[:, 0:1], -1.0, ALU.mult, ALU.mult))
                    V(dve.tensor_tensor_scan(acs[:, :], ones[:, :], dta[:, :], 0.0, ALU.mult, ALU.add))
                    dve.drain().then_inc(acs_ready, 1)
                    for k in range(XBC_TILES // 4):
                        causal_conv(dve, V, u[:, 4 * k:4 * k + 4, :], conv[:, 4 * k:4 * k + 4, :], 4,
                                    lambda j, i: st.vec.col("conv_w", j * XBC_TILES + 4 * k + i),
                                    lambda i, src: dve.tensor_scalar(conv[:, 4 * k + i, :], src,
                                                                     st.vec.col("conv_w", (CONV_TAPS - 1) * XBC_TILES + 4 * k + i),
                                                                     st.vec.col("conv_b", 4 * k + i), ALU.mult, ALU.add))
                        dve.drain().then_inc(conv_sum, 1)
                    bank = m.to_dve.get(dve)
                    n = TT * SSM_HEADS
                    dve.tensor_copy(dtc[:, :, :], bank[:, 0:n])
                    m.to_dve.free(dve.tensor_copy(acsc[:, :, :], bank[:, n:2 * n]))
                    for g in range(SSM_GROUPS):
                        bank = m.to_dve.get(dve)
                        dve.tensor_tensor(cb[:, g, 0, 0:P], bank[:, 0:P], st.incl[:, :], ALU.mult)
                        dve.tensor_copy(cb[:, g, 0, P:T], bank[:, P:T])
                        m.to_dve.free(dve.tensor_tensor(cb[:, g, 1, P:T], bank[:, T + P:2 * T], st.incl[:, :], ALU.mult))
                    for tt in range(TT):
                        for k in range(2):
                            bank = m.to_dve.get(dve)
                            m.to_dve.free(dve.tensor_copy(xr[:, tt, k * CHUNK:(k + 1) * CHUNK], bank[:, :]))
        with ExitStack() as c2:
            GH = SSM_HEADS // SSM_GROUPS
            M = m.sb(c2, "decay_T", [P, GH, T + P])
            seg, dec, mready = m.sem("segments_ready"), m.sem("decays_ready"), m.sem("ssm_mix_ready")
            y_read = m.sem("ssm_y_read")
            with nc.Block() as block:
                @block.tensor
                def _(pe):
                    for g in range(SSM_GROUPS):
                        for j in range(GH // 2):
                            bank = m.to_dve.take(pe)
                            for e in range(2):
                                h = g * GH + 2 * j + e
                                mm = pe.matmul(bank[:, e * T:(e + 1) * T], view(st.ident[0:SSM_HEADS, h:h + 1], [[0, P]]),
                                               acs[:, :], start=True, stop=True)
                            m.to_dve.put(mm)
                        pe.wait_ge(mready, g + 1)
                        for lt in range(TT):
                            bank = m.to_dve.take(pe)
                            for h in range(GH):
                                for s in range(lt + 1):
                                    lhs = M[:, h, lt * P:(lt + 1) * P] if s == 0 else M[:, h, T:T + P]
                                    c = (g * GH + h) * DH
                                    mm = pe.matmul(bank[:, h * DH:(h + 1) * DH], lhs, xr[:, s, c:c + DH],
                                                   start=(s == 0), stop=(s == lt))
                            m.to_dve.put(mm)

                @block.scalar
                def _(act):
                    for g in range(SSM_GROUPS):
                        act.wait_ge(seg, g + 1)
                        act.activation(M[:, :, :], M[:, :, :], ACT.Exp).then_inc(dec, 1)

                @block.vector
                def _(dve):
                    V = m.dve_chain.on(dve)
                    for g in range(SSM_GROUPS):
                        for j in range(GH // 2):
                            bank = m.to_dve.get(dve)
                            for e in range(2):
                                h = g * GH + 2 * j + e
                                dve.tensor_scalar(M[:, 2 * j + e, 0:T], bank[:, e * T:(e + 1) * T], acsc[:, 0, h:h + 1], 0.0,
                                                  ALU.subtract, ALU.min)
                                ins = dve.tensor_scalar(M[:, 2 * j + e, T:T + P], bank[:, e * T + P:(e + 1) * T],
                                                        acsc[:, 1, h:h + 1], 0.0, ALU.subtract, ALU.min)
                            m.to_dve.free(ins)
                        dve.drain().then_inc(seg, 1)
                        dve.wait_ge(dec, g + 1)
                        for j in range(GH):
                            h = g * GH + j
                            dve.scalar_tensor_tensor(out=M[:, j, 0:T], in0=M[:, j, 0:T], scalar=dtc[:, 0, h:h + 1],
                                                     in1=cb[:, g, 0, :], op0=ALU.mult, op1=ALU.mult)
                            dve.scalar_tensor_tensor(out=M[:, j, T:T + P], in0=M[:, j, T:T + P], scalar=dtc[:, 1, h:h + 1],
                                                     in1=cb[:, g, 1, P:T], op0=ALU.mult, op1=ALU.mult)
                        dve.drain().then_inc(mready, 1)
                        for lt in range(TT):
                            cols = slice(g * CHUNK, (g + 1) * CHUNK)
                            V(dve.tensor_tensor(view(y[:, lt, g * CHUNK:g * CHUNK + 1], [[DH, GH], [1, DH]]),
                                                view(xr[:, lt, g * CHUNK:g * CHUNK + 1], [[DH, GH], [1, DH]]),
                                                spread(dsk[:, g * GH:(g + 1) * GH], DH), ALU.mult))
                            bank = m.to_dve.get(dve)
                            m.to_dve.free(dve.tensor_tensor(y[:, lt, cols], bank[:, :], y[:, lt, cols], ALU.add))
                            V(dve.engine_nop())
                            V(dve.tensor_tensor(y[:, lt, cols], y[:, lt, cols],
                                                proj[:, lt, Z0 + g * CHUNK:Z0 + (g + 1) * CHUNK], ALU.mult))


def project_residual(nc, m, st, w, gain=None):
    with ExitStack() as ctx:
        tmp = m.sb(ctx, "residual_tmp", [P, TT, CHUNK])
        if gain is not None:
            row = m.sb(ctx, "residual_gain", [P, D])
        gain_loaded = m.sem("residual_gain_loaded")
        st.gain_count += gain is not None
        with nc.Block() as block:
            @block.sync
            def _(sp):
                if gain is not None:
                    sp.dma_start(row[:, :], everywhere(gain, D)).then_inc(gain_loaded, 16)
                for c, size in chunks(D):
                    m.weights.load(sp, w, c, size)

            @block.tensor
            def _(pe):
                for c, size in chunks(D):
                    m.weights.multiply(pe, st.acts, KD, size, m.to_dve)

            @block.vector
            def _(dve):
                V = m.dve_chain.on(dve)
                if gain is not None:
                    dve.wait_ge(gain_loaded, 16 * st.gain_count)
                for c, size in chunks(D):
                    for tt in range(TT):
                        bank = m.to_dve.get(dve)
                        xs = st.x[:, tt, c:c + size]
                        if gain is None:
                            m.to_dve.free(dve.tensor_tensor(xs, bank[:, :], xs, ALU.add))
                            continue
                        m.to_dve.free(dve.tensor_tensor(tmp[:, tt, :], bank[:, :], row[:, c:c + size], ALU.mult))
                        V(dve.engine_nop())
                        dve.tensor_tensor(xs, xs, tmp[:, tt, :], ALU.add)


def norm_rows(nc, m, st, name, x, gain, store=None):
    with ExitStack() as ctx:
        squares = m.sb(ctx, f"{name}_squares", [P, D])
        row = m.sb(ctx, f"{name}_gain", [P, D])
        ms = m.sb(ctx, f"{name}_ms", [P, TT])
        rinv = m.sb(ctx, f"{name}_rinv", [P, TT])
        squared, mean_ready, root_ready = m.sem(f"{name}_squared"), m.sem(f"{name}_mean_ready"), m.sem(f"{name}_root_ready")
        row_loaded, stored, scaled = m.sem(f"{name}_gain_loaded"), m.sem(f"{name}_stored"), m.sem(f"{name}_rows_scaled")
        with nc.Block() as block:
            @block.sync
            def _(sp):
                sp.dma_start(row[:, :], everywhere(gain, D)).then_inc(row_loaded, 16)
                if store is not None:
                    for tt in range(TT):
                        sp.wait_ge(scaled, tt + 1)
                        sp.dma_start(store[0, tt * P:(tt + 1) * P, :], x[:, tt, :]).then_inc(stored, 16)
                    sp.wait_ge(stored, 16 * TT)

            @block.scalar
            def _(act):
                A = m.act_chain.on(act)
                for tt in range(TT):
                    A(act.activation(squares[:, :], x[:, tt, :], ACT.Square, accum_out=ms[:, tt:tt + 1]))
                act.drain().then_inc(squared, 1)
                act.wait_ge(mean_ready, 1)
                act.activation(rinv[:, :], ms[:, :], ACT.Sqrt).then_inc(root_ready, 1)

            @block.vector
            def _(dve):
                V = m.dve_chain.on(dve)
                dve.wait_ge(squared, 1)
                dve.tensor_scalar(ms[:, :], ms[:, :], 1.0 / D, EPS, ALU.mult, ALU.add).then_inc(mean_ready, 1)
                dve.wait_ge(root_ready, 1)
                V(dve.reciprocal(rinv[:, :], rinv[:, :]))
                dve.wait_ge(row_loaded, 16)
                for tt in range(TT):
                    dve.scalar_tensor_tensor(out=x[:, tt, :], in0=x[:, tt, :], scalar=rinv[:, tt:tt + 1], in1=row[:, :],
                                             op0=ALU.mult, op1=ALU.mult).then_inc(scaled, 1)



HK = PEER_HEADS * TOPK


def stage_choose(nc, m, io, st, i1T, i2T, gateT):
    LISTS = 2 * PEER_HEADS
    with ExitStack() as ctx:
        sc = m.sb(ctx, "key_scores", [P, TT, LISTS, P])
        with ExitStack() as c1:
            q = m.sb(c1, "peer_q", [P, TT, D])
            qT = m.sb(c1, "peer_qT", [P, LISTS, T])
            sk = m.sb(c1, "subkeys", [P, 2, P])
            skT = m.sb(c1, "subkeys_T", [P, 2, P])
            project(nc, m, st, st.acts, KD, io["peer_wq"][0], 0, D, lambda tt, c, n: q[:, tt, c:c + n])
            sk_loaded, turned = m.sem("subkeys_loaded"), m.sem("peer_q_turned")
            with nc.Block() as block:
                @block.sync
                def _(sp):
                    sp.dma_start(sk[:, :, :], io["peer_subkeys"][0].rearrange("s k d -> k s d")).then_inc(sk_loaded, 16)

                @block.tensor
                def _(pe):
                    turn_to_columns(pe, m.to_dve, st.ident[:, :], lambda k, tt: q[:, tt, k * P:(k + 1) * P], LISTS)
                    pe.wait_ge(sk_loaded, 16)
                    bank = m.to_dve.take(pe)
                    for s in range(2):
                        mm = pe.transpose(bank[:, s * P:(s + 1) * P], sk[:, s, :], st.ident[:, :])
                    m.to_dve.put(mm)
                    pe.wait_ge(turned, 1)
                    for tt in range(TT):
                        for j in range(LISTS // 4):
                            bank = m.to_dve.take(pe)
                            for e in range(4):
                                mm = pe.matmul(bank[:, e * P:(e + 1) * P], qT[:, 4 * j + e, tt * P:(tt + 1) * P],
                                               skT[:, e % 2, :], start=True, stop=True)
                            m.to_dve.put(mm)

                @block.vector
                def _(dve):
                    for j in range(LISTS // 2):
                        bank = m.to_dve.get(dve)
                        m.to_dve.free(dve.tensor_copy(qT[:, 2 * j:2 * j + 2, :], bank[:, :]))
                    bank = m.to_dve.get(dve)
                    m.to_dve.free(dve.tensor_copy(skT[:, :, :], bank[:, 0:2 * P]))
                    dve.drain().then_inc(turned, 1)
                    for tt in range(TT):
                        for j in range(LISTS // 4):
                            bank = m.to_dve.get(dve)
                            m.to_dve.free(dve.tensor_copy(sc[:, tt, 4 * j:4 * j + 4, :], bank[:, :]))
        with ExitStack() as c2:
            vals = m.sb(c2, "key_best", [P, TT, LISTS, TOPK])
            idx = m.sb(c2, "key_index", [P, TT, LISTS, TOPK], U32)
            idxf = m.sb(c2, "key_index_f", [P, TT, LISTS, TOPK])
            cand = m.sb(c2, "candidates", [P, PEER_HEADS, TOPK * TOPK])
            best = m.sb(c2, "best", [P, TT, PEER_HEADS, TOPK])
            pos = m.sb(c2, "best_pos", [P, TT, PEER_HEADS, TOPK], U32)
            part = m.sb(c2, "pos_part", [P, TT, HK], U32)
            partf = m.sb(c2, "pos_part_f", [P, TT, HK])
            picks = m.sb(c2, "picks", [P, 3, TT, HK])
            hot = m.sb(c2, "rank_onehot", [P, HK, TOPK])
            tot = m.sb(c2, "gate_sums", [P, TT, PEER_HEADS])
            shifted, expd, ready = m.sem("best_shifted"), m.sem("best_exp"), m.sem("picks_ready")
            LOW = -3.0e38
            with nc.Block() as block:
                @block.vector
                def _(dve):
                    V = m.dve_chain.on(dve)

                    def top16(lists, v, ix):
                        for lo in (0, 8):
                            for i, src in enumerate(lists):
                                ins = dve.max(v(i)[:, lo:lo + 8], src)
                            V(ins)
                            for i, src in enumerate(lists):
                                ins = dve.max_index(ix(i)[:, lo:lo + 8], v(i)[:, lo:lo + 8], src)
                            V(ins)
                            if lo == 0:
                                for i, src in enumerate(lists):
                                    ins = dve.match_replace(src, v(i)[:, 0:8], src, LOW)
                                V(ins)

                    for tt in range(TT):
                        top16([sc[:, tt, i, :] for i in range(LISTS)], lambda i: vals[:, tt, i, :], lambda i: idx[:, tt, i, :])
                    V(dve.tensor_copy(idxf[:, :, :, :], idx[:, :, :, :]))
                    for tt in range(TT):
                        for h in range(PEER_HEADS):
                            ins = dve.tensor_tensor(cand[:, h, :].rearrange("p (a b) -> p a b", b=TOPK),
                                                    spread(vals[:, tt, 2 * h, :], TOPK),
                                                    view(vals[:, tt, 2 * h + 1, 0:1], [[0, TOPK], [1, TOPK]]), ALU.add)
                        V(ins)
                        top16([cand[:, h, :] for h in range(PEER_HEADS)], lambda h: best[:, tt, h, :], lambda h: pos[:, tt, h, :])
                    for half in range(2):
                        posv = pos[:, :, :, :].rearrange("p t h k -> p t (h k)")
                        if half == 0:
                            V(dve.tensor_scalar(part[:, :, :], posv, 4, None, ALU.logical_shift_right))
                        else:
                            V(dve.tensor_scalar(part[:, :, :], posv, TOPK - 1, None, ALU.bitwise_and))
                        V(dve.tensor_copy(partf[:, :, :], part[:, :, :]))
                        for tt in range(TT):
                            V(dve.tensor_tensor(hot[:, :, :], view(st.iota_row[:, 0:1], [[0, HK], [1, TOPK]]),
                                                spread(partf[:, tt, :], TOPK), ALU.is_equal))
                            keyv = view(idxf[:, tt, half, 0:1], [[2 * TOPK, PEER_HEADS], [0, TOPK], [1, TOPK]])
                            hotv = hot[:, :, :].rearrange("p (h k) a -> p h k a", k=TOPK)
                            V(dve.tensor_tensor(hotv, hotv, keyv, ALU.mult))
                            V(dve.tensor_reduce(picks[:, half, tt, :], hot[:, :, :], AX_X, ALU.add))
                    for tt in range(TT):
                        V(dve.tensor_copy(tot[:, tt, :], view(best[:, tt, 0, 0:1], [[TOPK, PEER_HEADS]])))
                        V(dve.tensor_tensor(best[:, tt, :, :], best[:, tt, :, :], spread(tot[:, tt, :], TOPK), ALU.subtract))
                    dve.drain().then_inc(shifted, 1)
                    dve.wait_ge(expd, 1)
                    V(dve.tensor_reduce(tot[:, :, :], best[:, :, :, :], AX_X, ALU.add))
                    V(dve.reciprocal(tot[:, :, :], tot[:, :, :]))
                    for tt in range(TT):
                        dve.tensor_tensor(picks[:, 2, tt, :].rearrange("p (h k) -> p h k", k=TOPK), best[:, tt, :, :],
                                          spread(tot[:, tt, :], TOPK), ALU.mult)
                    dve.drain().then_inc(ready, 1)
                    for dst in (i1T, i2T, gateT):
                        bank = m.to_dve.get(dve)
                        m.to_dve.free(dve.tensor_copy(dst[:, :], bank[:, 0:T]))

                @block.scalar
                def _(act):
                    act.wait_ge(shifted, 1)
                    act.activation(best[:, :, :, :], best[:, :, :, :], ACT.Exp).then_inc(expd, 1)

                @block.tensor
                def _(pe):
                    pe.wait_ge(ready, 1)
                    for i in range(3):
                        bank = m.to_dve.take(pe)
                        for tt in range(TT):
                            mm = pe.transpose(bank[:, tt * P:(tt + 1) * P], picks[:, i, tt, :], st.ident[:, :])
                        m.to_dve.put(mm)


def stage_experts(nc, m, io, st):
    NT = EXPERTS_SIDE // 2
    STEP = 4
    TOK = 8
    with ExitStack() as ctx:
        i1T, i2T, gateT = (m.sb(ctx, n, [P, T]) for n in ("i1_cols", "i2_cols", "gate_cols"))
        stage_choose(nc, m, io, st, i1T, i2T, gateT)
        gates = m.sb(ctx, "gates", [P, T, NT])
        y = m.sb(ctx, "expert_sum", [P, TT, D])
        act_sb = m.sb(ctx, "expert_act", [P, STEP, T])
        uv = [b[:, :, :].rearrange("p k n -> p (k n)").rearrange("p (s d) -> p s d", d=D) for b in m.weights.buf]
        u_sb, uT, v_sb = uv[0][:, 0:2, :], uv[0][:, 2:4, :], uv[1]
        uTv = uT.rearrange("p b (k e) -> p b k e", e=P)
        u_loaded = [m.sem(f"u_loaded{b}") for b in range(2)]
        v_loaded = [m.sem(f"v_loaded{b}") for b in range(STEP)]
        uT_ready, act_ready, gated, y_added = m.sem("uT_ready"), m.sem("expert_act_ready"), m.sem("expert_gated"), m.sem("expert_sum_added")
        hot_ready, hot_used = m.sem("onehots_ready"), [m.sem(f"onehots_used{b}") for b in range(2)]
        y_zero = m.sem("expert_sum_zeroed")
        for half in range(2):
            with ExitStack() as c1:
                hot2 = m.sb(c1, "onehot_i2", [P, 2, TOK, P])
                hot1 = m.sb(c1, "onehot_i1", [P, 2, TOK, NT])
                groups = T // TOK
                g0 = half * groups
                with nc.Block() as block:
                    @block.vector
                    def _(dve):
                        if half == 0:
                            dve.memset(y[:, :, :], 0.0).then_inc(y_zero, 1)
                        m.dve_chain.on(dve)
                        V = m.dve_chain
                        with dve.Fori(0, groups // 2) as i:
                            V.enter(i, 4)
                            for b in range(2):
                                tok = i * 2 * TOK + b * TOK
                                dve.wait_ge(hot_used[b], g0 // 2 + i)
                                V(dve.tensor_tensor(hot1[:, b, :, :], view(st.iota_row[:, 0:1], [[0, TOK], [1, NT]], half * NT),
                                                    spread(i1T[:, bass.ds(tok, TOK)], NT), ALU.is_equal))
                                V(dve.tensor_tensor(hot1[:, b, :, :], hot1[:, b, :, :],
                                                    spread(gateT[:, bass.ds(tok, TOK)], NT), ALU.mult))
                                dve.tensor_tensor(hot2[:, b, :, :], view(st.iota_row[:, 0:1], [[0, TOK], [1, P]]),
                                                  spread(i2T[:, bass.ds(tok, TOK)], P), ALU.is_equal).then_inc(hot_ready, 1)
                        V.leave(groups // 2)

                    @block.tensor
                    def _(pe):
                        with pe.Fori(0, groups // 4) as i:
                            m.to_act.enter_fill(i, 4)
                            for q4 in range(4):
                                b = q4 % 2
                                pe.wait_ge(hot_ready, g0 + 4 * i + q4 + 1)
                                bank = m.to_act.take(pe)
                                for t in range(TOK):
                                    mm = pe.matmul(bank[:, t * NT:(t + 1) * NT], hot2[:, b, t, :], hot1[:, b, t, :],
                                                   start=True, stop=True)
                                m.to_act.put(mm)
                        m.to_act.leave_fill(groups // 4, 4)

                    @block.scalar
                    def _(act):
                        with act.Fori(0, groups // 4) as i:
                            m.to_act.enter_empty(i, 4)
                            for q4 in range(4):
                                bank = m.to_act.get(act)
                                tok = i * 4 * TOK + q4 * TOK
                                m.to_act.free(act.activation(gates[:, bass.ds(tok, TOK), :],
                                                             bank[:, :].rearrange("p (t e) -> p t e", e=NT), ACT.Copy))
                                act.drain().then_inc(hot_used[q4 % 2], 1)
                        m.to_act.leave_empty(groups // 4, 4)
            steps = NT // STEP
            s0 = half * steps
            with nc.Block() as block:
                @block.sync
                def _(sp):
                    with sp.Fori(0, steps) as i:
                        for t in range(STEP):
                            row = (half * NT + i * STEP + t) * P
                            n = (s0 + i) * STEP + t
                            sp.wait_ge(uT_ready, n - t if half == 0 and t < 2 else n - 1)
                            sp.dma_start(u_sb[:, t % 2, :], io["peer_u"][0, bass.ds(row, P), :]).then_inc(u_loaded[t % 2], 16)

                @block.gpsimd
                def _(pool):
                    with pool.Fori(0, steps) as i:
                        pool.wait_ge(y_added, (s0 + i) * 2)
                        for t in range(STEP):
                            row = (half * NT + i * STEP + t) * P
                            pool.dma_start(v_sb[:, t, :], io["peer_v"][0, bass.ds(row, P), :]).then_inc(v_loaded[t], 16)

                @block.tensor
                def _(pe):
                    def turn(i, t):
                        pe.wait_ge(u_loaded[t % 2], 16 * (2 * (s0 + i) + t // 2 + 1))
                        for j in range(4):
                            bank = m.to_act.take(pe)
                            for e in range(4):
                                k = 4 * j + e
                                mm = pe.transpose(bank[:, e * P:(e + 1) * P], u_sb[:, t % 2, k * P:(k + 1) * P], st.ident[:, :])
                            m.to_act.put(mm)

                    def scores(i, t):
                        pe.wait_ge(uT_ready, (s0 + i) * STEP + t + 1)
                        bank = m.to_act.take(pe)
                        for k in range(KD):
                            mm = pe.matmul(bank[:, 0:T], uTv[:, t % 2, k, :], st.acts[:, k, :], start=(k == 0), stop=(k == KD - 1))
                        m.to_act.put(mm)

                    def sums(i, pair):
                        for t in (2 * pair, 2 * pair + 1):
                            pe.wait_ge(v_loaded[t], 16 * (s0 + i + 1))
                        pe.wait_ge(gated, (s0 + i) * STEP + 2 * pair + 2)
                        for tt in range(TT):
                            for c in range(4):
                                bank = m.to_dve.take(pe)
                                for t in (2 * pair, 2 * pair + 1):
                                    mm = pe.matmul(bank[:, :], act_sb[:, t, tt * P:(tt + 1) * P],
                                                   v_sb[:, t, c * CHUNK:(c + 1) * CHUNK], start=(t % 2 == 0), stop=(t % 2 == 1))
                                m.to_dve.put(mm)

                    with pe.Fori(0, steps) as i:
                        m.to_act.enter_fill(i, 20)
                        m.to_dve.enter_fill(i, 16)
                        turn(i, 0)
                        turn(i, 1)
                        scores(i, 0)
                        turn(i, 2)
                        scores(i, 1)
                        turn(i, 3)
                        scores(i, 2)
                        sums(i, 0)
                        scores(i, 3)
                        sums(i, 1)
                    m.to_act.leave_fill(steps, 20)
                    m.to_dve.leave_fill(steps, 16)

                @block.scalar
                def _(act):
                    def turned(i, t):
                        for j in range(4):
                            bank = m.to_act.get(act)
                            m.to_act.free(act.activation(uTv[:, t % 2, 4 * j:4 * j + 4, :], bank[:, :], ACT.Copy))
                        act.drain().then_inc(uT_ready, 1)

                    def gelu(i, t):
                        bank = m.to_act.get(act)
                        act.wait_ge(y_added, 2 * (s0 + i))
                        m.to_act.free(act.activation(act_sb[:, t, :], bank[:, 0:T], ACT.Gelu_apprx_tanh))
                        act.drain().then_inc(act_ready, 1)

                    with act.Fori(0, steps) as i:
                        m.to_act.enter_empty(i, 20)
                        turned(i, 0)
                        turned(i, 1)
                        gelu(i, 0)
                        turned(i, 2)
                        gelu(i, 1)
                        turned(i, 3)
                        gelu(i, 2)
                        gelu(i, 3)
                    m.to_act.leave_empty(steps, 20)

                @block.vector
                def _(dve):
                    def gate(i, t):
                        dve.wait_ge(act_ready, (s0 + i) * STEP + t + 1)
                        g = gates[:, :, bass.ds(i * STEP + t, 1)].rearrange("p t e -> p (t e)")
                        dve.tensor_tensor(act_sb[:, t, :], act_sb[:, t, :], g, ALU.mult).then_inc(gated, 1)

                    def add(i, pair):
                        dve.wait_ge(y_added, 2 * (s0 + i) + pair)
                        for tt in range(TT):
                            for c in range(4):
                                bank = m.to_dve.get(dve)
                                part = y[:, tt, c * CHUNK:(c + 1) * CHUNK]
                                m.to_dve.free(dve.tensor_tensor(part, bank[:, :], part, ALU.add))
                        dve.drain().then_inc(y_added, 1)

                    dve.wait_ge(y_zero, 1)
                    with dve.Fori(0, steps) as i:
                        m.to_dve.enter_empty(i, 16)
                        gate(i, 0)
                        gate(i, 1)
                        gate(i, 2)
                        add(i, 0)
                        gate(i, 3)
                        add(i, 1)
                    m.to_dve.leave_empty(steps, 16)
        with ExitStack() as c3:
            row = m.sb(c3, "g2_row", [P, D])
            loaded = m.sem("g2_loaded")
            with nc.Block() as block:
                @block.sync
                def _(sp):
                    sp.dma_start(row[:, :], everywhere(st.mod_dram[5 * D:6 * D], D)).then_inc(loaded, 16)

                @block.vector
                def _(dve):
                    V = m.dve_chain.on(dve)
                    dve.wait_ge(loaded, 16)
                    for tt in range(TT):
                        V(dve.tensor_tensor(y[:, tt, :], y[:, tt, :], row[:, :], ALU.mult))
                        V(dve.tensor_tensor(st.x[:, tt, :], st.x[:, tt, :], y[:, tt, :], ALU.add))



UNITS = 8


class Inverse:

    def __init__(self, m, st, name, levels, AT, Tm, TT_, X, M):
        self.m, self.st, self.levels = m, st, levels
        self.AT, self.T, self.TT, self.X, self.M = AT, Tm, TT_, X, M
        self.first, self.mask, self.x = m.sem(f"{name}_first_ready"), m.sem(f"{name}_level_masked"), m.sem(f"{name}_x_ready")
        self.t, self.ready = m.sem(f"{name}_t_updated"), m.sem(f"{name}_a_ready")
        self.n = 0

    @staticmethod
    def h(a, half):
        return a[:, 4 * half:4 * half + 4, :]

    def bank3(self, bank):
        return bank[:, :].rearrange("p (u t) -> p u t", t=P)

    def level(self, lv):
        return view(self.st.level[:, lv, 0:1], [[0, 4], [1, P]])

    def on_pool(self, pool):
        pool.wait_ge(self.ready, self.n + 1)
        for lv in range(1, self.levels):
            for half in range(2):
                pool.wait_ge(self.x, 2 * ((self.levels - 1) * self.n + lv - 1) + half + (0 if lv > 1 else 0))
                pool.tensor_tensor(self.h(self.M, half), self.h(self.AT, half), self.level(lv), ALU.mult)\
                    .then_inc(self.mask, 1)

    def on_pe(self, pe):
        m, base = self.m, 2 * (self.levels - 1) * self.n
        pe.wait_ge(self.first, self.n + 1)
        for half in range(2):
            bank = m.to_dve.take(pe)
            for u in range(4):
                mm = pe.transpose(bank[:, u * P:(u + 1) * P], self.TT[:, 4 * half + u, :], self.st.ident[:, :])
            m.to_dve.put(mm)
        for lv in range(1, self.levels):
            last = lv == self.levels - 1
            for half in range(2):
                n = base + 2 * (lv - 1) + half
                pe.wait_ge(self.mask, n + 1)
                pe.wait_ge(self.t, n + 2 * self.n + 1)
                bank = m.to_act.take(pe)
                for u in range(4 * half, 4 * half + 4):
                    mm = pe.matmul(bank[:, (u % 4) * P:(u % 4 + 1) * P], self.M[:, u, :], self.T[:, u, :], start=True, stop=True)
                m.to_act.put(mm)
            for half in range(2):
                n = base + 2 * (lv - 1) + half
                pe.wait_ge(self.x, n + 1)
                if not last:
                    bank = m.to_dve.take(pe)
                    for u in range(4 * half, 4 * half + 4):
                        mm = pe.matmul(bank[:, (u % 4) * P:(u % 4 + 1) * P], self.TT[:, u, :], self.X[:, u, :], start=True, stop=True)
                    m.to_dve.put(mm)
                bank = m.to_dve.take(pe)
                for u in range(4 * half, 4 * half + 4):
                    mm = pe.matmul(bank[:, (u % 4) * P:(u % 4 + 1) * P], self.X[:, u, :], self.TT[:, u, :], start=True, stop=True)
                m.to_dve.put(mm)

    def on_act(self, act):
        for lv in range(1, self.levels):
            for half in range(2):
                bank = self.m.to_act.get(act)
                self.m.to_act.free(act.activation(self.h(self.X, half), self.bank3(bank), ACT.Copy))
                act.drain().then_inc(self.x, 1)

    def on_dve(self, dve, V):
        m = self.m
        dve.drain().then_inc(self.ready, 1)
        for half in range(2):
            V(dve.tensor_tensor(self.h(self.TT, half), self.h(self.AT, half), self.level(0), ALU.mult))
            V(dve.tensor_tensor(self.h(self.TT, half), view(self.st.ident[:, 0:1], [[0, 4], [1, P]]),
                                self.h(self.TT, half), ALU.subtract))
        dve.drain().then_inc(self.first, 1)
        for half in range(2):
            bank = m.to_dve.get(dve)
            m.to_dve.free(dve.tensor_copy(self.h(self.T, half), self.bank3(bank)))
            dve.drain().then_inc(self.t, 1)
        for lv in range(1, self.levels):
            last = lv == self.levels - 1
            for half in range(2):
                for dst in ((self.TT,) if last else (self.T, self.TT)):
                    if dst is self.TT and not last:
                        pass
                    bank = m.to_dve.get(dve)
                    if dst is self.T:
                        bank_t = bank
                        ins = dve.tensor_tensor(self.h(self.T, half), self.h(self.T, half), self.bank3(bank), ALU.subtract)
                    else:
                        ins = dve.tensor_tensor(self.h(self.TT, half), self.h(self.TT, half), self.bank3(bank), ALU.subtract)
                    m.to_dve.free(ins)
                dve.drain().then_inc(self.t, 1)
        dve.wait_ge(self.t, 2 * self.levels * (self.n + 1))


def arrays_of(buf, n, shape):
    size = int(np.prod(shape))
    flat_buf = buf[:, :, :].rearrange("p k n -> p (k n)")
    names = "abcd"[:len(shape)]
    out = []
    for i in range(n):
        a = flat_buf[:, i * size:(i + 1) * size]
        if len(shape) > 1:
            a = a.rearrange(f"p ({' '.join(names)}) -> p {' '.join(names)}", **{c: s for c, s in zip(names[1:], shape[1:])})
        out.append(a)
    return out



GH, GD = 8, 128


def stage_gdn(nc, m, io, st, cols):
    with ExitStack() as ctx:
        NP_ = RF0
        pr = m.sb(ctx, "gdn_rows", [P, TT, NP_])
        project(nc, m, st, st.acts, KD, io["w_in_2"][0], GQKV0, NP_, lambda tt, c, n: pr[:, tt, c:c + n])
        beta = m.sb(ctx, "gdn_beta", [P, TT, GH])
        gcum = m.sb(ctx, "gdn_gcum", [GH, T])
        gcol = m.sb(ctx, "gdn_gcol", [P, TT, GH])
        egcol = m.sb(ctx, "gdn_exp_gcol", [P, TT, GH])
        gl = m.sb(ctx, "gdn_g_last", [P, GH])
        nw = m.sb(ctx, "gdn_norm_row", [P, GD])
        ss = m.sb(ctx, "gdn_square_sums", [P, TT, 2 * GH])
        with ExitStack() as c1:
            u = m.sb(c1, "gdn_padded", [P, GH, T + CONV_TAPS - 1])
            cv = m.sb(c1, "gdn_conv", [P, GH, T])
            sp_ = Softplus(m, c1, "gdn", GH)
            g = m.sb(c1, "gdn_g", [GH, T])
            ones = m.sb(c1, "gdn_ones", [GH, T])
            bias, alog = m.sb(c1, "gdn_bias_col", [GH, 1]), m.sb(c1, "gdn_a_log_col", [GH, 1])
            loaded, exp_a, summed, silu = m.sem("gdn_small_loaded"), m.sem("gdn_exp_a"), m.sem("gdn_conv_summed"), m.sem("gdn_conv_done")
            gready, col_ready = m.sem("gdn_gcum_ready"), m.sem("gdn_gcol_ready")
            squared, ss_ready, root = m.sem("gdn_squared"), m.sem("gdn_ss_ready"), m.sem("gdn_root_ready")
            sq = arrays_of(m.weights.buf[0], 2, [2 * GH, GD])
            with nc.Block() as block:
                @block.sync
                def _(sp):
                    sp.dma_start(bias[:, :], io["gdn_dt_bias_2"].rearrange("a h -> h a")).then_inc(loaded, 16)
                    sp.dma_start(alog[:, :], io["gdn_a_log_2"].rearrange("a h -> h a")).then_inc(loaded, 16)
                    sp.dma_start(nw[:, :], everywhere(io["gdn_norm_w_2"], GD)).then_inc(loaded, 16)
                    sp.wait_ge(loaded, 48)

                @block.tensor
                def _(pe):
                    bank = m.to_dve.take(pe)
                    for tt in range(TT):
                        mm = pe.transpose(bank[0:GH, tt * P:(tt + 1) * P], pr[:, tt, GA0:GA0 + GH], st.ident[:, :])
                    m.to_dve.put(mm)
                    for part in range(3):
                        turn_to_columns(pe, m.to_dve, st.ident[:, :],
                                        lambda k, tt: pr[:, tt, (part * GH + k) * P:(part * GH + k + 1) * P], GH)
                        pe.wait_ge(silu, part + 1)
                        turn_to_rows(pe, m.to_dve, st.ident[:, :], lambda k, tt: cv[:, k, tt * P:(tt + 1) * P], GH)
                    pe.wait_ge(gready, 1)
                    bank = m.to_dve.take(pe)
                    for tt in range(TT):
                        mm = pe.transpose(bank[:, tt * GH:(tt + 1) * GH], gcum[:, tt * P:(tt + 1) * P], st.ident[0:GH, 0:GH])
                    m.to_dve.put(mm)

                @block.scalar
                def _(act):
                    sp_.on_act(act)
                    act.wait_ge(loaded, 48)
                    act.activation(alog[:, :], alog[:, :], ACT.Exp).then_inc(exp_a, 1)
                    act.activation(beta[:, :, :], pr[:, :, GB0:GB0 + GH], ACT.Sigmoid)
                    act.activation(pr[:, :, GZ0:GZ0 + HALF], pr[:, :, GZ0:GZ0 + HALF], ACT.Silu)
                    for part in range(3):
                        act.wait_ge(summed, part + 1)
                        act.activation(cv[:, :, :], cv[:, :, :], ACT.Silu).then_inc(silu, 1)
                    act.wait_ge(col_ready, 1)
                    act.activation(egcol[:, :, :], gcol[:, :, :], ACT.Exp)
                    for tt in range(TT):
                        act.activation(sq[tt], pr[:, tt, 0:2 * HALF].rearrange("p (h d) -> p h d", d=GD), ACT.Square)
                    act.drain().then_inc(squared, 1)
                    act.wait_ge(ss_ready, 1)
                    act.activation(ss[:, :, :], ss[:, :, :], ACT.Sqrt).then_inc(root, 1)

                @block.vector
                def _(dve):
                    V = m.dve_chain.on(dve)
                    V(dve.memset(u[:, :, 0:CONV_TAPS - 1], 0.0))
                    V(dve.memset(ones[:, :], 1.0))
                    dve.wait_ge(loaded, 48)
                    bank = m.to_dve.get(dve)
                    m.to_dve.free(dve.tensor_scalar(sp_.x[:, :], bank[0:GH, 0:T], bias[:, 0:1], None, ALU.add))
                    V(dve.engine_nop())
                    sp_.on_dve(dve, V, g[:, :])
                    dve.wait_ge(exp_a, 1)
                    V(dve.tensor_scalar(g[:, :], g[:, :], alog[:, 0:1], -1.0, ALU.mult, ALU.mult))
                    for tt in range(TT):
                        V(dve.tensor_tensor_scan(gcum[:, tt * P:(tt + 1) * P], ones[:, 0:P], g[:, tt * P:(tt + 1) * P],
                                                 0.0, ALU.mult, ALU.add))
                    dve.drain().then_inc(gready, 1)
                    for part in range(3):
                        for j in range(GH // 2):
                            bank = m.to_dve.get(dve)
                            m.to_dve.free(dve.tensor_copy(u[:, 2 * j:2 * j + 2, CONV_TAPS - 1:], view(bank[:, 0:1], [[T, 2], [1, T]])))
                        V(dve.engine_nop())
                        nt = 3 * GH
                        causal_conv(dve, V, u, cv, GH, lambda j, k: st.vec.col("gdn_conv_w_2", j * nt + part * GH + k),
                                    lambda k, src: dve.tensor_scalar(cv[:, k, :], src,
                                                                     st.vec.col("gdn_conv_w_2", (CONV_TAPS - 1) * nt + part * GH + k),
                                                                     None, ALU.mult))
                        dve.drain().then_inc(summed, 1)
                        for tt in range(TT):
                            for k in range(2):
                                bank = m.to_dve.get(dve)
                                c = part * HALF + k * CHUNK
                                m.to_dve.free(dve.tensor_copy(pr[:, tt, c:c + CHUNK], bank[:, :]))
                    bank = m.to_dve.get(dve)
                    m.to_dve.free(dve.tensor_copy(gcol[:, :, :], bank[:, 0:TT * GH]))
                    dve.drain().then_inc(col_ready, 1)
                    dve.wait_ge(squared, 1)
                    for tt in range(TT):
                        V(dve.tensor_reduce(ss[:, tt, :], sq[tt], AX_X, ALU.add))
                    V(dve.tensor_scalar(ss[:, :, :], ss[:, :, :], EPS, None, ALU.add))
                    dve.drain().then_inc(ss_ready, 1)
                    dve.wait_ge(root, 1)
                    V(dve.reciprocal(ss[:, :, :], ss[:, :, :]))
                    V(dve.tensor_scalar(ss[:, :, 0:GH], ss[:, :, 0:GH], GD ** -0.5, None, ALU.mult))
                    for tt in range(TT):
                        qk = pr[:, tt, 0:2 * HALF].rearrange("p (h d) -> p h d", d=GD)
                        V(dve.tensor_tensor(qk, qk, spread(ss[:, tt, :], GD), ALU.mult))

        def part_rows(i, tt):
            return pr[:, tt, i * HALF:(i + 1) * HALF].rearrange("p (h d) -> p h d", d=GD)

        with ExitStack() as c2:
            kb = m.sb(c2, "gdn_k_beta", [P, TT, GH, GD])
            kbg = m.sb(c2, "gdn_k_beta_decayed", [P, GH, GD])
            qd = m.sb(c2, "gdn_q_decayed", [P, GH, GD])
            kd = m.sb(c2, "gdn_k_decayed", [P, GH, GD])
            S = m.sb(c2, "gdn_state", [P, GH, GD])
            kT, kbT, qT, qdT, E, AT, QT, Tm = arrays_of(m.weights.buf[0], 8, [GH, GD])
            TT_, X, M, wT, un, sq2 = arrays_of(m.weights.buf[1], 6, [GH, GD])
            inv = Inverse(m, st, "gdn", 7, AT, Tm, TT_, X, M)
            rows_ready, seg, dec, cols_ready = m.sem("gdn_rows_ready"), m.sem("gdn_seg_ready"), m.sem("gdn_dec_ready"), m.sem("gdn_cols_ready")
            kq_ready, kd_sub, kd_exp, kd_ready = m.sem("gdn_kq_masked"), m.sem("gdn_kd_sub"), m.sem("gdn_kd_exp"), m.sem("gdn_kd_ready")
            tt_ready, u_ready, vn_ready, s_ready, w_ready = (m.sem("gdn_" + s) for s in ("tt_ready", "u_ready", "vn_ready", "s_ready", "w_ready"))
            o_ready, o_sq, o_ms, o_root, o_done = (m.sem("gdn_o_" + s) for s in ("ready", "squared", "ms", "root", "done"))
            with nc.Block() as block:
                @block.gpsimd
                def _(pool):
                    for c in range(TT):
                        inv.n = c
                        inv.on_pool(pool)

                @block.scalar
                def _(act):
                    for c in range(TT):
                        inv.n = c
                        act.wait_ge(seg, c + 1)
                        act.activation(E, E, ACT.Exp).then_inc(dec, 1)
                        if c == 0:
                            act.wait_ge(kd_sub, 1)
                            act.activation(gl[:, :], gl[:, :], ACT.Exp).then_inc(kd_exp, 1)
                        inv.on_act(act)
                    for tt in range(TT):
                        act.wait_ge(o_ready, tt + 1)
                        act.activation(sq2, part_rows(2, tt), ACT.Square).then_inc(o_sq, 1)
                        act.wait_ge(o_ms, tt + 1)
                        act.activation(ss[:, tt, 0:GH], ss[:, tt, 0:GH], ACT.Sqrt).then_inc(o_root, 1)

                @block.tensor
                def _(pe):
                    pe.wait_ge(rows_ready, 1)
                    for c in range(TT):
                        inv.n = c
                        srcs = [part_rows(1, c), kb[:, c, :, :], part_rows(0, c)] + ([qd[:, :, :]] if c else [])
                        for half in range(2):
                            for src in srcs:
                                bank = m.to_dve.take(pe)
                                for e in range(4):
                                    mm = pe.transpose(bank[:, e * P:(e + 1) * P], src[:, 4 * half + e, :], st.ident[:, :])
                                m.to_dve.put(mm)
                            bank = m.to_dve.take(pe)
                            for e in range(4):
                                h = 4 * half + e
                                mm = pe.matmul(bank[:, e * P:(e + 1) * P], view(st.ident[0:GH, h:h + 1], [[0, P]]),
                                               gcum[:, c * P:(c + 1) * P], start=True, stop=True)
                            m.to_dve.put(mm)
                        pe.wait_ge(cols_ready, c + 1)
                        for rhs in (kbT, qT):
                            for half in range(2):
                                bank = m.to_dve.take(pe)
                                for e in range(4):
                                    h = 4 * half + e
                                    mm = pe.matmul(bank[:, e * P:(e + 1) * P], kT[:, h, :], rhs[:, h, :], start=True, stop=True)
                                m.to_dve.put(mm)
                        inv.on_pe(pe)
                        pe.wait_ge(tt_ready, c + 1)

                        def per_head(fn):
                            for half in range(2):
                                bank = m.to_dve.take(pe)
                                for e in range(4):
                                    ins = fn(4 * half + e, bank[:, e * P:(e + 1) * P])
                                m.to_dve.put(ins)

                        v = part_rows(2, c)
                        per_head(lambda h, o: pe.matmul(o, TT_[:, h, :], v[:, h, :], start=True, stop=True))
                        if c:
                            per_head(lambda h, o: pe.matmul(o, kbg[:, h, :], TT_[:, h, :], start=True, stop=True))
                            pe.wait_ge(w_ready, 1)
                            per_head(lambda h, o: pe.matmul(o, wT[:, h, :], S[:, h, :], start=True, stop=True))
                        pe.wait_ge(vn_ready, c + 1)
                        if c == 0:
                            per_head(lambda h, o: pe.matmul(o, QT[:, h, :], un[:, h, :], start=True, stop=True))
                            pe.wait_ge(kd_ready, 1)
                            per_head(lambda h, o: pe.matmul(o, kd[:, h, :], un[:, h, :], start=True, stop=True))
                        else:
                            def out(h, o):
                                pe.matmul(o, qdT[:, h, :], S[:, h, :], start=True, stop=False)
                                return pe.matmul(o, QT[:, h, :], un[:, h, :], start=False, stop=True)
                            per_head(out)
                    pe.wait_ge(o_done, 1)
                    turn_to_columns(pe, m.to_dve, st.ident[:, :], lambda k, tt: part_rows(2, tt)[:, k, :], GH)

                @block.vector
                def _(dve):
                    V = m.dve_chain.on(dve)
                    for tt in range(TT):
                        dve.tensor_tensor(kb[:, tt, :, :], part_rows(1, tt), spread(beta[:, tt, :], GD), ALU.mult)
                        V(dve.tensor_tensor(part_rows(2, tt), part_rows(2, tt), spread(beta[:, tt, :], GD), ALU.mult))
                    V(dve.tensor_tensor(kbg[:, :, :], kb[:, 1, :, :], spread(egcol[:, 1, :], GD), ALU.mult))
                    V(dve.tensor_tensor(qd[:, :, :], part_rows(0, 1), spread(egcol[:, 1, :], GD), ALU.mult))
                    dve.drain().then_inc(rows_ready, 1)
                    for c in range(TT):
                        inv.n = c
                        h4 = inv.h
                        for half in range(2):
                            for dst in [kT, kbT, qT] + ([qdT] if c else []):
                                bank = m.to_dve.get(dve)
                                m.to_dve.free(dve.tensor_copy(h4(dst, half), inv.bank3(bank)))
                            bank = m.to_dve.get(dve)
                            if c == 0:
                                dve.tensor_copy(gl[:, 4 * half:4 * half + 4], view(bank[:, 0:1], [[P, 4]], P - 1))
                            for e in range(4):
                                h = 4 * half + e
                                ins = dve.tensor_scalar(E[:, h, :], bank[:, e * P:(e + 1) * P], gcol[:, c, h:h + 1], 0.0,
                                                        ALU.subtract, ALU.min)
                            m.to_dve.free(ins)
                        dve.drain().then_inc(seg, 1)
                        dve.drain().then_inc(cols_ready, 1)
                        dve.wait_ge(dec, c + 1)
                        if c == 0:
                            V(dve.tensor_tensor(gl[:, :], gl[:, :], gcol[:, 0, :], ALU.subtract))
                            dve.drain().then_inc(kd_sub, 1)
                        for dst, mask in ((AT, st.strict), (QT, st.incl)):
                            for half in range(2):
                                bank = m.to_dve.get(dve)
                                m.to_dve.free(dve.tensor_tensor(h4(dst, half), inv.bank3(bank), h4(E, half), ALU.mult))
                                V(dve.engine_nop())
                                V(dve.tensor_tensor(h4(dst, half), h4(dst, half), view(mask[:, 0:1], [[0, 4], [1, P]]), ALU.mult))
                        inv.on_dve(dve, V)
                        dve.drain().then_inc(tt_ready, 1)
                        for half in range(2):
                            bank = m.to_dve.get(dve)
                            m.to_dve.free(dve.tensor_copy(h4(un, half), inv.bank3(bank)))
                        if c:
                            for half in range(2):
                                bank = m.to_dve.get(dve)
                                m.to_dve.free(dve.tensor_copy(h4(wT, half), inv.bank3(bank)))
                            dve.drain().then_inc(w_ready, 1)
                            V(dve.engine_nop())
                            for half in range(2):
                                bank = m.to_dve.get(dve)
                                m.to_dve.free(dve.tensor_tensor(h4(un, half), h4(un, half), inv.bank3(bank), ALU.subtract))
                        dve.drain().then_inc(vn_ready, 1)
                        if c == 0:
                            dve.wait_ge(kd_exp, 1)
                            V(dve.tensor_tensor(kd[:, :, :], part_rows(1, 0), spread(gl[:, :], GD), ALU.mult))
                            dve.drain().then_inc(kd_ready, 1)
                        for half in range(2):
                            bank = m.to_dve.get(dve)
                            m.to_dve.free(dve.tensor_copy(h4(part_rows(2, c), half), inv.bank3(bank)))
                        dve.drain().then_inc(o_ready, 1)
                        if c == 0:
                            for half in range(2):
                                bank = m.to_dve.get(dve)
                                m.to_dve.free(dve.tensor_copy(h4(S, half), inv.bank3(bank)))
                            dve.drain().then_inc(s_ready, 1)
                            dve.wait_ge(s_ready, 1)
                    for tt in range(TT):
                        o = part_rows(2, tt)
                        dve.wait_ge(o_sq, tt + 1)
                        V(dve.tensor_reduce(ss[:, tt, 0:GH], sq2, AX_X, ALU.add))
                        dve.tensor_scalar(ss[:, tt, 0:GH], ss[:, tt, 0:GH], 1.0 / GD, EPS, ALU.mult, ALU.add).then_inc(o_ms, 1)
                        dve.wait_ge(o_root, tt + 1)
                        V(dve.reciprocal(ss[:, tt, 0:GH], ss[:, tt, 0:GH]))
                        V(dve.tensor_tensor(o, o, spread(ss[:, tt, 0:GH], GD), ALU.mult))
                        V(dve.tensor_tensor(o, o, view(nw[:, 0:1], [[0, GH], [1, GD]]), ALU.mult))
                        V(dve.tensor_tensor(o, o, part_rows(3, tt), ALU.mult))
                    dve.drain().then_inc(o_done, 1)
                    for j in range(GH // 2):
                        bank = m.to_dve.get(dve)
                        m.to_dve.free(dve.tensor_copy(cols[:, 2 * j:2 * j + 2, :], view(bank[:, 0:1], [[T, 2], [1, T]])))



RH, RN, RC = 16, 64, 64
LORA = 96
NR = 3 * HALF + 2 * LORA
PAIRS = RH // 2
LN_EPS = 64e-5


def stage_rwkv(nc, m, io, st, cols):
    with ExitStack() as ctx:
        NP_ = NR + HALF
        pr = m.sb(ctx, "rwkv_rows", [P, TT, NP_])
        project(nc, m, st, st.acts, KD, io["w_in_2"][0], RF0, NP_, lambda tt, c, n: pr[:, tt, c:c + n])
        Kt = m.sb(ctx, "rwkv_K", [P, TT, HALF])
        B = m.sb(ctx, "rwkv_B", [P, TT, HALF])
        pc = m.sb(ctx, "rwkv_chunk_decay", [P, PAIRS, 2 * TT])
        bonus = m.sb(ctx, "rwkv_bonus", [P, TT, RH])
        mask2 = m.sb(ctx, "rwkv_masks", [P, 2, P])
        small = m.sb(ctx, "rwkv_small", [P, TT, RH])
        small2 = m.sb(ctx, "rwkv_small2", [P, TT, RH])
        chunk_ind = m.sb(ctx, "chunk_indicator", [P, 2])

        def part(i, tt):
            return pr[:, tt, i * HALF:(i + 1) * HALF]

        def heads(ap):
            return ap.rearrange("p (h d) -> p h d", d=RN)

        with ExitStack() as c1:
            prev = arrays_of(m.weights.buf[0], 1, [TT, NR])[0]
            mu = arrays_of(m.weights.buf[1], 1, [NR])[0]
            shifted, mu_loaded, first_zero = m.sem("rwkv_prev_loaded"), m.sem("rwkv_mu_loaded"), m.sem("rwkv_first_zeroed")
            ind0 = m.sem("indicator_ones")
            with nc.Block() as block:
                @block.sync
                def _(sp):
                    sp.dma_start(mu, everywhere(io["rwkv_mu_2"], NR)).then_inc(mu_loaded, 16)
                    for tt in range(TT):
                        sp.dma_start(prev[1:P, tt, :], pr[0:P - 1, tt, 0:NR]).then_inc(shifted, 16)
                    sp.dma_start(prev[0:1, 1, :], pr[P - 1:P, 0, 0:NR]).then_inc(shifted, 16)

                @block.gpsimd
                def _(pool):
                    pool.memset(chunk_ind[:, :], 1.0).then_inc(ind0, 1)
                    pool.wait_ge(ind0, 1)
                    L = m.pool_chain.on(pool)
                    L(pool.affine_select(out=chunk_ind[:, 0:1], in_=chunk_ind[:, 0:1], compare_op=ALU.is_ge, fill=0.0,
                                         base=RC - 1, pattern=[[0, 1]], channel_multiplier=-1))
                    L(pool.affine_select(out=chunk_ind[:, 1:2], in_=chunk_ind[:, 1:2], compare_op=ALU.is_ge, fill=0.0,
                                         base=-RC, pattern=[[0, 1]], channel_multiplier=1))

                @block.vector
                def _(dve):
                    V = m.dve_chain.on(dve)
                    V(dve.memset(prev[0:1, 0, :], 0.0))
                    for i, mk in enumerate((st.strict, st.incl)):
                        V(dve.tensor_tensor(mask2[:, i, :], mk[:, :], st.same64[:, :], ALU.mult))
                    dve.wait_ge(shifted, 48)
                    dve.wait_ge(mu_loaded, 16)
                    for tt in range(TT):
                        f = pr[:, tt, 0:NR]
                        V(dve.tensor_tensor(prev[:, tt, :], prev[:, tt, :], f, ALU.subtract))
                        V(dve.tensor_tensor(prev[:, tt, :], prev[:, tt, :], mu, ALU.mult))
                        V(dve.tensor_tensor(f, f, prev[:, tt, :], ALU.add))
        bufs1 = arrays_of(m.weights.buf[0], 4, [TT, HALF]) + arrays_of(m.weights.buf[1], 3, [TT, HALF])
        lw, cum, ea, eb, kk, sq, aa = bufs1
        rows1 = arrays_of(m.weights.buf[1], 8, [HALF])[6:8]
        with ExitStack() as c1:
            wup = m.sb(c1, "rwkv_lora_up", [LORA, 2, HALF])
            lT = m.sb(c1, "rwkv_lora_T", [LORA, 2, T])
            brow = m.sb(c1, "rwkv_lora_bias", [P, 1, HALF])
            brow2, krow = rows1
            up_loaded, r_loaded, r_used = m.sem("rwkv_up_loaded"), m.sem("rwkv_row_loaded"), m.sem("rwkv_row_used")
            th_ready, l_ready, wp_ready, sg_ready = (m.sem("rwkv_" + s) for s in ("tanh_ready", "lora_T_ready", "pre_ready", "sigmoid_ready"))
            lw_ready, cum_ready, exps_ready, sqd, ssr, rtr = (m.sem("rwkv_" + s) for s in ("lw_ready", "cum_ready", "exps_ready", "kk_squared", "kk_ss_ready", "kk_root"))
            sq_used, ea_used = m.sem("rwkv_sq_used"), m.sem("rwkv_ea_used")
            with nc.Block() as block:
                @block.sync
                def _(sp):
                    sp.dma_start(wup[:, 0, :], io["rwkv_w_up_2"][0]).then_inc(up_loaded, 16)
                    sp.dma_start(wup[:, 1, :], io["rwkv_a_up_2"][0]).then_inc(up_loaded, 16)
                    sp.dma_start(brow[:, 0, :], everywhere(io["rwkv_w0_2"], HALF)).then_inc(r_loaded, 16)
                    sp.wait_ge(r_loaded, 16)
                    sp.dma_start(brow2, everywhere(io["rwkv_a0_2"], HALF)).then_inc(r_loaded, 16)
                    sp.wait_ge(r_loaded, 32)
                    for i, name in enumerate(("rwkv_k_k_2", "rwkv_k_a_2", "rwkv_r_k_2")):
                        if i:
                            sp.wait_ge(r_used, i)
                        sp.dma_start(krow, everywhere(flat(io[name]), HALF)).then_inc(r_loaded, 16)
                        sp.wait_ge(r_loaded, 16 * (i + 3))

                @block.tensor
                def _(pe):
                    pe.wait_ge(th_ready, 1)
                    for i in range(2):
                        bank = m.to_dve.take(pe)
                        for tt in range(TT):
                            c = 3 * HALF + i * LORA
                            mm = pe.transpose(bank[0:LORA, tt * P:(tt + 1) * P], pr[:, tt, c:c + LORA], st.ident[:, :])
                        m.to_dve.put(mm)
                    pe.wait_ge(l_ready, 1)
                    pe.wait_ge(up_loaded, 32)
                    for i in range(2):
                        for tt in range(TT):
                            for c in range(2):
                                bank = m.to_dve.take(pe)
                                m.to_dve.put(pe.matmul(bank[:, :], lT[:, i, tt * P:(tt + 1) * P],
                                                       wup[:, i, c * CHUNK:(c + 1) * CHUNK], start=True, stop=True))
                    pe.wait_ge(lw_ready, 1)
                    for tt in range(TT):
                        for c in range(2):
                            bank = m.to_dve.take(pe)
                            m.to_dve.put(pe.matmul(bank[:, :], mask2[:, 1, :], lw[:, tt, c * CHUNK:(c + 1) * CHUNK],
                                                   start=True, stop=True))
                    bank = m.to_act.take(pe)
                    for q in range(PAIRS):
                        for tt in range(TT):
                            c = (q * TT + tt) * 2
                            mm = pe.matmul(bank[:, c:c + 2], lw[:, tt, q * P:(q + 1) * P], chunk_ind[:, :], start=True, stop=True)
                    m.to_act.put(mm)

                @block.scalar
                def _(act):
                    act.activation(pr[:, :, 3 * HALF:3 * HALF + LORA], pr[:, :, 3 * HALF:3 * HALF + LORA], ACT.Tanh).then_inc(th_ready, 1)
                    act.wait_ge(wp_ready, 1)
                    act.activation(lw, lw, ACT.Sigmoid).then_inc(sg_ready, 1)
                    act.wait_ge(wp_ready, 2)
                    act.activation(aa, aa, ACT.Sigmoid).then_inc(sg_ready, 1)
                    bank = m.to_act.get(act)
                    m.to_act.free(act.activation(pc[:, :, :], bank[:, 0:4 * PAIRS], ACT.Exp))
                    act.wait_ge(sqd, 1)
                    act.activation(sq, kk, ACT.Square).then_inc(ssr, 1)
                    act.wait_ge(cum_ready, 1)
                    act.activation(ea, cum, ACT.Exp)
                    act.activation(eb, cum, ACT.Exp, scale=-1.0).then_inc(exps_ready, 1)
                    act.wait_ge(sqd, 2)
                    act.activation(small[:, :, :], small[:, :, :], ACT.Sqrt).then_inc(rtr, 1)
                    act.wait_ge(ea_used, 1)
                    act.activation(ea, cum, ACT.Exp).then_inc(exps_ready, 1)
                    act.activation(pr[:, :, NR:NR + HALF], pr[:, :, NR:NR + HALF], ACT.Silu)

                @block.vector
                def _(dve):
                    V = m.dve_chain.on(dve)
                    for i in range(2):
                        bank = m.to_dve.get(dve)
                        m.to_dve.free(dve.tensor_copy(lT[:, i, :], bank[0:LORA, 0:T]))
                    dve.drain().then_inc(l_ready, 1)
                    dve.wait_ge(r_loaded, 32)
                    for i, (dst, row) in enumerate(((lw, brow[:, 0, :]), (aa, brow2))):
                        for tt in range(TT):
                            for c in range(2):
                                bank = m.to_dve.get(dve)
                                m.to_dve.free(dve.tensor_tensor(dst[:, tt, c * CHUNK:(c + 1) * CHUNK], bank[:, :],
                                                                row[:, c * CHUNK:(c + 1) * CHUNK], ALU.add))
                        dve.drain().then_inc(wp_ready, 1)
                    dve.wait_ge(sg_ready, 1)
                    V(dve.tensor_scalar(lw, lw, -float(np.exp(np.float32(-0.5))), None, ALU.mult))
                    dve.drain().then_inc(lw_ready, 1)
                    dve.wait_ge(r_loaded, 48)
                    for tt in range(TT):
                        V(dve.tensor_tensor(kk[:, tt, :], part(1, tt), krow, ALU.mult))
                    dve.drain().then_inc(sqd, 1)
                    dve.drain().then_inc(r_used, 1)
                    for tt in range(TT):
                        for c in range(2):
                            bank = m.to_dve.get(dve)
                            m.to_dve.free(dve.tensor_copy(cum[:, tt, c * CHUNK:(c + 1) * CHUNK], bank[:, :]))
                    dve.drain().then_inc(cum_ready, 1)
                    dve.wait_ge(ssr, 1)
                    V(dve.tensor_reduce(small[:, :, :], sq.rearrange("p t (h d) -> p (t h) d", d=RN), AX_X, ALU.add))
                    V(dve.tensor_scalar(small[:, :, :], small[:, :, :], EPS, None, ALU.add))
                    dve.drain().then_inc(sqd, 1)
                    dve.wait_ge(rtr, 1)
                    V(dve.reciprocal(small[:, :, :], small[:, :, :]))
                    for tt in range(TT):
                        V(dve.tensor_tensor(heads(kk[:, tt, :]), heads(kk[:, tt, :]), spread(small[:, tt, :], RN), ALU.mult))
                    dve.wait_ge(sg_ready, 2)
                    dve.wait_ge(r_loaded, 64)
                    for tt in range(TT):
                        V(dve.scalar_tensor_tensor(out=sq[:, tt, :], in0=aa[:, tt, :], scalar=1.0, in1=krow,
                                                   op0=ALU.subtract, op1=ALU.mult))
                        V(dve.scalar_tensor_tensor(out=part(1, tt), in0=sq[:, tt, :], scalar=1.0, in1=part(1, tt),
                                                   op0=ALU.add, op1=ALU.mult))
                    dve.drain().then_inc(r_used, 1)
                    dve.wait_ge(r_loaded, 80)
                    for tt in range(TT):
                        V(dve.tensor_tensor(sq[:, tt, :], part(0, tt), part(1, tt), ALU.mult))
                        V(dve.tensor_tensor(sq[:, tt, :], sq[:, tt, :], krow, ALU.mult))
                    V(dve.tensor_reduce(bonus[:, :, :], sq.rearrange("p t (h d) -> p (t h) d", d=RN), AX_X, ALU.add))
                    dve.wait_ge(exps_ready, 1)
                    for tt in range(TT):
                        V(dve.tensor_tensor(part(0, tt), part(0, tt), ea[:, tt, :], ALU.mult))
                        V(dve.tensor_tensor(part(1, tt), part(1, tt), eb[:, tt, :], ALU.mult))
                        V(dve.tensor_tensor(B[:, tt, :], kk[:, tt, :], aa[:, tt, :], ALU.mult))
                        V(dve.tensor_tensor(B[:, tt, :], B[:, tt, :], eb[:, tt, :], ALU.mult))
                    V(dve.tensor_tensor(cum, cum, lw, ALU.subtract))
                    dve.drain().then_inc(ea_used, 1)
                    dve.wait_ge(exps_ready, 2)
                    for tt in range(TT):
                        V(dve.tensor_tensor(Kt[:, tt, :], kk[:, tt, :], ea[:, tt, :], ALU.mult))
        y = m.sb(ctx, "rwkv_y", [P, TT, HALF])
        S = m.sb(ctx, "rwkv_state", [P, PAIRS, 2, RN])
        flat0 = m.weights.buf[0][:, :, :].rearrange("p k n -> p (k n)")
        KR = flat0[:, 0:4096].rearrange("p (q f t) -> p q f t", q=PAIRS, f=2)
        BT = flat0[:, 4096:6144].rearrange("p (q t) -> p q t", t=T)
        DT = flat0[:, 6144:8192].rearrange("p (q t) -> p q t", t=T)
        flat1 = m.weights.buf[1][:, :, :].rearrange("p k n -> p (k n)")
        ABm = flat1[:, 0:2048].rearrange("p (u f t) -> p u f t", u=UNITS, f=2)
        ADm = flat1[:, 2048:4096].rearrange("p (u f t) -> p u f t", u=UNITS, f=2)
        Tm, TT_, X, M = (flat1[:, 4096 + i * 1024:4096 + (i + 1) * 1024].rearrange("p (u t) -> p u t", t=P) for i in range(4))
        AT = ABm[:, :, 0, :]
        with ExitStack() as c2:
            xu = m.sb(c2, "rwkv_xu", [P, 2, UNITS * RN])
            inv = Inverse(m, st, "rwkv", 6, AT, Tm, TT_, X, M)
            turned, masked, x_ready, u_ready, s_ready, y_ready = (m.sem("rwkv_" + s) for s in ("turned", "masked", "xk_ready", "u_ready", "s_ready", "y_ready"))
            tready = m.sem("rwkv_tt_ready")
            groups = [(hg, tt) for hg in range(2) for tt in range(TT)]
            with nc.Block() as block:
                @block.gpsimd
                def _(pool):
                    for n in range(len(groups)):
                        inv.n = n
                        inv.on_pool(pool)

                @block.scalar
                def _(act):
                    for n in range(len(groups)):
                        inv.n = n
                        inv.on_act(act)

                @block.tensor
                def _(pe):
                    for src in (lambda k, tt: Kt[:, tt, k * P:(k + 1) * P], lambda k, tt: part(0, tt)[:, k * P:(k + 1) * P],
                                lambda k, tt: B[:, tt, k * P:(k + 1) * P], lambda k, tt: part(1, tt)[:, k * P:(k + 1) * P]):
                        turn_to_columns(pe, m.to_dve, st.ident[:, :], src, PAIRS)
                    pe.wait_ge(turned, 1)
                    for n, (hg, tt) in enumerate(groups):
                        inv.n = n
                        tok = slice(tt * P, (tt + 1) * P)
                        hs = [(u, hg * UNITS + u) for u in range(UNITS)]

                        def rng(h):
                            return slice((h % 2) * RN, (h % 2 + 1) * RN)

                        for left in (BT, DT):
                            for j in range(UNITS // 2):
                                bank = m.to_dve.take(pe)
                                u0 = (j // 2) * 4 + j % 2
                                for i, (u, h) in enumerate((hs[u0], hs[u0 + 2])):
                                    mm = pe.matmul(bank[:, i * 2 * P:(i + 1) * 2 * P].rearrange("p (f t) -> p f t", f=2),
                                                   left[rng(h), h // 2, tok], KR[rng(h), h // 2, :, tok], start=True, stop=True)
                                m.to_dve.put(mm)
                        inv.on_pe(pe)
                        pe.wait_ge(tready, n + 1)
                        for c in range(2):
                            step = 2 * n + c
                            ps = slice(c * RC, (c + 1) * RC)
                            ct = slice(tt * P + c * RC, tt * P + (c + 1) * RC)
                            first = tt == 0 and c == 0
                            if not first:
                                pe.wait_ge(s_ready, step - hg)
                            bank = m.to_dve.take(pe)
                            for u, h in hs:
                                o = bank[ps, u * RN:(u + 1) * RN]
                                if not first:
                                    pe.matmul(o, KR[:, h // 2, 0, ct], S[:, h // 2, h % 2, :], start=True, stop=False)
                                mm = pe.matmul(o, ADm[:, u, 0, ps], part(2, tt)[:, h * RN:(h + 1) * RN], start=first, stop=True)
                            m.to_dve.put(mm)
                            pe.wait_ge(x_ready, step + 1)
                            bank = m.to_dve.take(pe)
                            for u, h in hs:
                                mm = pe.matmul(bank[ps, u * RN:(u + 1) * RN], TT_[:, u, ps], xu[:, 0, u * RN:(u + 1) * RN],
                                               start=True, stop=True)
                            m.to_dve.put(mm)
                            pe.wait_ge(u_ready, step + 1)
                            bank = m.to_dve.take(pe)
                            for u, h in hs:
                                o = bank[ps, u * RN:(u + 1) * RN]
                                if not first:
                                    pe.matmul(o, KR[:, h // 2, 1, ct], S[:, h // 2, h % 2, :], start=True, stop=False)
                                pe.matmul(o, ABm[:, u, 1, ps], xu[:, 1, u * RN:(u + 1) * RN], start=first, stop=False)
                                mm = pe.matmul(o, ADm[:, u, 1, ps], part(2, tt)[:, h * RN:(h + 1) * RN], start=False, stop=True)
                            m.to_dve.put(mm)
                            if tt == TT - 1 and c == 1:
                                continue
                            bank = m.to_dve.take(pe)
                            for u, h in hs:
                                o = bank[rng(h), (u // 2) * RN:(u // 2 + 1) * RN]
                                hc = slice(h * RN, (h + 1) * RN)
                                pe.matmul(o, B[ps, tt, hc], xu[ps, 1, u * RN:(u + 1) * RN], start=True, stop=False)
                                mm = pe.matmul(o, part(1, tt)[ps, hc], part(2, tt)[ps, hc], start=False, stop=True)
                            m.to_dve.put(mm)

                @block.vector
                def _(dve):
                    V = m.dve_chain.on(dve)
                    V(dve.memset(S[:, :, :, :], 0.0))
                    V(dve.memset(xu[:, :, :], 0.0))
                    for dst in (KR[:, :, 0, :], KR[:, :, 1, :], BT, DT):
                        for j in range(PAIRS // 2):
                            bank = m.to_dve.get(dve)
                            m.to_dve.free(dve.tensor_copy(dst[:, 2 * j:2 * j + 2, :], view(bank[:, 0:1], [[T, 2], [1, T]])))
                    dve.drain().then_inc(turned, 1)
                    for n, (hg, tt) in enumerate(groups):
                        inv.n = n
                        for dst in (ABm, ADm):
                            for j in range(UNITS // 2):
                                bank = m.to_dve.get(dve)
                                u0 = (j // 2) * 4 + j % 2
                                m.to_dve.free(dve.tensor_tensor(view(dst[:, u0, 0, 0:1], [[4 * P, 2], [1, 2 * P]]),
                                                                view(bank[:, 0:1], [[2 * P, 2], [1, 2 * P]]),
                                                                view(mask2[:, 0, 0:1], [[0, 2], [1, 2 * P]]), ALU.mult))
                        V(dve.engine_nop())
                        inv.on_dve(dve, V)
                        dve.drain().then_inc(tready, 1)
                        for c in range(2):
                            step = 2 * n + c
                            ps = slice(c * RC, (c + 1) * RC)
                            bank = m.to_dve.get(dve)
                            m.to_dve.free(dve.tensor_scalar(xu[ps, 0, :], bank[ps, :], -1.0, None, ALU.mult))
                            dve.drain().then_inc(x_ready, 1)
                            bank = m.to_dve.get(dve)
                            m.to_dve.free(dve.tensor_copy(xu[ps, 1, :], bank[ps, :]))
                            dve.drain().then_inc(u_ready, 1)
                            bank = m.to_dve.get(dve)
                            m.to_dve.free(dve.tensor_copy(y[ps, tt, hg * CHUNK:(hg + 1) * CHUNK], bank[ps, :]))
                            if tt == TT - 1 and c == 1:
                                continue
                            bank = m.to_dve.get(dve)
                            later = tt > 0 or c > 0
                            for e in range(2):
                                er = slice(e * RN, (e + 1) * RN)
                                Se = S[er, hg * 4:hg * 4 + 4, e, :]
                                src = view(bank[er, 0:1], [[RN, 4], [1, RN]])
                                last = dve.tensor_tensor(Se, src, Se, ALU.add) if later else dve.tensor_copy(Se, src)
                            m.to_dve.free(last)
                            V(dve.engine_nop())
                            for e in range(2):
                                er = slice(e * RN, (e + 1) * RN)
                                Se = S[er, hg * 4:hg * 4 + 4, e, :]
                                V(dve.tensor_tensor(Se, Se, spread(pc[er, hg * 4:hg * 4 + 4, 2 * tt + c], RN), ALU.mult))
                            dve.drain().then_inc(s_ready, 1)
        yy, lnw, lnb = arrays_of(m.weights.buf[0], 1, [TT, HALF]) + arrays_of(m.weights.buf[1], 2, [HALF])
        ln_loaded, cent, sqr, msr, rootr, out_ready = (m.sem("rwkv_" + s) for s in ("ln_loaded", "centred", "y_squared", "var_ready", "var_root", "out_ready"))
        with nc.Block() as block:
            @block.sync
            def _(sp):
                sp.dma_start(lnw, everywhere(io["rwkv_lnx_w_2"], HALF)).then_inc(ln_loaded, 16)
                sp.dma_start(lnb, everywhere(io["rwkv_lnx_b_2"], HALF)).then_inc(ln_loaded, 16)

            @block.scalar
            def _(act):
                act.wait_ge(cent, 1)
                act.activation(yy, y[:, :, :], ACT.Square).then_inc(sqr, 1)
                act.wait_ge(msr, 1)
                act.activation(small2[:, :, :], small2[:, :, :], ACT.Sqrt).then_inc(rootr, 1)

            @block.vector
            def _(dve):
                V = m.dve_chain.on(dve)
                V(dve.tensor_reduce(small[:, :, :], y[:, :, :].rearrange("p t (h d) -> p (t h) d", d=RN), AX_X, ALU.add))
                V(dve.tensor_scalar(small[:, :, :], small[:, :, :], 1.0 / RN, None, ALU.mult))
                for tt in range(TT):
                    V(dve.tensor_tensor(heads(y[:, tt, :]), heads(y[:, tt, :]), spread(small[:, tt, :], RN), ALU.subtract))
                dve.drain().then_inc(cent, 1)
                dve.wait_ge(sqr, 1)
                V(dve.tensor_reduce(small2[:, :, :], yy.rearrange("p t (h d) -> p (t h) d", d=RN), AX_X, ALU.add))
                dve.tensor_scalar(small2[:, :, :], small2[:, :, :], 1.0 / RN, LN_EPS, ALU.mult, ALU.add).then_inc(msr, 1)
                dve.wait_ge(rootr, 1)
                V(dve.reciprocal(small2[:, :, :], small2[:, :, :]))
                dve.wait_ge(ln_loaded, 32)
                for tt in range(TT):
                    o = y[:, tt, :]
                    V(dve.tensor_tensor(heads(o), heads(o), spread(small2[:, tt, :], RN), ALU.mult))
                    V(dve.tensor_tensor(o, o, lnw, ALU.mult))
                    V(dve.tensor_tensor(o, o, lnb, ALU.add))
                    V(dve.tensor_tensor(heads(part(2, tt)), heads(part(2, tt)), spread(bonus[:, tt, :], RN), ALU.mult))
                    V(dve.tensor_tensor(o, o, part(2, tt), ALU.add))
                    V(dve.tensor_tensor(o, o, pr[:, tt, NR:NR + HALF], ALU.mult))
                dve.drain().then_inc(out_ready, 1)
                for j in range(PAIRS // 2):
                    bank = m.to_dve.get(dve)
                    m.to_dve.free(dve.tensor_copy(cols[:, 2 * j:2 * j + 2, :], view(bank[:, 0:1], [[T, 2], [1, T]])))

            @block.tensor
            def _(pe):
                pe.wait_ge(out_ready, 1)
                turn_to_columns(pe, m.to_dve, st.ident[:, :], lambda k, tt: y[:, tt, k * P:(k + 1) * P], PAIRS)



S5_TILES, S5_BLOCK = 32, 16
S5_BLOCKS = T // S5_BLOCK
S5_AT_DVE = 20
S5_CARRY_TILES = 2
TWO_PI_PARTS = (6.28125, 0.0019353071693331003, 1.0253131677018246e-11)
ROUND = 1.5 * 2 ** 23


def s5_complex(eng, C, out, x, y, tmp):
    eng.tensor_tensor(out[0], x[0], y[0], ALU.mult)
    eng.tensor_tensor(out[1], x[0], y[1], ALU.mult)
    eng.tensor_tensor(tmp[0], x[1], y[1], ALU.mult)
    C(eng.tensor_tensor(tmp[1], x[1], y[0], ALU.mult))
    eng.tensor_tensor(out[0], out[0], tmp[0], ALU.subtract)
    C(eng.tensor_tensor(out[1], out[1], tmp[1], ALU.add))


def s5_accumulate(eng, C, out, x, y, tmp):
    eng.tensor_tensor(tmp[0], x[0], y[0], ALU.mult)
    eng.tensor_tensor(tmp[1], x[0], y[1], ALU.mult)
    eng.tensor_tensor(tmp[2], x[1], y[1], ALU.mult)
    C(eng.tensor_tensor(tmp[3], x[1], y[0], ALU.mult))
    eng.tensor_tensor(out[0], out[0], tmp[0], ALU.add)
    C(eng.tensor_tensor(out[1], out[1], tmp[1], ALU.add))
    eng.tensor_tensor(out[0], out[0], tmp[2], ALU.subtract)
    C(eng.tensor_tensor(out[1], out[1], tmp[3], ALU.add))


def s5_scan(eng, C, i0, i1, S, a, pw, carry, tmp):
    n = i1 - i0

    def temps(dims):
        names = "abc"[:len(dims)]
        size = int(np.prod(dims))
        spec = {c: s for c, s in zip(names[1:], dims[1:])}
        return [t[:, 0:size].rearrange(f"p ({' '.join(names)}) -> p {' '.join(names)}", **spec) for t in tmp]

    for f in range(2):
        C(eng.tensor_copy(pw[f][:, i0:i1, 0:1], a[f][:, i0:i1].rearrange("p (i o) -> p i o", o=1)))
    m = 1
    while m < S5_BLOCK:
        s5_complex(eng, C, [w[:, i0:i1, m:2 * m] for w in pw], [w[:, i0:i1, 0:m] for w in pw],
                   [spread(w[:, i0:i1, m - 1], m) for w in pw], temps([n, m]))
        m *= 2
    cut = [s[:, i0:i1, :].rearrange("p i (b j) -> p i b j", j=S5_BLOCK) for s in S]
    for j in range(1, S5_BLOCK):
        s5_accumulate(eng, C, [s[:, :, :, j] for s in cut], [spread(x[:, i0:i1], S5_BLOCKS) for x in a],
                      [s[:, :, :, j - 1] for s in cut], temps([n, S5_BLOCKS]))
    for f in range(2):
        C(eng.tensor_copy(carry[f][:, i0:i1, 1:], cut[f][:, :, 0:S5_BLOCKS - 1, S5_BLOCK - 1]))
    for b in range(2, S5_BLOCKS):
        s5_accumulate(eng, C, [x[:, i0:i1, b] for x in carry], [w[:, i0:i1, S5_BLOCK - 1] for w in pw],
                      [x[:, i0:i1, b - 1] for x in carry], temps([n]))
    for i in range(i0, i1, S5_CARRY_TILES):
        q = S5_CARRY_TILES
        powers = [bass.AP(tensor=w.tensor, offset=w[:, i:i + q, :].offset,
                          ap=[list(w.ap[0]), [S5_BLOCK, q], [0, S5_BLOCKS - 1], [1, S5_BLOCK]]) for w in pw]
        s5_accumulate(eng, C, [s[:, i:i + q, S5_BLOCK:].rearrange("p i (b j) -> p i b j", j=S5_BLOCK) for s in S],
                      powers, [spread(x[:, i:i + q, 1:], S5_BLOCK) for x in carry], temps([q, S5_BLOCKS - 1, S5_BLOCK]))
        yield i


def stage_s5(nc, m, io, st, cols):
    with ExitStack() as ctx:
        pr = m.sb(ctx, "s5_rows", [P, TT, 2 * HALF])
        project(nc, m, st, st.acts, KD, io["w_in_2"][0], SU0, 2 * HALF, lambda tt, c, n: pr[:, tt, c:c + n])
        uT = m.sb(ctx, "s5_u_columns", [P, 8, T])
        BT = m.sb(ctx, "s5_B_T", [P, 8, 2, P])
        CT = m.sb(ctx, "s5_C_T", [P, 8, 2, P])
        consts = m.sb(ctx, "s5_coefs", [P, 4, S5_TILES])
        par = m.sb(ctx, "s5_parity", [P, 2])
        with ExitStack() as c1:
            R = S5_TILES
            rr = m.sb(c1, "s5_row_work", [R, 14, P])
            are, aim, mag, th, n_, rd, sn, sh, den, w0, abr, abi, cr, ci = (rr[:, q, :] for q in range(14))
            ldt = m.sb(c1, "s5_log_dt", [R, 2])
            par8 = m.sb(c1, "s5_parity8", [P, 8])
            dbs = arrays_of(m.weights.buf[0], 2, [R, 2, 16])
            bl = arrays_of(m.weights.buf[0], 8, [R, 16])[4:]
            crows = arrays_of(m.weights.buf[1], 2, [8, 2, 64])
            cl = arrays_of(m.weights.buf[1], 6, [8, 64])[4:]
            loaded, dt_ready, th_ready, trig, rows_ready = (m.sem("s5_" + s) for s in ("loaded", "dt_ready", "theta_ready", "trig_ready", "coefs_ready"))
            c_ready, b_ready = m.sem("s5_c_ready"), m.sem("s5_b_ready")
            with nc.Block() as block:
                @block.sync
                def _(sp):
                    sp.dma_start(are, io["s5_a_re_2"][0].rearrange("(i g) p -> i (g p)", g=2)).then_inc(loaded, 16)
                    sp.dma_start(aim, io["s5_a_im_2"][0].rearrange("(i g) p -> i (g p)", g=2)).then_inc(loaded, 16)
                    sp.dma_start(ldt[:, :], io["s5_log_dt_2"][0].rearrange("(i g) -> i g", g=2)).then_inc(loaded, 16)
                    for f, nm in enumerate(("re", "im")):
                        sp.dma_start(cl[f], io[f"s5_c_{nm}_2"][0].rearrange("(k g) c p -> (g c) k p", g=8)).then_inc(loaded, 16)
                        sp.dma_start(bl[f], io[f"s5_b_{nm}_2"][0].rearrange("(i g) p c -> (g p) i c", g=2)).then_inc(loaded, 16)

                @block.scalar
                def _(act):
                    A = m.act_chain.on(act)
                    act.activation(pr[:, :, HALF:2 * HALF], pr[:, :, HALF:2 * HALF], ACT.Silu)
                    act.wait_ge(loaded, 112)
                    A(act.activation(ldt[:, :], ldt[:, :], ACT.Exp))
                    act.drain().then_inc(dt_ready, 1)
                    act.wait_ge(th_ready, 1)
                    act.activation(mag, mag, ACT.Exp)
                    act.activation(sn, rd, ACT.Sin)
                    act.activation(sh, rd, ACT.Sin, scale=0.5)
                    act.drain().then_inc(trig, 1)

                @block.vector
                def _(dve):
                    V = m.dve_chain.on(dve)
                    V(dve.tensor_reduce(par8[:, :], st.ident[:, :].rearrange("p (b c) -> p b c", c=16), AX_X, ALU.add))
                    V(dve.tensor_reduce(par[:, :], view(par8[:, 0:1], [[1, 2], [2, 4]]), AX_X, ALU.add))
                    V(dve.memset(dbs[0], 0.0))
                    V(dve.memset(dbs[1], 0.0))
                    for j in range(4):
                        bank = m.to_dve.get(dve)
                        m.to_dve.free(dve.tensor_copy(uT[:, 2 * j:2 * j + 2, :], view(bank[:, 0:1], [[T, 2], [1, T]])))
                    dve.wait_ge(dt_ready, 1)
                    dve.tensor_tensor(mag.rearrange("i (g p) -> i g p", g=2), are.rearrange("i (g p) -> i g p", g=2),
                                      spread(ldt[:, :], 64), ALU.mult)
                    V(dve.tensor_tensor(th.rearrange("i (g p) -> i g p", g=2), aim.rearrange("i (g p) -> i g p", g=2),
                                        spread(ldt[:, :], 64), ALU.mult))
                    V(dve.tensor_scalar(n_, th, 1.0 / (2 * np.pi), None, ALU.mult))
                    V(dve.tensor_scalar(n_, n_, ROUND, None, ALU.add))
                    V(dve.tensor_scalar(n_, n_, ROUND, None, ALU.subtract))
                    V(dve.scalar_tensor_tensor(out=rd, in0=n_, scalar=-TWO_PI_PARTS[0], in1=th, op0=ALU.mult, op1=ALU.add))
                    for part in TWO_PI_PARTS[1:]:
                        V(dve.scalar_tensor_tensor(out=rd, in0=n_, scalar=-part, in1=rd, op0=ALU.mult, op1=ALU.add))
                    V(dve.tensor_scalar(rd, rd, 3.1415925, -3.1415925, ALU.min, ALU.max))
                    dve.drain().then_inc(th_ready, 1)
                    for f in range(2):
                        for g in range(2):
                            V(dve.tensor_scalar(crows[f][:, :, g, :], cl[f], par[:, g:g + 1], -1.0 if f else 1.0, ALU.mult, ALU.mult))
                    dve.drain().then_inc(c_ready, 1)
                    for j in range(4):
                        bank = m.to_dve.get(dve)
                        m.to_dve.free(dve.tensor_copy(CT[:, 2 * j:2 * j + 2, :, :].rearrange("p k f s -> p (k f s)"), bank[:, :]))
                    dve.wait_ge(trig, 1)
                    V(dve.tensor_tensor(abr, sh, sh, ALU.mult))
                    V(dve.tensor_scalar(abr, abr, -2.0, 1.0, ALU.mult, ALU.add))
                    V(dve.tensor_tensor(abr, abr, mag, ALU.mult))
                    V(dve.tensor_tensor(abi, sn, mag, ALU.mult))
                    V(dve.tensor_tensor(den, are, are, ALU.mult))
                    V(dve.tensor_tensor(w0, aim, aim, ALU.mult))
                    V(dve.tensor_tensor(den, den, w0, ALU.add))
                    V(dve.reciprocal(den, den))
                    V(dve.tensor_scalar(n_, abr, 1.0, None, ALU.subtract))
                    V(dve.tensor_tensor(cr, n_, are, ALU.mult))
                    V(dve.tensor_tensor(w0, abi, aim, ALU.mult))
                    V(dve.tensor_tensor(cr, cr, w0, ALU.add))
                    V(dve.tensor_tensor(cr, cr, den, ALU.mult))
                    V(dve.tensor_tensor(ci, abi, are, ALU.mult))
                    V(dve.tensor_tensor(w0, n_, aim, ALU.mult))
                    V(dve.tensor_tensor(ci, ci, w0, ALU.subtract))
                    V(dve.tensor_tensor(ci, ci, den, ALU.mult))
                    dve.drain().then_inc(rows_ready, 1)
                    bank = m.to_dve.get(dve)
                    m.to_dve.free(dve.tensor_copy(consts[:, :, :].rearrange("p f i -> p (f i)"), bank[:, 0:4 * R]))
                    V(dve.engine_nop())
                    tmp = bl[2]
                    for g in range(2):
                        hp = slice(g * 64, (g + 1) * 64)
                        cre, cim = (spread(consts[hp, f, :], 16) for f in (2, 3))
                        for f, (x, y, op) in enumerate(((0, 1, ALU.subtract), (1, 0, ALU.add))):
                            o = dbs[f][hp, :, g, :]
                            V(dve.tensor_tensor(o, cre, bl[x][hp], ALU.mult))
                            V(dve.tensor_tensor(tmp[hp], cim, bl[y][hp], ALU.mult))
                            V(dve.tensor_tensor(o, o, tmp[hp], op))
                    dve.drain().then_inc(b_ready, 1)
                    for j in range(4):
                        bank = m.to_dve.get(dve)
                        m.to_dve.free(dve.tensor_copy(BT[:, 2 * j:2 * j + 2, :, :].rearrange("p k f s -> p (k f s)"), bank[:, :]))

                @block.tensor
                def _(pe):
                    turn_to_columns(pe, m.to_dve, st.ident[:, :], lambda k, tt: pr[:, tt, k * P:(k + 1) * P], 8)

                    def turn(src):
                        for j in range(4):
                            bank = m.to_dve.take(pe)
                            for u in range(4):
                                mm = pe.transpose(bank[:, u * P:(u + 1) * P], src(2 * j + u // 2, u % 2), st.ident[:, :])
                            m.to_dve.put(mm)

                    pe.wait_ge(c_ready, 1)
                    turn(lambda k, f: crows[f][:, k, :, :].rearrange("p g s -> p (g s)"))
                    pe.wait_ge(rows_ready, 1)
                    bank = m.to_dve.take(pe)
                    for f in range(4):
                        mm = pe.transpose(bank[:, f * R:(f + 1) * R], rr[:, 10 + f, :], st.ident[0:R, 0:R])
                    m.to_dve.put(mm)
                    pe.wait_ge(b_ready, 1)
                    turn(lambda k, f: dbs[f][:, 4 * k:4 * k + 4, :, :].rearrange("p i g c -> p (i g c)"))
        S = arrays_of(m.weights.buf[0], 1, [S5_TILES, T]) + arrays_of(m.weights.buf[1], 1, [S5_TILES, T])
        with ExitStack() as c2:
            pw = [m.sb(c2, f"s5_powers{f}", [P, S5_TILES, S5_BLOCK])[:, :, :] for f in range(2)]
            carry = [m.sb(c2, f"s5_carry{f}", [P, S5_TILES, S5_BLOCKS])[:, :, :] for f in range(2)]
            size = S5_CARRY_TILES * (S5_BLOCKS - 1) * S5_BLOCK
            tmp_dve = [m.sb(c2, f"s5_tmp_dve{q}", [P, size])[:, :] for q in range(4)]
            tmp_pool = [m.sb(c2, f"s5_tmp_pool{q}", [P, size])[:, :] for q in range(4)]
            a = [consts[:, f, :] for f in range(2)]
            bu_ready, bu_act, s_dve, s_pool, y_ready = (m.sem("s5_" + s) for s in ("bu_by_dve", "bu_by_act", "states_dve", "states_pool", "y_ready"))
            with nc.Block() as block:
                @block.tensor
                def _(pe):
                    for i in range(S5_TILES):
                        ring = m.to_act if i % 2 else m.to_dve
                        bank = ring.take(pe)
                        q = slice((i % 4) * 32, (i % 4 + 1) * 32)
                        for f in range(2):
                            mm = pe.matmul(bank[:, f * T:(f + 1) * T], BT[q, i // 4, f, :], uT[q, i // 4, :], start=True, stop=True)
                        ring.put(mm)
                    for j in range(4):
                        bank = m.to_dve.take(pe)
                        for i in range(8 * j, 8 * j + 8):
                            if i < S5_AT_DVE:
                                pe.wait_ge(s_dve, i // S5_CARRY_TILES + 1)
                            else:
                                pe.wait_ge(s_pool, (i - S5_AT_DVE) // S5_CARRY_TILES + 1)
                            o = bank[(i % 4) * 32:(i % 4 + 1) * 32, (i // 4 % 2) * T:(i // 4 % 2 + 1) * T]
                            for f in range(2):
                                mm = pe.matmul(o, CT[:, i // 4, f, (i % 4) * 32:(i % 4 + 1) * 32], S[f][:, i, :],
                                               start=(f == 0), stop=(f == 1))
                        m.to_dve.put(mm)

                @block.scalar
                def _(act):
                    for i in range(1, S5_TILES, 2):
                        bank = m.to_act.get(act)
                        act.activation(S[0][:, i, :], bank[:, 0:T], ACT.Copy)
                        m.to_act.free(act.activation(S[1][:, i, :], bank[:, T:2 * T], ACT.Copy))
                    act.drain().then_inc(bu_act, 1)
                    act.wait_ge(y_ready, 1)
                    act.activation(cols, cols, ACT.Gelu_apprx_tanh)

                @block.gpsimd
                def _(pool):
                    L = m.pool_chain.on(pool)
                    pool.wait_ge(bu_act, 1)
                    pool.wait_ge(bu_ready, 1)
                    for _i in s5_scan(pool, L, S5_AT_DVE, S5_TILES, S, a, pw, carry, tmp_pool):
                        pool.drain().then_inc(s_pool, 1)

                @block.vector
                def _(dve):
                    V = m.dve_chain.on(dve)
                    for i in range(0, S5_TILES, 2):
                        bank = m.to_dve.get(dve)
                        dve.tensor_copy(S[0][:, i, :], bank[:, 0:T])
                        m.to_dve.free(dve.tensor_copy(S[1][:, i, :], bank[:, T:2 * T]))
                    dve.drain().then_inc(bu_ready, 1)
                    V(dve.engine_nop())
                    dve.wait_ge(bu_act, 1)
                    for _i in s5_scan(dve, V, 0, S5_AT_DVE, S, a, pw, carry, tmp_dve):
                        dve.drain().then_inc(s_dve, 1)
                    for j in range(4):
                        bank = m.to_dve.get(dve)
                        for u in range(2):
                            k = 2 * j + u
                            ins = dve.scalar_tensor_tensor(out=cols[:, k, :], in0=uT[:, k, :], scalar=st.vec.col("s5_d_2", k),
                                                           in1=bank[:, u * T:(u + 1) * T], op0=ALU.mult, op1=ALU.add)
                        m.to_dve.free(ins)
                    dve.drain().then_inc(y_ready, 1)
        project(nc, m, st, cols, 8, io["s5_glu_w_2"][0], 0, HALF, lambda tt, c, n: pr[:, tt, c:c + n])
        with ExitStack() as c3:
            yr = m.sb(c3, "s5_y_rows", [P, TT, HALF])
            gb = m.sb(c3, "s5_glu_b_row", [P, HALF])
            gb_loaded, added, sig, outr = (m.sem("s5_" + s) for s in ("glu_b_loaded", "glu_b_added", "glu_sigmoid", "out_ready"))
            with nc.Block() as block:
                @block.sync
                def _(sp):
                    sp.dma_start(gb[:, :], everywhere(io["s5_glu_b_2"], HALF)).then_inc(gb_loaded, 16)

                @block.tensor
                def _(pe):
                    turn_to_rows(pe, m.to_dve, st.ident[:, :], lambda k, tt: cols[:, k, tt * P:(tt + 1) * P], 8)
                    pe.wait_ge(outr, 1)
                    turn_to_columns(pe, m.to_dve, st.ident[:, :], lambda k, tt: yr[:, tt, k * P:(k + 1) * P], 8)

                @block.scalar
                def _(act):
                    act.wait_ge(added, 1)
                    act.activation(pr[:, :, 0:HALF], pr[:, :, 0:HALF], ACT.Sigmoid).then_inc(sig, 1)

                @block.vector
                def _(dve):
                    V = m.dve_chain.on(dve)
                    dve.wait_ge(gb_loaded, 16)
                    for tt in range(TT):
                        V(dve.tensor_tensor(pr[:, tt, 0:HALF], pr[:, tt, 0:HALF], gb[:, :], ALU.add))
                    dve.drain().then_inc(added, 1)
                    for tt in range(TT):
                        for k in range(2):
                            bank = m.to_dve.get(dve)
                            c = k * CHUNK
                            m.to_dve.free(dve.tensor_tensor(yr[:, tt, c:c + CHUNK], bank[:, :], pr[:, tt, HALF + c:HALF + c + CHUNK], ALU.mult))
                    V(dve.engine_nop())
                    dve.wait_ge(sig, 1)
                    V(dve.tensor_tensor(yr[:, :, :], yr[:, :, :], pr[:, :, 0:HALF], ALU.mult))
                    dve.drain().then_inc(outr, 1)
                    for j in range(4):
                        bank = m.to_dve.get(dve)
                        m.to_dve.free(dve.tensor_copy(cols[:, 2 * j:2 * j + 2, :], view(bank[:, 0:1], [[T, 2], [1, T]])))



BRANCHES = 3


def stage_merge(nc, m, io, st, cols):
    with ExitStack() as ctx:
        merged = m.sb(ctx, "merged_rows", [P, TT, D])
        gb = m.sb(ctx, "gate_b_row", [P, BRANCHES * D])
        gate = [m.sb(ctx, f"gates{b}", [P, TT, CHUNK]) for b in range(2)]
        tmp = m.sb(ctx, "merge_tmp", [P, TT, CHUNK])
        gb_loaded, gate_ready, sig, done = (m.sem("merge_" + s) for s in ("gate_b_loaded", "logits_ready", "gates_ready", "rows_ready"))
        work = [(c, size, br) for c, size in chunks(D) for br in range(BRANCHES)]
        with nc.Block() as block:
            @block.sync
            def _(sp):
                for i, (c, size, br) in enumerate(work):
                    m.weights.load(sp, io["w_in_2"][0], MG0 + br * D + c, size)
                    if i == 0:
                        sp.dma_start(gb[:, :], everywhere(flat(io["gate_b_2"]), BRANCHES * D)).then_inc(gb_loaded, 16)
                    m.weights.load(sp, io["w_branch_2"][0, br], c, size)

            @block.tensor
            def _(pe):
                for c, size, br in work:
                    m.weights.multiply(pe, st.acts, KD, size, m.to_dve)
                    m.weights.multiply(pe, cols[:, 8 * br:8 * br + 8, :], HALF // P, size, m.to_dve)
                pe.wait_ge(done, 1)
                turn_to_columns(pe, m.to_dve, st.ident[:, :], lambda k, tt: merged[:, tt, k * P:(k + 1) * P], KD)

            @block.scalar
            def _(act):
                for i in range(len(work)):
                    act.wait_ge(gate_ready, i + 1)
                    g = gate[i % 2]
                    act.activation(g[:, :, :], g[:, :, :], ACT.Sigmoid).then_inc(sig, 1)

            @block.vector
            def _(dve):
                V = m.dve_chain.on(dve)
                dve.wait_ge(gb_loaded, 16)
                for i, (c, size, br) in enumerate(work):
                    g = gate[i % 2]
                    for tt in range(TT):
                        bank = m.to_dve.get(dve)
                        m.to_dve.free(dve.tensor_tensor(g[:, tt, :], bank[:, :], gb[:, br * D + c:br * D + c + size], ALU.add))
                    dve.drain().then_inc(gate_ready, 1)
                    dve.wait_ge(sig, i + 1)
                    for tt in range(TT):
                        bank = m.to_dve.get(dve)
                        o = merged[:, tt, c:c + size]
                        dst = o if br == 0 else tmp[:, tt, :]
                        m.to_dve.free(dve.tensor_tensor(dst, bank[:, :], g[:, tt, :], ALU.mult))
                        V(dve.engine_nop())
                        if br:
                            V(dve.tensor_tensor(o, o, tmp[:, tt, :], ALU.add))
                dve.drain().then_inc(done, 1)
                for j in range(KD // 2):
                    bank = m.to_dve.get(dve)
                    m.to_dve.free(dve.tensor_copy(st.acts[:, 2 * j:2 * j + 2, :], view(bank[:, 0:1], [[T, 2], [1, T]])))


def whole_program(nc, io, out):
    with ExitStack() as ctx:
        m = Machine(nc, ctx)
        st = shared_state(m)
        stage_modulation(nc, m, io, st)
        norm_to_columns(nc, m, st, "norm1", st.x, D, lambda j: st.acts[:, j, :], lambda j: st.gain1[:, j:j + 1],
                        lambda j: st.mod_cols[:, j:j + 1], x_sem=(m.sem("x_loaded"), 32))
        with ExitStack() as c1:
            proj = m.sb(c1, "projection_rows", [P, TT, N_IN])
            project(nc, m, st, st.acts, KD, io["w_in"][0], 0, N_IN, lambda tt, c, n: proj[:, tt, c:c + n])
            with ExitStack() as c2:
                attn = m.sb(c2, "mixer_rows", [P, TT, HALF])
                stage_attention(nc, m, io, st, proj, attn)
                norm_to_columns(nc, m, st, "attn_norm", attn, HALF, lambda j: st.acts[:, j, :],
                                lambda j: st.vec.col("attn_out_norm", j), None)
                stage_mamba(nc, m, io, st, proj, attn)
                norm_to_columns(nc, m, st, "ssm_norm", attn, HALF, lambda j: st.acts[:, 8 + j, :],
                                lambda j: st.vec.col("ssm_norm", j), None, groups=2)
        project_residual(nc, m, st, io["w_out"][0], st.mod_dram[2 * D:3 * D])
        norm_to_columns(nc, m, st, "norm2", st.x, D, lambda j: st.acts[:, j, :], lambda j: st.gain2[:, j:j + 1],
                        lambda j: st.mod_cols[:, 48 + j:49 + j])
        stage_experts(nc, m, io, st)
        norm_rows(nc, m, st, "block1_norm", st.x, io["norm_final"])
        m.clear_stage_semaphores()
        norm_to_columns(nc, m, st, "norm3", st.x, D, lambda j: st.acts[:, j, :], lambda j: st.vec.col("norm_w_2", j), None)
        with ExitStack() as c1:
            cols = m.sb(c1, "branch_columns", [P, BRANCHES * 8, T])
            stage_gdn(nc, m, io, st, cols[:, 0:8, :])
            stage_rwkv(nc, m, io, st, cols[:, 8:16, :])
            stage_s5(nc, m, io, st, cols[:, 16:24, :])
            stage_merge(nc, m, io, st, cols)
        project_residual(nc, m, st, io["w_out_2"][0])
        norm_rows(nc, m, st, "block2_norm", st.x, io["final_norm_w_2"], store=out)


_INS = ["x", "c", "ada_w", "ada_b", "norm_mix", "norm_ffn", "w_in", "cmp_pe", "cmp_w1", "cmp_w2", "rel_bias",
        "attn_out_norm", "conv_w", "conv_b", "dt_bias", "a_log", "d_skip", "ssm_norm", "w_out", "peer_wq",
        "peer_subkeys", "peer_u", "peer_v", "norm_final", "norm_w_2", "w_in_2", "gdn_conv_w_2", "gdn_a_log_2",
        "gdn_dt_bias_2", "gdn_norm_w_2", "rwkv_mu_2", "rwkv_w0_2", "rwkv_w_up_2", "rwkv_a0_2", "rwkv_a_up_2",
        "rwkv_k_k_2", "rwkv_k_a_2", "rwkv_r_k_2", "rwkv_lnx_w_2", "rwkv_lnx_b_2", "s5_a_re_2", "s5_a_im_2",
        "s5_log_dt_2", "s5_b_re_2", "s5_b_im_2", "s5_c_re_2", "s5_c_im_2", "s5_d_2", "s5_glu_w_2", "s5_glu_b_2",
        "gate_b_2", "w_branch_2", "w_out_2", "final_norm_w_2"]


def kernel(**inputs):
    import numpy as _np
    import concourse.bacc as _bacc
    from concourse import mybir as _mybir
    from concourse.bass_utils import run_bass_kernel_spmd as _run

    nc = _bacc.Bacc("TRN2", target_bir_lowering=False, num_devices=1)
    arrays, io = {}, {}
    for name in _INS:
        a = _np.ascontiguousarray(inputs[name])
        arrays[f"in_{name}_dram"] = a
        io[name] = nc.dram_tensor(f"in_{name}_dram", a.shape, _mybir.dt.from_np(a.dtype), kind="ExternalInput").ap()
    out = nc.dram_tensor("out_0_dram", (1, T, D), _mybir.dt.float32, kind="ExternalOutput").ap()
    whole_program(nc, io, out)
    r = _run(nc, [arrays], core_ids=[0])
    return r.results[0]["out_0_dram"]
```

```python
from contextlib import ExitStack

import numpy as np

import concourse.bass as bass
from concourse import mybir

ALU = mybir.AluOpType
ACT = mybir.ActivationFunctionType
F32 = mybir.dt.float32
F32R = mybir.dt.float32r
I32 = mybir.dt.int32
U32 = mybir.dt.uint32
AX_X = mybir.AxisListType.X

P = 128
T = 256
TT = T // P
D = 2048
KD = D // P
CHUNK = 512
HALF = 1024
EPS = 1e-6
NEG = -1e30
HEADS, KV_HEADS, GROUP, DH = 16, 2, 8, 64
N_IN = 4416
CONV_TAPS = 4
EXPERTS_SIDE = 128
PEER_HEADS, TOPK = 8, 16

Q0, KV0, GATE0, Z0, XBC0, DT0 = 0, 1024, 1792, 1840, 2864, 4400
GQKV0, GZ0, GB0, GA0, RF0, RZ0, SU0, SZ0, MG0 = 0, 3072, 4096, 4104, 4112, 7376, 8400, 9424, 10448


class Chain:

    def __init__(self, sem):
        self.sem, self.n = sem, 0

    def __call__(self, ins):
        ins.then_inc(self.sem, 1)
        self.n = self.n + 1
        self.eng.wait_ge(self.sem, self.n)

    def on(self, eng):
        self.eng = eng
        return self

    def enter(self, i, per):
        self.base, self.per = self.n, per
        self.n = self.n + i * per

    def leave(self, steps):
        self.n = self.base + steps * self.per


class BankRing:

    def __init__(self, banks, filled, emptied):
        self.banks, self.filled, self.emptied = banks, filled, emptied
        self.nf = self.ne = self.of = self.oe = 0

    def take(self, pe):
        if self.of + self.nf >= len(self.banks):
            pe.wait_ge(self.emptied, self.wf + self.nf + self.of - len(self.banks) + 1)
        return self.banks[(self.of + self.nf) % len(self.banks)]

    def take_next(self, pe):
        self.nf += 1
        bank = self.take(pe)
        self.nf -= 1
        return bank

    wf = we = 0

    def put(self, ins):
        ins.then_inc(self.filled, 1)
        self.nf += 1

    def get(self, eng):
        eng.wait_ge(self.filled, self.we + self.ne + self.oe + 1)
        return self.banks[(self.oe + self.ne) % len(self.banks)]

    def free(self, ins):
        ins.then_inc(self.emptied, 1)
        self.ne += 1

    def passed_on(self):
        self.ne += 1

    def enter_fill(self, i, per):
        self.of, self.nf, self.wf = self.of + self.nf, 0, i * per

    def leave_fill(self, steps, per):
        assert self.nf == per and per % len(self.banks) == 0 and self.of >= len(self.banks)
        self.of, self.nf, self.wf = self.of + steps * per, 0, 0

    def enter_empty(self, i, per):
        self.oe, self.ne, self.we = self.oe + self.ne, 0, i * per

    def leave_empty(self, steps, per):
        assert self.ne == per and per % len(self.banks) == 0
        self.oe, self.ne, self.we = self.oe + steps * per, 0, 0


class Machine:

    def __init__(self, nc, ctx):
        self.nc, self.ctx, self.sems, self.uses = nc, ctx, {}, {}
        banks = [ctx.enter_context(nc.psum_tensor(f"bank{i}", [P, CHUNK], F32)) for i in range(8)]
        self.to_dve = BankRing(banks[:4], self.sem("dve_banks_filled"), self.sem("dve_banks_emptied"))
        self.to_act = BankRing(banks[4:], self.sem("act_banks_filled"), self.sem("act_banks_emptied"))
        self.banks = banks
        self.dve_chain = Chain(self.sem("dve_done"))
        self.act_chain = Chain(self.sem("act_done"))
        self.pool_chain = Chain(self.sem("pool_done"))
        self.weights = WeightStream(self)
        self.shared = set(self.sems) | {"residual_gain_loaded"}

    def sem(self, name):
        if name not in self.sems:
            self.sems[name] = self.nc.alloc_semaphore(name=name)
        return self.sems[name]

    def clear_stage_semaphores(self):
        stage = [name for name in self.sems if name not in self.shared]
        self.nc.clear_and_free_semaphores([self.sems.pop(name) for name in stage])
        self.nc.all_engine_barrier()

    def sb(self, ctx, name, shape, dt=F32):
        self.uses[name] = self.uses.get(name, 0) + 1
        unique = name if self.uses[name] == 1 else f"{name}_{self.uses[name]}"
        return ctx.enter_context(self.nc.sbuf_tensor(unique, shape, dt))

    def dram(self, name, shape):
        return self.nc.dram_tensor(name, shape, F32, kind="Internal").ap()


class Split:

    def __init__(self, m, ctx, name, kt):
        self.h = m.sb(ctx, name + "_high", [P, kt, T], F32R)
        self.l = m.sb(ctx, name + "_low", [P, kt, T], F32R)


class WeightStream:

    UNIT, UNITS_HELD = 2, 3

    def __init__(self, m):
        self.m = m
        self.loaded = [m.sem(f"weights_loaded{b}") for b in range(2)]
        self.used = [m.sem(f"weights_used{b}") for b in range(2)]
        self.high_ready, self.low_ready = m.sem("weight_high_ready"), m.sem("weight_low_ready")
        self.unit_used = m.sem("weight_unit_used")
        self.n_load = self.n_use = 0
        self.chunk = {"act": 0, "dve": 0}
        self.unit = {"act": 0, "dve": 0, "pe": 0}

    def memory(self, ctx):
        self.buf = [self.m.sb(ctx, f"weights{b}", [P, KD, CHUNK]) for b in range(2)]

    def split_memory(self, ctx):
        shape = [P, self.UNITS_HELD, self.UNIT, CHUNK]
        self.high = self.m.sb(ctx, "weights_high", shape, F32R)
        self.low = self.m.sb(ctx, "weights_low", shape, F32R)

    def load(self, sp, w, c0, n):
        b, turn = self.n_load % 2, self.n_load // 2
        if turn:
            sp.wait_ge(self.used[b], turn)
        kt = w.shape[0] // P
        src = w.rearrange("(k p) n -> p k n", p=P)[:, :, c0:c0 + n]
        sp.dma_start(self.buf[b][:, 0:kt, 0:n], src).then_inc(self.loaded[b], 16)
        self.n_load += 1

    def multiply(self, pe, acts, kt, n, ring):
        b, turn = self.n_use % 2, self.n_use // 2
        pe.wait_ge(self.loaded[b], 16 * (turn + 1))
        for tt in range(TT):
            bank = ring.take(pe)
            for k in range(kt):
                mm = pe.matmul(bank[:, 0:n], acts[:, k, tt * P:(tt + 1) * P], self.buf[b][:, k, 0:n],
                               start=(k == 0), stop=(k == kt - 1))
            ring.put(mm)
        pe.drain().then_inc(self.used[b], 1)
        self.n_use += 1

    def seen(self, *engines):
        for e in engines:
            self.chunk[e] += 1

    def split_high(self, act, kt, n):
        b, turn = self.chunk["act"] % 2, self.chunk["act"] // 2
        act.wait_ge(self.loaded[b], 16 * (turn + 1))
        for k in range(0, kt, self.UNIT):
            u = self.unit["act"]
            if u >= self.UNITS_HELD:
                act.wait_ge(self.unit_used, u - self.UNITS_HELD + 1)
            act.activation(self.high[:, u % self.UNITS_HELD, :, 0:n], self.buf[b][:, k:k + self.UNIT, 0:n],
                           ACT.Copy).then_inc(self.high_ready, 1)
            self.unit["act"] += 1
        self.chunk["act"] += 1

    def split_low(self, dve, kt, n, k0=0, k1=None, between=None):
        k1 = kt if k1 is None else k1
        b = self.chunk["dve"] % 2
        for k in range(k0, k1, self.UNIT):
            u = self.unit["dve"]
            dve.wait_ge(self.high_ready, u + 1)
            dve.tensor_tensor(self.low[:, u % self.UNITS_HELD, :, 0:n], self.buf[b][:, k:k + self.UNIT, 0:n],
                              self.high[:, u % self.UNITS_HELD, :, 0:n], ALU.subtract).then_inc(self.low_ready, 1)
            self.unit["dve"] += 1
            if between:
                between(dve)
        if k1 == kt:
            dve.drain().then_inc(self.used[b], 1)
            self.chunk["dve"] += 1

    def multiply_split(self, pe, acts, kt, n, ring):
        both = [ring.take(pe), ring.take_next(pe)]
        for k0 in range(0, kt, self.UNIT):
            u = self.unit["pe"]
            slot = u % self.UNITS_HELD
            pe.wait_ge(self.low_ready, u + 1)
            last = k0 + self.UNIT == kt
            for tt in range(TT):
                tok = slice(tt * P, (tt + 1) * P)
                for i in range(self.UNIT):
                    k = k0 + i
                    o, first, end = both[tt][:, 0:n], k == 0, k == kt - 1
                    pe.matmul(o, acts.h[:, k, tok], self.high[:, slot, i, 0:n], start=first, stop=False)
                    pe.matmul(o, acts.h[:, k, tok], self.low[:, slot, i, 0:n], start=False, stop=False)
                    mm = pe.matmul(o, acts.l[:, k, tok], self.high[:, slot, i, 0:n], start=False, stop=end)
                if last:
                    ring.put(mm)
            if last:
                pe.drain().then_inc(self.unit_used, 1)
            else:
                mm.then_inc(self.unit_used, 1)
            self.unit["pe"] += 1
        self.n_use += 1


def chunks(n, size=CHUNK):
    return [(c, min(size, n - c)) for c in range(0, n, size)]


class Vectors:

    LISTS = [
        [("c", 16), ("norm_mix", 16), ("norm_ffn", 16), ("norm_w_2", 16), ("ssm_norm", 8), ("attn_out_norm", 8),
         ("conv_w", 48)],
        [("ada_b", 96), ("conv_b", 12), ("s5_d_2", 8)],
        [("gdn_conv_w_2", 96), ("cmp_pe", 32)],
    ]

    def __init__(self, m):
        self.cols = m.sb(m.ctx, "vector_columns", [P, len(self.LISTS), P])
        self.at = {}
        for g, names in enumerate(self.LISTS):
            c = 0
            for name, n in names:
                self.at[name] = (g, c, n)
                c += n

    def col(self, name, k, n=1):
        g, c, _ = self.at[name]
        return self.cols[:, g, c + k:c + k + n]


def turn_to_columns(pe, ring, ident, src, kt):
    for j in range(kt // 2):
        bank = ring.take(pe)
        for u in range(2):
            for tt in range(TT):
                mm = pe.transpose(bank[:, (u * TT + tt) * P:(u * TT + tt + 1) * P], src(2 * j + u, tt), ident)
        ring.put(mm)



def stage_modulation(nc, m, io, st):
    NM = 3 * D
    PIECE = NM // 4
    with ExitStack() as ctx:
        rows = m.sb(ctx, "vector_rows", [P, 3, P])
        ring = m.sb(ctx, "ada_ring", [P, 4, PIECE])
        acc = m.sb(ctx, "ada_acc", [P, NM])
        cond, ones = st.cond, st.ones
        xor = m.sb(ctx, "xor_bits", [P, P], I32)
        s_idx = m.sb(ctx, "s_idx", [P, P], I32)
        t_idx = m.sb(ctx, "t_idx", [P, P], I32)
        xorf = m.sb(ctx, "xor_f", [P, P])
        tmp = m.sb(ctx, "mask_tmp", [P, P])
        vec_loaded, vec_zero = m.sem("vectors_loaded"), m.sem("vector_rows_zeroed")
        piece_loaded = [m.sem(f"ada_piece_loaded{b}") for b in range(4)]
        piece_used = [m.sem(f"ada_piece_used{b}") for b in range(4)]
        iotas_ready, ident_ready = m.sem("iotas_ready"), m.sem("identity_ready")
        cond_ready, acc_ready, ones_ready = m.sem("cond_ready"), m.sem("ada_sum_ready"), m.sem("ones_ready")
        cols_ready = m.sem("vector_columns_ready")
        mod_cols_ready = m.sem("mod_columns_ready")
        ident0 = m.sem("identity_zeroed")
        n_vec = sum(len(names) for names in Vectors.LISTS)

        with nc.Block() as block:
            @block.sync
            def _(sp):
                sp.wait_ge(vec_zero, 1)
                for g, names in enumerate(Vectors.LISTS):
                    for name, n in names:
                        _, c, _ = st.vec.at[name]
                        sp.dma_start(rows[c:c + n, g, :], flat(io[name]).rearrange("(r p) -> r p", p=P))\
                          .then_inc(vec_loaded, 16)
                for t in range(TT):
                    sp.dma_start(st.x[:, t, :], io["x"][0, t * P:(t + 1) * P, :]).then_inc(m.sem("x_loaded"), 16)
                with sp.Fori(0, KD) as k:
                    for b in range(4):
                        sp.wait_ge(piece_used[b], k)
                        sp.dma_start(ring[:, b, :], io["ada_w"][0, bass.ds(k * P, P), b * PIECE:(b + 1) * PIECE])\
                          .then_inc(piece_loaded[b], 16)

            @block.gpsimd
            def _(pool):
                pool.memset(rows[:, :, :], 0.0).then_inc(vec_zero, 1)
                pool.memset(st.ident[:, :], 0.0).then_inc(ident0, 1)
                pool.wait_ge(ident0, 1)
                pool.affine_select(out=st.ident[:, :], in_=st.ident[:, :], compare_op=ALU.not_equal, fill=1.0,
                                   base=0, pattern=[[-1, P]], channel_multiplier=1).then_inc(ident_ready, 1)
                pool.iota(s_idx[:, :], pattern=[[0, P]], base=0, channel_multiplier=1)
                pool.iota(t_idx[:, :], pattern=[[1, P]], base=0, channel_multiplier=0).then_inc(iotas_ready, 1)

            @block.vector
            def _(dve):
                V = m.dve_chain.on(dve)
                dve.memset(ones[:, :], 1.0).then_inc(ones_ready, 1)
                V(dve.memset(acc[:, :], 0.0))
                dve.wait_ge(iotas_ready, 1)
                V(dve.tensor_tensor(xor[:, :], s_idx[:, :], t_idx[:, :], ALU.bitwise_xor))
                V(dve.tensor_tensor(st.strict[:, :], s_idx[:, :], t_idx[:, :], ALU.is_lt))
                V(dve.tensor_tensor(st.incl[:, :], s_idx[:, :], t_idx[:, :], ALU.is_le))
                V(dve.tensor_copy(xorf[:, :], xor[:, :]))
                V(dve.tensor_copy(st.iota_row[:, :], t_idx[:, :]))
                V(dve.tensor_scalar(st.same64[:, :], xorf[:, :], 64.0, None, ALU.is_lt))
                for lv in range(7):
                    V(dve.tensor_scalar(tmp[:, :], xorf[:, :], float(2 ** lv), None, ALU.is_ge))
                    V(dve.scalar_tensor_tensor(out=tmp[:, :], in0=xorf[:, :], scalar=float(2 ** (lv + 1)),
                                               in1=tmp[:, :], op0=ALU.is_lt, op1=ALU.mult))
                    V(dve.tensor_tensor(st.level[:, lv, :], tmp[:, :], st.strict[:, :], ALU.mult))
                for g in range(3):
                    bank = m.to_dve.get(dve)
                    m.to_dve.free(dve.tensor_copy(st.vec.cols[:, g, :], bank[:, 0:P]))
                dve.engine_nop()
                dve.drain().then_inc(cols_ready, 1)
                dve.wait_ge(cond_ready, 1)
                with dve.Fori(0, KD) as k:
                    for b in range(4):
                        dve.wait_ge(piece_loaded[b], 16 * (k + 1))
                        part = acc[:, b * PIECE:(b + 1) * PIECE]
                        dve.scalar_tensor_tensor(out=part, in0=ring[:, b, :], scalar=cond[:, bass.ds(k, 1)],
                                                 in1=part, op0=ALU.mult, op1=ALU.add).then_inc(piece_used[b], 1)
                        dve.wait_ge(piece_used[b], k + 1)
                dve.drain().then_inc(acc_ready, 1)
                bank = m.to_dve.get(dve)
                m.to_dve.free(dve.tensor_tensor(st.mod_cols[:, 0:NM // P], bank[:, 0:NM // P],
                                                st.vec.col("ada_b", 0, NM // P), ALU.add))
                dve.drain().then_inc(mod_cols_ready, 1)
                dve.wait_ge(mod_cols_ready, 1)
                modulated_gain(dve, st, "norm_mix", 1, st.gain1)

            @block.scalar
            def _(act):
                act.wait_ge(cols_ready, 1)
                act.activation(cond[:, :], st.vec.col("c", 0, KD), ACT.Silu).then_inc(cond_ready, 1)

            @block.tensor
            def _(pe):
                pe.wait_ge(ident_ready, 1)
                pe.wait_ge(vec_loaded, 16 * n_vec)
                for g in range(3):
                    bank = m.to_dve.take(pe)
                    m.to_dve.put(pe.transpose(bank[:, 0:P], rows[:, g, :], st.ident[:, :]))
                pe.wait_ge(acc_ready, 1)
                pe.wait_ge(ones_ready, 1)
                bank = m.to_dve.take(pe)
                for j in range(NM // P):
                    mm = pe.matmul(bank[:, j:j + 1], acc[:, j * P:(j + 1) * P], ones[:, :], start=True, stop=True)
                m.to_dve.put(mm)


def modulated_gain(dve, st, name, part, dst):
    return dve.scalar_tensor_tensor(out=dst[:, :], in0=st.mod_cols[:, part * KD:(part + 1) * KD], scalar=1.0,
                                    in1=st.vec.col(name, 0, KD), op0=ALU.add, op1=ALU.mult)


class ModulationParts:

    PIECE, RING = 1024, 5

    def __init__(self, m, io, st, ctx, name, parts):
        self.m, self.st, self.w = m, st, io["ada_w"][0]
        self.starts = [part * D + c for part in parts for c in range(0, D, self.PIECE)]
        self.ring = m.sb(ctx, name + "_ring", [P, self.RING, self.PIECE])
        self.acc = m.sb(ctx, name + "_acc", [P, 2, self.PIECE])
        self.row = m.sb(ctx, name + "_row", [KD, P])
        self.loaded = [m.sem(f"{name}_loaded{b}") for b in range(self.RING)]
        self.added, self.summed, self.cols_ready = m.sem(name + "_added"), m.sem(name + "_summed"), m.sem(name + "_cols_ready")
        self.biased = m.sem(name + "_biased")
        self.row_ready, self.stored = m.sem(name + "_row_ready"), m.sem(name + "_row_stored")
        self.n_add = self.n_sum = self.n_col = 0
        self.tiles = len(self.starts) * KD

    def on_pool(self, pool):
        for n in range(self.tiles):
            if n >= self.RING:
                pool.wait_ge(self.added, n - self.RING + 1)
            c0, k = self.starts[n // KD], n % KD
            pool.dma_start(self.ring[:, n % self.RING, :], self.w[k * P:(k + 1) * P, c0:c0 + self.PIECE])\
                .then_inc(self.loaded[n % self.RING], 16)

    def add_tile(self, dve):
        n = self.n_add
        if n == self.tiles:
            return
        piece, k = divmod(n, KD)
        a, tile = self.acc[:, piece % 2, :], self.ring[:, n % self.RING, :]
        if k == 0 and piece >= 2:
            dve.wait_ge(self.summed, piece - 1)
        dve.wait_ge(self.loaded[n % self.RING], 16 * (n // self.RING + 1))
        if n:
            dve.wait_ge(self.added, n)
        if k == 0:
            ins = dve.tensor_scalar(a, tile, self.st.cond[:, 0:1], None, ALU.mult)
        else:
            ins = dve.scalar_tensor_tensor(out=a, in0=tile, scalar=self.st.cond[:, k:k + 1], in1=a,
                                           op0=ALU.mult, op1=ALU.add)
        ins.then_inc(self.added, 1)
        self.n_add = n + 1

    def on_pe(self, pe):
        pe.wait_ge(self.added, (self.n_sum + 1) * KD)
        bank = self.m.to_act.take(pe)
        for j in range(self.PIECE // P):
            mm = pe.matmul(bank[:, j:j + 1], self.acc[:, self.n_sum % 2, j * P:(j + 1) * P], self.st.ones[:, :],
                           start=True, stop=True)
        self.m.to_act.put(mm)
        pe.drain().then_inc(self.summed, 1)
        self.n_sum += 1

    def on_act(self, act):
        bank = self.m.to_act.get(act)
        c, n = self.starts[self.n_col] // P, self.PIECE // P
        self.m.to_act.free(act.activation(self.st.mod_cols[:, c:c + n], bank[:, 0:n], ACT.Copy))
        act.drain().then_inc(self.cols_ready, 1)
        self.n_col += 1

    def add_bias(self, dve):
        dve.wait_ge(self.cols_ready, len(self.starts))
        c, n = self.starts[0] // P, len(self.starts) * self.PIECE // P
        cols = self.st.mod_cols[:, c:c + n]
        dve.tensor_tensor(cols, cols, self.st.vec.col("ada_b", c, n), ALU.add).then_inc(self.biased, 1)
        dve.wait_ge(self.biased, 1)

    def row_pe(self, pe, part):
        pe.wait_ge(self.biased, 1)
        bank = self.m.to_dve.take(pe)
        self.m.to_dve.put(pe.transpose(bank[0:KD, 0:P], self.st.mod_cols[:, part * KD:(part + 1) * KD], self.st.ident[:, :]))

    def row_dve(self, dve):
        bank = self.m.to_dve.get(dve)
        self.m.to_dve.free(dve.tensor_copy(self.row[:, :], bank[0:KD, 0:P]))
        dve.drain().then_inc(self.row_ready, 1)

    def row_store(self, sp, part):
        sp.wait_ge(self.row_ready, 1)
        sp.dma_start(self.st.mod_dram[part * D:(part + 1) * D].rearrange("(r p) -> r p", p=P), self.row[:, :])\
          .then_inc(self.stored, 16)
        sp.wait_ge(self.stored, 16)


def flat(ap):
    names = "abcdefg"[:len(ap.shape)]
    return ap.rearrange(f"{' '.join(names)} -> ({' '.join(names)})") if len(names) > 1 else ap



def norm_to_columns(nc, m, st, name, x, width, dst, gain, shift, x_sem=None, groups=1, k0=0, ahead=()):
    kt = width // P
    with ExitStack() as ctx:
        squares = m.sb(ctx, f"{name}_squares", [P, width // groups])
        scaled = m.sb(ctx, f"{name}_scaled", [P, TT, width])
        ms = m.sb(ctx, f"{name}_ms", [P, TT * groups])
        rms = m.sb(ctx, f"{name}_rms", [P, TT * groups])
        rinv = m.sb(ctx, f"{name}_rinv", [P, TT * groups])
        squared, mean_ready = m.sem(f"{name}_squared"), m.sem(f"{name}_mean_ready")
        root_ready, scaled_ready = m.sem(f"{name}_root_ready"), m.sem(f"{name}_scaled_ready")
        w = width // groups
        whole = m.sb(ctx, f"{name}_whole", [P, 2, 2, T])
        whole_ready, high_ready = m.sem(f"{name}_whole_ready"), m.sem(f"{name}_high_ready")
        low_done = m.sem(f"{name}_low_done")
        with nc.Block() as block:
            @block.sync
            def _(sp):
                for w, c0, n in ahead:
                    m.weights.load(sp, w, c0, n)

            @block.scalar
            def _(act):
                A = m.act_chain.on(act)
                if x_sem:
                    act.wait_ge(*x_sem)
                for tt in range(TT):
                    for g in range(groups):
                        A(act.activation(squares[:, :], x[:, tt, g * w:(g + 1) * w], ACT.Square,
                                         accum_out=ms[:, tt * groups + g:tt * groups + g + 1]))
                act.drain().then_inc(squared, 1)
                act.wait_ge(mean_ready, 1)
                act.activation(rms[:, :], ms[:, :], ACT.Sqrt).then_inc(root_ready, 1)
                for j in range(kt // 2):
                    act.wait_ge(whole_ready, j + 1)
                    act.activation(dst.h[:, k0 + 2 * j:k0 + 2 * j + 2, :], whole[:, j % 2, :, :], ACT.Copy).then_inc(high_ready, 1)

            @block.vector
            def _(dve):
                V = m.dve_chain.on(dve)
                dve.wait_ge(squared, 1)
                dve.tensor_scalar(ms[:, :], ms[:, :], 1.0 / w, EPS, ALU.mult, ALU.add).then_inc(mean_ready, 1)
                dve.wait_ge(root_ready, 1)
                V(dve.reciprocal(rinv[:, :], rms[:, :]))
                for tt in range(TT):
                    for g in range(groups):
                        dve.tensor_scalar(scaled[:, tt, g * w:(g + 1) * w], x[:, tt, g * w:(g + 1) * w],
                                          rinv[:, tt * groups + g:tt * groups + g + 1], None, ALU.mult)
                dve.drain().then_inc(scaled_ready, 1)
                def low(j):
                    dve.wait_ge(high_ready, j + 1)
                    k = k0 + 2 * j
                    dve.tensor_tensor(dst.l[:, k:k + 2, :], whole[:, j % 2, :, :], dst.h[:, k:k + 2, :],
                                      ALU.subtract).then_inc(low_done, 1)

                for j in range(kt // 2):
                    if j >= 2:
                        dve.wait_ge(low_done, j - 1)
                    bank = m.to_dve.get(dve)
                    for u in range(2):
                        k = 2 * j + u
                        src, o = bank[:, u * T:(u + 1) * T], whole[:, j % 2, u, :]
                        if shift:
                            ins = dve.tensor_scalar(o, src, gain(k), shift(k), ALU.mult, ALU.add)
                        else:
                            ins = dve.tensor_scalar(o, src, gain(k), None, ALU.mult)
                    m.to_dve.free(ins)
                    dve.drain().then_inc(whole_ready, 1)
                    if j:
                        low(j - 1)
                low(kt // 2 - 1)

            @block.tensor
            def _(pe):
                pe.wait_ge(scaled_ready, 1)
                turn_to_columns(pe, m.to_dve, st.ident[:, :], lambda k, tt: scaled[:, tt, k * P:(k + 1) * P], kt)


def first_chunks(w, c0=0):
    return [(w, c0 + c, CHUNK) for c in (0, CHUNK)]


def project(nc, m, st, acts, kt, w, c0, n, out, loaded=0):
    work = chunks(n)
    with ExitStack() as ctx:
        m.weights.split_memory(ctx)
        with nc.Block() as block:
            @block.sync
            def _(sp):
                for c, size in work[loaded:]:
                    m.weights.load(sp, w, c0 + c, size)

            @block.tensor
            def _(pe):
                for c, size in work:
                    m.weights.multiply_split(pe, acts, kt, size, m.to_dve)

            @block.scalar
            def _(act):
                for c, size in work:
                    m.weights.split_high(act, kt, size)

            @block.vector
            def _(dve):
                for i, (c, size) in enumerate(work + [(None, 0)]):
                    if c is not None:
                        m.weights.split_low(dve, kt, size)
                    if i:
                        c, size = work[i - 1]
                        for tt in range(TT):
                            bank = m.to_dve.get(dve)
                            m.to_dve.free(dve.tensor_copy(out(tt, c, size), bank[:, 0:size]))


def project_in(nc, m, io, st, acts, out):
    work = chunks(N_IN)
    with ExitStack() as ctx:
        m.weights.split_memory(ctx)
        mod = ModulationParts(m, io, st, ctx, "mod_mid", (3, 4))
        w = io["w_in"][0]
        pieces = len(mod.starts)
        after = {2 * p + 3: p for p in range(pieces) if 2 * p + 3 < len(work)}
        with nc.Block() as block:
            @block.sync
            def _(sp):
                for c, size in work[2:]:
                    m.weights.load(sp, w, c, size)
                mod.row_store(sp, 2)

            @block.gpsimd
            def _(pool):
                mod.on_pool(pool)

            @block.tensor
            def _(pe):
                for i, (c, size) in enumerate(work):
                    m.weights.multiply_split(pe, acts, KD, size, m.to_dve)
                    if i in after:
                        mod.on_pe(pe)
                for _p in range(pieces - mod.n_sum):
                    mod.on_pe(pe)
                mod.row_pe(pe, 2)

            @block.scalar
            def _(act):
                for i, (c, size) in enumerate(work):
                    m.weights.split_high(act, KD, size)
                    if i - 1 in after:
                        mod.on_act(act)
                for _p in range(pieces - mod.n_col):
                    mod.on_act(act)

            @block.vector
            def _(dve):
                for i in range(len(work) + 1):
                    if i < len(work):
                        m.weights.split_low(dve, KD, work[i][1], between=mod.add_tile)
                    if i:
                        c, size = work[i - 1]
                        for tt in range(TT):
                            bank = m.to_dve.get(dve)
                            m.to_dve.free(dve.tensor_copy(out(tt, c, size), bank[:, 0:size]))
                mod.add_bias(dve)
                modulated_gain(dve, st, "norm_ffn", 4, st.gain2)
                mod.row_dve(dve)


def project_whole(nc, m, acts, kt, w, n, out):
    with nc.Block() as block:
        @block.sync
        def _(sp):
            for c, size in chunks(n):
                m.weights.load(sp, w, c, size)

        @block.tensor
        def _(pe):
            for c, size in chunks(n):
                m.weights.multiply(pe, acts, kt, size, m.to_dve)

        @block.vector
        def _(dve):
            for c, size in chunks(n):
                m.weights.seen("act", "dve")
                for tt in range(TT):
                    bank = m.to_dve.get(dve)
                    m.to_dve.free(dve.tensor_copy(out(tt, c, size), bank[:, 0:size]))


class State:
    pass


def shared_state(m):
    st = State()
    st.vec = Vectors(m)
    st.x = m.sb(m.ctx, "x_rows", [P, TT, D])
    st.ident = m.sb(m.ctx, "ident", [P, P])
    st.strict = m.sb(m.ctx, "strict_mask", [P, P])
    st.incl = m.sb(m.ctx, "incl_mask", [P, P])
    st.same64 = m.sb(m.ctx, "same64_mask", [P, P])
    st.level = m.sb(m.ctx, "level_masks", [P, 7, P])
    st.iota_row = m.sb(m.ctx, "iota_row", [P, P])
    st.mod_cols = m.sb(m.ctx, "mod_cols", [P, 6 * KD])
    st.gain1 = m.sb(m.ctx, "gain1", [P, KD])
    st.gain2 = m.sb(m.ctx, "gain2", [P, KD])
    st.cond = m.sb(m.ctx, "cond", [P, KD])
    st.ones = m.sb(m.ctx, "ones_col", [P, 1])
    st.gain_count = 0
    st.mod_dram = m.dram("mod_row", [6 * D])
    return st


def view(ap, dims, offset=0):
    return bass.AP(tensor=ap.tensor, offset=ap.offset + offset, ap=[list(ap.ap[0])] + [list(d) for d in dims])


def spread(ap, n):
    return bass.AP(tensor=ap.tensor, offset=ap.offset, ap=[list(d) for d in ap.ap] + [[0, n]])



BUCKETS, MAX_DIST = 32, 2048
CMP_BLOCK, CMP_STRIDE = 32, 16
N_CMP = (T - CMP_BLOCK) // CMP_STRIDE + 1
BIAS_W = T + P


def bucket_starts():
    exact = BUCKETS // 2
    d = np.arange(4 * MAX_DIST)
    ratio = np.log(np.maximum(d, exact).astype(np.float32) / np.float32(exact)) / np.float32(np.log(MAX_DIST / exact))
    large = exact + (ratio * np.float32(BUCKETS - exact)).astype(np.int32)
    b = np.where(d < exact, d, np.minimum(large, BUCKETS - 1))
    return [int(np.argmax(b >= i)) for i in range(BUCKETS)]


def stage_attention(nc, m, io, st, proj, attn):
    starts = bucket_starts()
    MASKED = BUCKETS
    bias_dram = m.dram("bias_rows", [HEADS, P, 2 * T])
    with ExitStack() as ctx:
        bias = m.sb(ctx, "bias", [P, HEADS, BIAS_W])
        qT = m.sb(ctx, "queries_T", [P, HEADS // 2, T])
        PT_memory = m.sb(ctx, "probs_T", [P, HEADS // 2, T])
        kvT = m.sb(ctx, "kvT", [P, 4, T])
        gates = m.sb(ctx, "gates", [P, TT, 3 * HEADS])
        kcT = m.sb(ctx, "kcT", [P, N_CMP])
        vblk = m.sb(ctx, "v_cmp_blocks", [8 * N_CMP, KV_HEADS, GROUP * DH])
        with ExitStack() as c1:
            table = m.sb(c1, "bias_table", [BUCKETS + 1, HEADS])
            lo = m.sb(c1, "bucket_lo", [BUCKETS + 1, 1])
            hi = m.sb(c1, "bucket_hi", [BUCKETS + 1, 1])
            dist = m.sb(c1, "dist_row", [BUCKETS + 1, 2 * T])
            dge = m.sb(c1, "dist_ge", [BUCKETS + 1, 2 * T])
            onehot = m.sb(c1, "bucket_onehot", [BUCKETS + 1, 2 * T])
            vec = m.sb(c1, "bias_vec", [HEADS, 2 * T])
            pairs = m.sb(c1, "token_pairs", [P, 2, KV_HEADS, T])
            blocks = m.sb(c1, "cmp_inputs", [P, 2, CMP_BLOCK // 2, KV_HEADS, N_CMP])
            hid = m.sb(c1, "cmp_hidden", [P, 2, 2, KV_HEADS * N_CMP])
            w2 = m.sb(c1, "cmp_w2_sb", [P, 2, 2, DH])
            qpair = attn[:, :, :].rearrange("p t (j g d) -> p t j g d", g=KV_HEADS, d=DH)
            qpair_ready = m.sem("query_pairs_ready")
            vc = m.sb(c1, "v_cmp", [N_CMP, KV_HEADS, DH])
            lo_ready, hi_ready, table_loaded = m.sem("bucket_lo_ready"), m.sem("bucket_hi_ready"), m.sem("bias_table_loaded")
            onehot_ready, vec_ready, vec_stored = m.sem("onehot_ready"), m.sem("bias_vec_ready"), m.sem("bias_vec_stored")
            kv_turned, pairs_zero, pairs_loaded = m.sem("kv_turned"), m.sem("pairs_zeroed"), m.sem("pairs_loaded")
            blocks_ready, hid_ready, w2_loaded = m.sem("cmp_inputs_ready"), m.sem("cmp_hidden_ready"), m.sem("cmp_w2_loaded")
            vc_ready, bias_loaded = m.sem("v_cmp_ready"), m.sem("bias_loaded")
            with nc.Block() as block:
                @block.gpsimd
                def _(pool):
                    L = m.pool_chain.on(pool)
                    L(pool.iota(dist[:, :], pattern=[[-1, 2 * T]], base=T - 1, channel_multiplier=0,
                                allow_small_or_imprecise_dtypes=True))
                    L(pool.memset(lo[:, :], -4.0 * T))
                    L(pool.memset(hi[:, :], 0.0))
                    for b in range(BUCKETS):
                        last = b == BUCKETS - 1
                        for t, v in ((lo, starts[b]), (hi, 8 * MAX_DIST if last else starts[b + 1])):
                            L(pool.affine_select(out=t[:, :], in_=t[:, :], compare_op=ALU.not_equal, fill=float(v),
                                                 base=-b, pattern=[[0, 1]], channel_multiplier=1))
                    pool.drain().then_inc(lo_ready, 1)
                    L(pool.memset(pairs[:, :, :, :], 0.0))
                    pool.memset(vblk[:, :, :], 0.0).then_inc(pairs_zero, 1)

                @block.sync
                def _(sp):
                    sp.dma_start(table[0:BUCKETS, :], io["rel_bias"]).then_inc(table_loaded, 16)
                    for kv in range(2):
                        m.weights.load(sp, io["cmp_w1"][0, kv], 0, 4 * DH)
                        sp.dma_start(w2[:, kv, :, :], io["cmp_w2"][0, kv].rearrange("(h p) d -> p h d", p=P)).then_inc(w2_loaded, 16)
                    sp.wait_ge(kv_turned, 1)
                    sp.wait_ge(pairs_zero, 1)
                    for kv in range(2):
                        for g in range(KV_HEADS):
                            src = kvT[g * DH:(g + 1) * DH, kv, :]
                            sp.dma_start(pairs[0:DH, kv, g, :], src).then_inc(pairs_loaded, 16)
                            sp.dma_start(pairs[DH:P, kv, g, 0:T - 1], src[:, 1:T]).then_inc(pairs_loaded, 16)
                    sp.wait_ge(vec_ready, 1)
                    sp.dma_start(bias_dram, view(vec[:, 0:1], [[0, P], [1, 2 * T]])).then_inc(vec_stored, 16)
                    sp.wait_ge(vec_stored, 16)
                    for h in range(HEADS):
                        src = bass.AP(tensor=bias_dram.tensor, offset=h * P * 2 * T + T - 1 - P, ap=[[2 * T - 1, P], [1, BIAS_W]])
                        sp.dma_start(bias[:, h, :], src).then_inc(bias_loaded, 16)
                    sp.wait_ge(vc_ready, 1)
                    for g in range(KV_HEADS):
                        for h in range(GROUP):
                            sp.dma_start(vblk[h * N_CMP:(h + 1) * N_CMP, g, h * DH:(h + 1) * DH], vc[:, g, :])\
                              .then_inc(bias_loaded, 16)
                    sp.wait_ge(bias_loaded, 16 * 2 * HEADS)

                @block.tensor
                def _(pe):
                    pe.wait_ge(qpair_ready, 1)
                    for j in range(2):
                        bank = m.to_dve.take(pe)
                        for u in range(2):
                            c = KV0 + (0, 1, 2, 4)[2 * j + u] * P
                            for tt in range(TT):
                                mm = pe.transpose(bank[:, (u * TT + tt) * P:(u * TT + tt + 1) * P],
                                                  proj[:, tt, c:c + P], st.ident[:, :])
                        m.to_dve.put(mm)
                    turn_to_columns(pe, m.to_dve, st.ident[:, :],
                                    lambda j, tt: qpair[:, tt, j, :, :].rearrange("p g d -> p (g d)"), 8)
                    pe.wait_ge(onehot_ready, 1)
                    bank = m.to_dve.take(pe)
                    m.to_dve.put(pe.matmul(bank[0:HEADS, :], table[:, :], onehot[:, :], start=True, stop=True))
                    pe.wait_ge(blocks_ready, 1)
                    for kv in range(2):
                        b, turn = m.weights.n_use % 2, m.weights.n_use // 2
                        pe.wait_ge(m.weights.loaded[b], 16 * (turn + 1))
                        bank = m.to_act.take(pe)
                        for hh in range(2):
                            for jj in range(KD):
                                mm = pe.matmul(bank[:, hh * 32:hh * 32 + KV_HEADS * N_CMP],
                                               m.weights.buf[b][:, jj, hh * P:(hh + 1) * P],
                                               blocks[:, kv, jj, :, :], start=(jj == 0), stop=(jj == KD - 1))
                        m.to_act.put(mm)
                        pe.drain().then_inc(m.weights.used[b], 1)
                        m.weights.n_use += 1
                        m.weights.seen("act", "dve")
                    pe.wait_ge(hid_ready, 1)
                    pe.wait_ge(w2_loaded, 32)
                    bank = m.to_dve.take(pe)
                    for g in range(KV_HEADS):
                        for hh in range(2):
                            mm = pe.matmul(bank[g * DH:(g + 1) * DH, 0:N_CMP], w2[:, 0, hh, :],
                                           hid[:, 0, hh, g * N_CMP:(g + 1) * N_CMP], start=(hh == 0), stop=(hh == 1))
                    m.to_dve.put(mm)
                    bank = m.to_dve.take(pe)
                    for g in range(KV_HEADS):
                        for hh in range(2):
                            mm = pe.matmul(bank[0:N_CMP, g * DH:(g + 1) * DH], hid[:, 1, hh, g * N_CMP:(g + 1) * N_CMP],
                                           w2[:, 1, hh, :], start=(hh == 0), stop=(hh == 1))
                    m.to_dve.put(mm)

                @block.scalar
                def _(act):
                    act.activation(gates[:, :, :], proj[:, :, GATE0:GATE0 + 3 * HEADS], ACT.Sigmoid)
                    for kv in range(2):
                        bank = m.to_act.get(act)
                        m.to_act.free(act.activation(hid[:, kv, :, :], view(bank[:, 0:1], [[32, 2], [1, KV_HEADS * N_CMP]]),
                                                     ACT.Gelu_apprx_tanh))
                    act.drain().then_inc(hid_ready, 1)

                @block.vector
                def _(dve):
                    V = m.dve_chain.on(dve)
                    for tt in range(TT):
                        for g in range(KV_HEADS):
                            src = proj[:, tt, Q0 + g * HALF // 2:Q0 + (g + 1) * HALF // 2].rearrange("p (j d) -> p j d", d=DH)
                            dve.tensor_scalar(qpair[:, tt, :, g, :], src, DH ** -0.5, None, ALU.mult)
                    dve.drain().then_inc(qpair_ready, 1)
                    for j in range(2):
                        bank = m.to_dve.get(dve)
                        m.to_dve.free(dve.tensor_copy(kvT[:, 2 * j:2 * j + 2, :], bank[:, :]))
                    dve.drain().then_inc(kv_turned, 1)
                    for j in range(4):
                        bank = m.to_dve.get(dve)
                        m.to_dve.free(dve.tensor_copy(qT[:, 2 * j:2 * j + 2, :], bank[:, :]))
                    V(dve.memset(table[BUCKETS:BUCKETS + 1, :], NEG))
                    dve.wait_ge(lo_ready, 1)
                    V(dve.tensor_scalar(dge[:, :], dist[:, :], lo[:, 0:1], None, ALU.is_ge))
                    V(dve.scalar_tensor_tensor(out=onehot[:, :], in0=dist[:, :], scalar=hi[:, 0:1], in1=dge[:, :],
                                               op0=ALU.is_lt, op1=ALU.mult))
                    dve.wait_ge(table_loaded, 16)
                    dve.drain().then_inc(onehot_ready, 1)
                    bank = m.to_dve.get(dve)
                    m.to_dve.free(dve.tensor_copy(vec[:, :], bank[0:HEADS, :]))
                    dve.drain().then_inc(vec_ready, 1)
                    dve.wait_ge(pairs_loaded, 8 * 16)
                    for kv in range(2):
                        for g in range(KV_HEADS):
                            dve.tensor_tensor(blocks[:, kv, :, g, :],
                                              view(pairs[:, kv, g, 0:1], [[2, CMP_BLOCK // 2], [CMP_STRIDE, N_CMP]]),
                                              spread(st.vec.col("cmp_pe", kv * 16, 16), N_CMP), ALU.add)
                    dve.drain().then_inc(blocks_ready, 1)
                    bank = m.to_dve.get(dve)
                    m.to_dve.free(dve.tensor_copy(kcT[:, :], bank[:, 0:N_CMP]))
                    bank = m.to_dve.get(dve)
                    m.to_dve.free(dve.tensor_copy(vc[:, :, :], bank[0:N_CMP, 0:P]))
                    dve.drain().then_inc(vc_ready, 1)

        units = [(qt, g, br) for qt in range(TT) for g in range(KV_HEADS) for br in range(3)]
        with ExitStack() as c2:
            S = m.sb(c2, "scores", [P, 2, GROUP, T])
            PT = PT_memory[:, :, :].rearrange("p k (e q) -> p (k e) q", q=P)\
                        .rearrange("p (t h) q -> p t h q", h=GROUP)
            nmax = m.sb(c2, "neg_max", [P, len(units), GROUP])
            sums = m.sb(c2, "prob_sums", [P, len(units), GROUP])
            coef = m.sb(c2, "branch_coef", [P, len(units), GROUP])
            part = m.sb(c2, "branch_part", [P, GROUP, DH])
            rowok = m.sb(c2, "cmp_row_ok", [P, 1])
            shifted, probs, turned = m.sem("scores_shifted"), m.sem("probs_ready"), m.sem("probs_turned")
            pv_done, rowok_ready = m.sem("pv_done"), m.sem("row_ok_ready")
            with nc.Block() as block:
                def keys(qt, br):
                    return N_CMP if br == 0 else (qt + 1) * P

                @block.gpsimd
                def _(pool):
                    L = m.pool_chain.on(pool)
                    L(pool.memset(rowok[:, :], 1.0))
                    pool.affine_select(out=rowok[:, :], in_=rowok[:, :], compare_op=ALU.is_ge, fill=0.0,
                                       base=-(CMP_BLOCK - 1), pattern=[[0, 1]], channel_multiplier=1).then_inc(rowok_ready, 1)

                @block.tensor
                def _(pe):
                    def scores(u):
                        qt, g, br = units[u]
                        gp = slice(g * DH, (g + 1) * DH)
                        if br == 0:
                            bank = m.to_dve.take(pe)
                            for h in range(GROUP):
                                mm = pe.matmul(bank[:, h * N_CMP:(h + 1) * N_CMP], qT[gp, h, qt * P:(qt + 1) * P],
                                               kcT[gp, :], start=True, stop=True)
                            m.to_dve.put(mm)
                            return
                        n = keys(qt, br)
                        for h in range(0, GROUP, 2):
                            bank = m.to_dve.take(pe)
                            for e in range(2):
                                mm = pe.matmul(bank[:, e * T:e * T + n], qT[gp, h + e, qt * P:(qt + 1) * P],
                                               kvT[gp, 1 + br, 0:n], start=True, stop=True)
                            m.to_dve.put(mm)

                    def values(u):
                        qt, g, br = units[u]
                        pe.wait_ge(probs, u + 1)
                        if br == 0:
                            bank = m.to_act.take(pe)
                            m.to_act.put(pe.transpose(bank[0:GROUP * N_CMP, 0:P], view(S[:, u % 2, 0, 0:1], [[1, GROUP * N_CMP]]),
                                                      st.ident[:, :]))
                            pe.wait_ge(turned, u + 1)
                            bank = m.to_dve.take(pe)
                            mm = pe.matmul(bank[:, :], PT[0:GROUP * N_CMP, 0, 0, :], vblk[:, g, :], start=True, stop=True)
                            m.to_dve.put(mm)
                        else:
                            for kt in range(qt + 1):
                                for q4 in range(2):
                                    bank = m.to_act.take(pe)
                                    for e in range(4):
                                        mm = pe.transpose(bank[:, e * P:(e + 1) * P],
                                                          S[:, u % 2, q4 * 4 + e, kt * P:(kt + 1) * P], st.ident[:, :])
                                    m.to_act.put(mm)
                            pe.wait_ge(turned, u + 1)
                            bank = m.to_dve.take(pe)
                            for h in range(GROUP):
                                for kt in range(qt + 1):
                                    c = KV0 + (2 * br + 1) * P + g * DH
                                    mm = pe.matmul(bank[:, h * DH:(h + 1) * DH], PT[:, kt, h, :], proj[:, kt, c:c + DH],
                                                   start=(kt == 0), stop=(kt == qt))
                            m.to_dve.put(mm)
                        pe.drain().then_inc(pv_done, 1)

                    for u in range(len(units) + 1):
                        if u < len(units):
                            scores(u)
                        if u:
                            values(u - 1)

                @block.scalar
                def _(act):
                    for u, (qt, g, br) in enumerate(units):
                        act.wait_ge(shifted, u + 1)
                        if br == 0:
                            flat_s = view(S[:, u % 2, 0, 0:1], [[1, GROUP * N_CMP]])
                            act.activation(flat_s, flat_s, ACT.Exp)
                        else:
                            for h in range(GROUP):
                                row = S[:, u % 2, h, 0:keys(qt, br)]
                                act.activation(row, row, ACT.Exp, bias=nmax[:, u, h:h + 1],
                                               accum_out=sums[:, u, h:h + 1])
                        act.drain().then_inc(probs, 1)
                        if u:
                            act.wait_ge(pv_done, u)
                        if br == 0:
                            bank = m.to_act.get(act)
                            m.to_act.free(act.activation(PT[0:GROUP * N_CMP, 0, 0, :], bank[0:GROUP * N_CMP, 0:P], ACT.Copy))
                        else:
                            for kt in range(qt + 1):
                                for q4 in range(2):
                                    bank = m.to_act.get(act)
                                    m.to_act.free(act.activation(PT[:, kt, q4 * 4:q4 * 4 + 4, :], bank[:, :], ACT.Copy))
                        act.drain().then_inc(turned, 1)

                @block.vector
                def _(dve):
                    V = m.dve_chain.on(dve)

                    def shift(u):
                        qt, g, br = units[u]
                        n = keys(qt, br)
                        off = (TT - 1 - qt) * P
                        if u >= 2:
                            dve.wait_ge(pv_done, u - 1)
                        if br == 0:
                            s = view(S[:, u % 2, 0, 0:1], [[N_CMP, GROUP], [1, N_CMP]])
                            bank = m.to_dve.get(dve)
                            b = view(bias[:, g * GROUP, 0:1], [[BIAS_W, GROUP], [CMP_STRIDE, N_CMP]], off + CMP_BLOCK - 1)
                            m.to_dve.free(dve.tensor_tensor(s, view(bank[:, 0:1], [[N_CMP, GROUP], [1, N_CMP]]), b, ALU.add))
                            V(dve.engine_nop())
                            V(dve.tensor_reduce(nmax[:, u, :], s, AX_X, ALU.max))
                            V(dve.tensor_tensor(s, s, spread(nmax[:, u, :], N_CMP), ALU.subtract))
                        else:
                            for h in range(0, GROUP, 2):
                                bank = m.to_dve.get(dve)
                                m.to_dve.free(dve.tensor_tensor(
                                    S[:, u % 2, h:h + 2, 0:n], view(bank[:, 0:1], [[T, 2], [1, n]]),
                                    bias[:, g * GROUP + h:g * GROUP + h + 2, off:off + n], ALU.add))
                            V(dve.engine_nop())
                            V(dve.tensor_reduce(nmax[:, u, :], S[:, u % 2, :, 0:n], AX_X, ALU.max, negate=True))
                        dve.drain().then_inc(shifted, 1)

                    def combine(u):
                        qt, g, br = units[u]
                        dve.wait_ge(probs, u + 1)
                        if br == 0:
                            V(dve.tensor_reduce(sums[:, u, :], view(S[:, u % 2, 0, 0:1], [[N_CMP, GROUP], [1, N_CMP]]),
                                                AX_X, ALU.add))
                        V(dve.reciprocal(coef[:, u, :], sums[:, u, :]))
                        gate = view(gates[:, qt, 0:1], [[3, GROUP]], g * GROUP * 3 + br)
                        V(dve.tensor_tensor(coef[:, u, :], coef[:, u, :], gate, ALU.mult))
                        if br == 0 and qt == 0:
                            dve.wait_ge(rowok_ready, 1)
                            V(dve.tensor_scalar(coef[:, u, :], coef[:, u, :], rowok[:, 0:1], None, ALU.mult))
                        bank = m.to_dve.get(dve)
                        src = view(bank[:, 0:1], [[DH, GROUP], [1, DH]])
                        out = view(attn[:, qt, g * GROUP * DH:g * GROUP * DH + 1], [[DH, GROUP], [1, DH]])
                        if br == 0:
                            m.to_dve.free(dve.tensor_tensor(out, src, spread(coef[:, u, :], DH), ALU.mult))
                        else:
                            m.to_dve.free(dve.tensor_tensor(part[:, :, :], src, spread(coef[:, u, :], DH), ALU.mult))
                            V(dve.engine_nop())
                            V(dve.tensor_tensor(out, out, part[:, :, :], ALU.add))
                        V(dve.engine_nop())

                    for u in range(len(units) + 1):
                        if u < len(units):
                            shift(u)
                        if u:
                            combine(u - 1)


def turn_to_rows(pe, ring, ident, src, kt, per=4):
    for tt in range(TT):
        for k0 in range(0, kt, per):
            bank = ring.take(pe)
            for e in range(per):
                mm = pe.transpose(bank[:, e * P:(e + 1) * P], src(k0 + e, tt), ident)
            ring.put(mm)


def everywhere(ap, n):
    return bass.AP(tensor=ap.tensor, offset=ap.offset, ap=[[0, P], [1, n]])


def causal_conv(dve, V, src, dst, tiles, tap, first):
    for j in range(CONV_TAPS - 1, -1, -1):
        for k in range(tiles):
            u = src[:, k, j:j + T]
            if j == CONV_TAPS - 1:
                ins = first(k, u)
            else:
                ins = dve.scalar_tensor_tensor(out=dst[:, k, :], in0=u, scalar=tap(j, k), in1=dst[:, k, :],
                                               op0=ALU.mult, op1=ALU.add)
        V(ins)


class Softplus:

    TERMS = 10

    def __init__(self, m, ctx, name, n):
        self.x, self.e, self.z, self.w, self.s = (m.sb(ctx, f"{name}_sp_{s}", [n, T]) for s in "xezws")
        self.abs_ready, self.e_ready = m.sem(f"{name}_abs_ready"), m.sem(f"{name}_exp_ready")

    def on_dve(self, dve, V, out):
        x, e, z, w, s = (a[:, :] for a in (self.x, self.e, self.z, self.w, self.s))
        V(dve.scalar_tensor_tensor(out=e, in0=x, scalar=-1.0, in1=x, op0=ALU.mult, op1=ALU.max))
        dve.drain().then_inc(self.abs_ready, 1)
        dve.wait_ge(self.e_ready, 1)
        V(dve.tensor_scalar(z, e, 2.0, None, ALU.add))
        V(dve.reciprocal(z, z))
        V(dve.tensor_tensor(z, z, e, ALU.mult))
        V(dve.tensor_tensor(w, z, z, ALU.mult))
        V(dve.tensor_scalar(s, w, 1.0 / (2 * self.TERMS - 1), None, ALU.mult))
        for k in range(self.TERMS - 2, 0, -1):
            V(dve.scalar_tensor_tensor(out=s, in0=s, scalar=1.0 / (2 * k + 1), in1=w, op0=ALU.add, op1=ALU.mult))
        V(dve.scalar_tensor_tensor(out=s, in0=s, scalar=1.0, in1=z, op0=ALU.add, op1=ALU.mult))
        V(dve.tensor_scalar(s, s, 2.0, None, ALU.mult))
        V(dve.scalar_tensor_tensor(out=out, in0=x, scalar=0.0, in1=s, op0=ALU.max, op1=ALU.add))

    def on_act(self, act):
        act.wait_ge(self.abs_ready, 1)
        act.activation(self.e[:, :], self.e[:, :], ACT.Exp, scale=-1.0).then_inc(self.e_ready, 1)



SSM_HEADS, SSM_GROUPS = 16, 2
XBC_TILES, X_TILES = 12, 8


def stage_mamba(nc, m, io, st, proj, y):
    with ExitStack() as ctx:
        conv = m.sb(ctx, "xbc_conv", [P, XBC_TILES, T])
        xr = arrays_of(m.weights.buf[0], 1, [TT, HALF])[0]
        dtc = m.sb(ctx, "dt_cols", [P, TT, SSM_HEADS])
        acsc = m.sb(ctx, "acs_cols", [P, TT, SSM_HEADS])
        cb = m.sb(ctx, "cb_masked", [P, SSM_GROUPS, TT, T])
        acs = m.sb(ctx, "acs", [SSM_HEADS, T])
        dsk = m.sb(ctx, "d_skip_rows", [P, SSM_HEADS])
        with ExitStack() as c1:
            u = m.sb(c1, "xbc_padded", [P, XBC_TILES, T + CONV_TAPS - 1])
            sp_ = Softplus(m, c1, "ssm", SSM_HEADS)
            dt = m.sb(c1, "dt", [SSM_HEADS, T])
            dta = m.sb(c1, "dt_a", [SSM_HEADS, T])
            ones = m.sb(c1, "ssm_ones", [SSM_HEADS, T])
            bias = m.sb(c1, "dt_bias_col", [SSM_HEADS, 1])
            alog = m.sb(c1, "a_log_col", [SSM_HEADS, 1])
            loaded, exp_a, conv_sum, conv_done = m.sem("ssm_small_loaded"), m.sem("ssm_exp_a"), m.sem("ssm_conv_summed"), m.sem("ssm_conv_done")
            acs_ready = m.sem("acs_ready")
            with nc.Block() as block:
                @block.sync
                def _(sp):
                    sp.dma_start(bias[:, :], io["dt_bias"].rearrange("a h -> h a")).then_inc(loaded, 16)
                    sp.dma_start(alog[:, :], io["a_log"].rearrange("a h -> h a")).then_inc(loaded, 16)
                    sp.dma_start(dsk[:, :], everywhere(io["d_skip"], SSM_HEADS)).then_inc(loaded, 16)
                    sp.wait_ge(loaded, 48)

                @block.scalar
                def _(act):
                    sp_.on_act(act)
                    act.wait_ge(loaded, 48)
                    act.activation(alog[:, :], alog[:, :], ACT.Exp).then_inc(exp_a, 1)
                    act.activation(proj[:, :, Z0:Z0 + HALF], proj[:, :, Z0:Z0 + HALF], ACT.Silu)
                    for k in range(XBC_TILES // 4):
                        act.wait_ge(conv_sum, k + 1)
                        act.activation(conv[:, 4 * k:4 * k + 4, :], conv[:, 4 * k:4 * k + 4, :], ACT.Silu)
                        act.drain().then_inc(conv_done, 1)

                @block.tensor
                def _(pe):
                    bank = m.to_dve.take(pe)
                    for tt in range(TT):
                        mm = pe.transpose(bank[0:SSM_HEADS, tt * P:(tt + 1) * P], proj[:, tt, DT0:DT0 + SSM_HEADS], st.ident[:, :])
                    m.to_dve.put(mm)
                    turn_to_columns(pe, m.to_dve, st.ident[:, :],
                                    lambda k, tt: proj[:, tt, XBC0 + k * P:XBC0 + (k + 1) * P], XBC_TILES)
                    pe.wait_ge(acs_ready, 1)
                    bank = m.to_dve.take(pe)
                    for i, src in enumerate((dt, acs)):
                        for tt in range(TT):
                            c = (i * TT + tt) * SSM_HEADS
                            mm = pe.transpose(bank[:, c:c + SSM_HEADS], src[:, tt * P:(tt + 1) * P],
                                              st.ident[0:SSM_HEADS, 0:SSM_HEADS])
                    m.to_dve.put(mm)
                    pe.wait_ge(conv_done, 3)
                    for g in range(SSM_GROUPS):
                        bank = m.to_dve.take(pe)
                        for tt in range(TT):
                            mm = pe.matmul(bank[:, tt * T:(tt + 1) * T], conv[:, X_TILES + g, tt * P:(tt + 1) * P],
                                           conv[:, X_TILES + SSM_GROUPS + g, :], start=True, stop=True)
                        m.to_dve.put(mm)
                    turn_to_rows(pe, m.to_dve, st.ident[:, :], lambda k, tt: conv[:, k, tt * P:(tt + 1) * P], X_TILES)

                @block.vector
                def _(dve):
                    V = m.dve_chain.on(dve)
                    V(dve.memset(u[:, :, 0:CONV_TAPS - 1], 0.0))
                    V(dve.memset(ones[:, :], 1.0))
                    dve.wait_ge(loaded, 48)
                    bank = m.to_dve.get(dve)
                    m.to_dve.free(dve.tensor_scalar(sp_.x[:, :], bank[0:SSM_HEADS, 0:T], bias[:, 0:1], None, ALU.add))
                    V(dve.engine_nop())
                    for j in range(XBC_TILES // 2):
                        bank = m.to_dve.get(dve)
                        m.to_dve.free(dve.tensor_copy(u[:, 2 * j:2 * j + 2, CONV_TAPS - 1:], view(bank[:, 0:1], [[T, 2], [1, T]])))
                    sp_.on_dve(dve, V, dt[:, :])
                    dve.wait_ge(exp_a, 1)
                    V(dve.tensor_scalar(dta[:, :], dt[:, :], alog[:, 0:1], -1.0, ALU.mult, ALU.mult))
                    V(dve.tensor_tensor_scan(acs[:, :], ones[:, :], dta[:, :], 0.0, ALU.mult, ALU.add))
                    dve.drain().then_inc(acs_ready, 1)
                    for k in range(XBC_TILES // 4):
                        causal_conv(dve, V, u[:, 4 * k:4 * k + 4, :], conv[:, 4 * k:4 * k + 4, :], 4,
                                    lambda j, i: st.vec.col("conv_w", j * XBC_TILES + 4 * k + i),
                                    lambda i, src: dve.tensor_scalar(conv[:, 4 * k + i, :], src,
                                                                     st.vec.col("conv_w", (CONV_TAPS - 1) * XBC_TILES + 4 * k + i),
                                                                     st.vec.col("conv_b", 4 * k + i), ALU.mult, ALU.add))
                        dve.drain().then_inc(conv_sum, 1)
                    bank = m.to_dve.get(dve)
                    n = TT * SSM_HEADS
                    dve.tensor_copy(dtc[:, :, :], bank[:, 0:n])
                    m.to_dve.free(dve.tensor_copy(acsc[:, :, :], bank[:, n:2 * n]))
                    for g in range(SSM_GROUPS):
                        bank = m.to_dve.get(dve)
                        dve.tensor_tensor(cb[:, g, 0, 0:P], bank[:, 0:P], st.incl[:, :], ALU.mult)
                        dve.tensor_copy(cb[:, g, 0, P:T], bank[:, P:T])
                        m.to_dve.free(dve.tensor_tensor(cb[:, g, 1, P:T], bank[:, T + P:2 * T], st.incl[:, :], ALU.mult))
                    for tt in range(TT):
                        for k in range(2):
                            bank = m.to_dve.get(dve)
                            m.to_dve.free(dve.tensor_copy(xr[:, tt, k * CHUNK:(k + 1) * CHUNK], bank[:, :]))
        with ExitStack() as c2:
            GH = SSM_HEADS // SSM_GROUPS
            M = m.sb(c2, "decay_T", [P, GH, T + P])
            seg, dec, mready = m.sem("segments_ready"), m.sem("decays_ready"), m.sem("ssm_mix_ready")
            y_read = m.sem("ssm_y_read")
            with nc.Block() as block:
                @block.tensor
                def _(pe):
                    for g in range(SSM_GROUPS):
                        for j in range(GH // 2):
                            bank = m.to_dve.take(pe)
                            for e in range(2):
                                h = g * GH + 2 * j + e
                                mm = pe.matmul(bank[:, e * T:(e + 1) * T], view(st.ident[0:SSM_HEADS, h:h + 1], [[0, P]]),
                                               acs[:, :], start=True, stop=True)
                            m.to_dve.put(mm)
                        pe.wait_ge(mready, g + 1)
                        for lt in range(TT):
                            bank = m.to_dve.take(pe)
                            for h in range(GH):
                                for s in range(lt + 1):
                                    lhs = M[:, h, lt * P:(lt + 1) * P] if s == 0 else M[:, h, T:T + P]
                                    c = (g * GH + h) * DH
                                    mm = pe.matmul(bank[:, h * DH:(h + 1) * DH], lhs, xr[:, s, c:c + DH],
                                                   start=(s == 0), stop=(s == lt))
                            m.to_dve.put(mm)

                @block.scalar
                def _(act):
                    for g in range(SSM_GROUPS):
                        act.wait_ge(seg, g + 1)
                        act.activation(M[:, :, :], M[:, :, :], ACT.Exp).then_inc(dec, 1)

                @block.vector
                def _(dve):
                    V = m.dve_chain.on(dve)
                    for g in range(SSM_GROUPS):
                        for j in range(GH // 2):
                            bank = m.to_dve.get(dve)
                            for e in range(2):
                                h = g * GH + 2 * j + e
                                dve.tensor_scalar(M[:, 2 * j + e, 0:T], bank[:, e * T:(e + 1) * T], acsc[:, 0, h:h + 1], 0.0,
                                                  ALU.subtract, ALU.min)
                                ins = dve.tensor_scalar(M[:, 2 * j + e, T:T + P], bank[:, e * T + P:(e + 1) * T],
                                                        acsc[:, 1, h:h + 1], 0.0, ALU.subtract, ALU.min)
                            m.to_dve.free(ins)
                        dve.drain().then_inc(seg, 1)
                        dve.wait_ge(dec, g + 1)
                        for j in range(GH):
                            h = g * GH + j
                            dve.scalar_tensor_tensor(out=M[:, j, 0:T], in0=M[:, j, 0:T], scalar=dtc[:, 0, h:h + 1],
                                                     in1=cb[:, g, 0, :], op0=ALU.mult, op1=ALU.mult)
                            dve.scalar_tensor_tensor(out=M[:, j, T:T + P], in0=M[:, j, T:T + P], scalar=dtc[:, 1, h:h + 1],
                                                     in1=cb[:, g, 1, P:T], op0=ALU.mult, op1=ALU.mult)
                        dve.drain().then_inc(mready, 1)
                        for lt in range(TT):
                            cols = slice(g * CHUNK, (g + 1) * CHUNK)
                            V(dve.tensor_tensor(view(y[:, lt, g * CHUNK:g * CHUNK + 1], [[DH, GH], [1, DH]]),
                                                view(xr[:, lt, g * CHUNK:g * CHUNK + 1], [[DH, GH], [1, DH]]),
                                                spread(dsk[:, g * GH:(g + 1) * GH], DH), ALU.mult))
                            bank = m.to_dve.get(dve)
                            m.to_dve.free(dve.tensor_tensor(y[:, lt, cols], bank[:, :], y[:, lt, cols], ALU.add))
                            V(dve.engine_nop())
                            V(dve.tensor_tensor(y[:, lt, cols], y[:, lt, cols],
                                                proj[:, lt, Z0 + g * CHUNK:Z0 + (g + 1) * CHUNK], ALU.mult))


def project_residual(nc, m, st, acts, w, gain=None):
    with ExitStack() as ctx:
        m.weights.split_memory(ctx)
        tmp = m.sb(ctx, "residual_tmp", [P, TT, CHUNK])
        if gain is not None:
            row = m.sb(ctx, "residual_gain", [P, D])
        gain_loaded = m.sem("residual_gain_loaded")
        st.gain_count += gain is not None
        with nc.Block() as block:
            @block.sync
            def _(sp):
                if gain is not None:
                    sp.dma_start(row[:, :], everywhere(gain, D)).then_inc(gain_loaded, 16)
                for c, size in chunks(D)[2:]:
                    m.weights.load(sp, w, c, size)

            @block.tensor
            def _(pe):
                for c, size in chunks(D):
                    m.weights.multiply_split(pe, acts, KD, size, m.to_dve)

            @block.scalar
            def _(act):
                for c, size in chunks(D):
                    m.weights.split_high(act, KD, size)

            @block.vector
            def _(dve):
                V = m.dve_chain.on(dve)
                if gain is not None:
                    dve.wait_ge(gain_loaded, 16 * st.gain_count)
                work = chunks(D)
                for i in range(len(work) + 1):
                    if i < len(work):
                        m.weights.split_low(dve, KD, work[i][1])
                    if i == 0:
                        continue
                    c, size = work[i - 1]
                    for tt in range(TT):
                        bank = m.to_dve.get(dve)
                        xs = st.x[:, tt, c:c + size]
                        if gain is None:
                            m.to_dve.free(dve.tensor_tensor(xs, bank[:, :], xs, ALU.add))
                            continue
                        m.to_dve.free(dve.tensor_tensor(tmp[:, tt, :], bank[:, :], row[:, c:c + size], ALU.mult))
                        V(dve.engine_nop())
                        dve.tensor_tensor(xs, xs, tmp[:, tt, :], ALU.add)


def norm_rows(nc, m, st, name, x, gain, store=None):
    with ExitStack() as ctx:
        squares = m.sb(ctx, f"{name}_squares", [P, D])
        row = m.sb(ctx, f"{name}_gain", [P, D])
        ms = m.sb(ctx, f"{name}_ms", [P, TT])
        rinv = m.sb(ctx, f"{name}_rinv", [P, TT])
        squared, mean_ready, root_ready = m.sem(f"{name}_squared"), m.sem(f"{name}_mean_ready"), m.sem(f"{name}_root_ready")
        row_loaded, stored, scaled = m.sem(f"{name}_gain_loaded"), m.sem(f"{name}_stored"), m.sem(f"{name}_rows_scaled")
        with nc.Block() as block:
            @block.sync
            def _(sp):
                sp.dma_start(row[:, :], everywhere(gain, D)).then_inc(row_loaded, 16)
                if store is not None:
                    for tt in range(TT):
                        sp.wait_ge(scaled, tt + 1)
                        sp.dma_start(store[0, tt * P:(tt + 1) * P, :], x[:, tt, :]).then_inc(stored, 16)
                    sp.wait_ge(stored, 16 * TT)

            @block.scalar
            def _(act):
                A = m.act_chain.on(act)
                for tt in range(TT):
                    A(act.activation(squares[:, :], x[:, tt, :], ACT.Square, accum_out=ms[:, tt:tt + 1]))
                act.drain().then_inc(squared, 1)
                act.wait_ge(mean_ready, 1)
                act.activation(rinv[:, :], ms[:, :], ACT.Sqrt).then_inc(root_ready, 1)

            @block.vector
            def _(dve):
                V = m.dve_chain.on(dve)
                dve.wait_ge(squared, 1)
                dve.tensor_scalar(ms[:, :], ms[:, :], 1.0 / D, EPS, ALU.mult, ALU.add).then_inc(mean_ready, 1)
                dve.wait_ge(root_ready, 1)
                V(dve.reciprocal(rinv[:, :], rinv[:, :]))
                dve.wait_ge(row_loaded, 16)
                for tt in range(TT):
                    dve.scalar_tensor_tensor(out=x[:, tt, :], in0=x[:, tt, :], scalar=rinv[:, tt:tt + 1], in1=row[:, :],
                                             op0=ALU.mult, op1=ALU.mult).then_inc(scaled, 1)



HK = PEER_HEADS * TOPK


def stage_choose(nc, m, io, st, acts, i1T, i2T, gateT):
    LISTS = 2 * PEER_HEADS
    with ExitStack() as ctx:
        sc = m.sb(ctx, "key_scores", [P, TT, LISTS, P])
        with ExitStack() as c1:
            q = m.sb(c1, "peer_q", [P, TT, D])
            qT = m.sb(c1, "peer_qT", [P, LISTS, T])
            sk = m.sb(c1, "subkeys", [P, 2, P])
            skT = m.sb(c1, "subkeys_T", [P, 2, P])
            project(nc, m, st, acts, KD, io["peer_wq"][0], 0, D, lambda tt, c, n: q[:, tt, c:c + n], loaded=2)
            sk_loaded, turned = m.sem("subkeys_loaded"), m.sem("peer_q_turned")
            with nc.Block() as block:
                @block.sync
                def _(sp):
                    sp.dma_start(sk[:, :, :], io["peer_subkeys"][0].rearrange("s k d -> k s d")).then_inc(sk_loaded, 16)

                @block.tensor
                def _(pe):
                    turn_to_columns(pe, m.to_dve, st.ident[:, :], lambda k, tt: q[:, tt, k * P:(k + 1) * P], LISTS)
                    pe.wait_ge(sk_loaded, 16)
                    bank = m.to_dve.take(pe)
                    for s in range(2):
                        mm = pe.transpose(bank[:, s * P:(s + 1) * P], sk[:, s, :], st.ident[:, :])
                    m.to_dve.put(mm)
                    pe.wait_ge(turned, 1)
                    for tt in range(TT):
                        for j in range(LISTS // 4):
                            bank = m.to_dve.take(pe)
                            for e in range(4):
                                mm = pe.matmul(bank[:, e * P:(e + 1) * P], qT[:, 4 * j + e, tt * P:(tt + 1) * P],
                                               skT[:, e % 2, :], start=True, stop=True)
                            m.to_dve.put(mm)

                @block.vector
                def _(dve):
                    for j in range(LISTS // 2):
                        bank = m.to_dve.get(dve)
                        m.to_dve.free(dve.tensor_copy(qT[:, 2 * j:2 * j + 2, :], bank[:, :]))
                    bank = m.to_dve.get(dve)
                    m.to_dve.free(dve.tensor_copy(skT[:, :, :], bank[:, 0:2 * P]))
                    dve.drain().then_inc(turned, 1)
                    for tt in range(TT):
                        for j in range(LISTS // 4):
                            bank = m.to_dve.get(dve)
                            m.to_dve.free(dve.tensor_copy(sc[:, tt, 4 * j:4 * j + 4, :], bank[:, :]))
        with ExitStack() as c2:
            vals = m.sb(c2, "key_best", [P, TT, LISTS, TOPK])
            idx = m.sb(c2, "key_index", [P, TT, LISTS, TOPK], U32)
            idxf = m.sb(c2, "key_index_f", [P, TT, LISTS, TOPK])
            cand = m.sb(c2, "candidates", [P, PEER_HEADS, TOPK * TOPK])
            best = m.sb(c2, "best", [P, TT, PEER_HEADS, TOPK])
            pos = m.sb(c2, "best_pos", [P, TT, PEER_HEADS, TOPK], U32)
            part = m.sb(c2, "pos_part", [P, TT, HK], U32)
            partf = m.sb(c2, "pos_part_f", [P, TT, HK])
            picks = m.sb(c2, "picks", [P, 3, TT, HK])
            hot = m.sb(c2, "rank_onehot", [P, HK, TOPK])
            tot = m.sb(c2, "gate_sums", [P, TT, PEER_HEADS])
            shifted, expd, ready = m.sem("best_shifted"), m.sem("best_exp"), m.sem("picks_ready")
            LOW = -3.0e38
            with nc.Block() as block:
                @block.vector
                def _(dve):
                    V = m.dve_chain.on(dve)

                    def top16(lists, v, ix):
                        for lo in (0, 8):
                            for i, src in enumerate(lists):
                                ins = dve.max(v(i)[:, lo:lo + 8], src)
                            V(ins)
                            for i, src in enumerate(lists):
                                ins = dve.max_index(ix(i)[:, lo:lo + 8], v(i)[:, lo:lo + 8], src)
                            V(ins)
                            if lo == 0:
                                for i, src in enumerate(lists):
                                    ins = dve.match_replace(src, v(i)[:, 0:8], src, LOW)
                                V(ins)

                    for tt in range(TT):
                        top16([sc[:, tt, i, :] for i in range(LISTS)], lambda i: vals[:, tt, i, :], lambda i: idx[:, tt, i, :])
                    V(dve.tensor_copy(idxf[:, :, :, :], idx[:, :, :, :]))
                    for tt in range(TT):
                        for h in range(PEER_HEADS):
                            ins = dve.tensor_tensor(cand[:, h, :].rearrange("p (a b) -> p a b", b=TOPK),
                                                    spread(vals[:, tt, 2 * h, :], TOPK),
                                                    view(vals[:, tt, 2 * h + 1, 0:1], [[0, TOPK], [1, TOPK]]), ALU.add)
                        V(ins)
                        top16([cand[:, h, :] for h in range(PEER_HEADS)], lambda h: best[:, tt, h, :], lambda h: pos[:, tt, h, :])
                    for half in range(2):
                        posv = pos[:, :, :, :].rearrange("p t h k -> p t (h k)")
                        if half == 0:
                            V(dve.tensor_scalar(part[:, :, :], posv, 4, None, ALU.logical_shift_right))
                        else:
                            V(dve.tensor_scalar(part[:, :, :], posv, TOPK - 1, None, ALU.bitwise_and))
                        V(dve.tensor_copy(partf[:, :, :], part[:, :, :]))
                        for tt in range(TT):
                            V(dve.tensor_tensor(hot[:, :, :], view(st.iota_row[:, 0:1], [[0, HK], [1, TOPK]]),
                                                spread(partf[:, tt, :], TOPK), ALU.is_equal))
                            keyv = view(idxf[:, tt, half, 0:1], [[2 * TOPK, PEER_HEADS], [0, TOPK], [1, TOPK]])
                            hotv = hot[:, :, :].rearrange("p (h k) a -> p h k a", k=TOPK)
                            V(dve.tensor_tensor(hotv, hotv, keyv, ALU.mult))
                            V(dve.tensor_reduce(picks[:, half, tt, :], hot[:, :, :], AX_X, ALU.add))
                    for tt in range(TT):
                        V(dve.tensor_copy(tot[:, tt, :], view(best[:, tt, 0, 0:1], [[TOPK, PEER_HEADS]])))
                        V(dve.tensor_tensor(best[:, tt, :, :], best[:, tt, :, :], spread(tot[:, tt, :], TOPK), ALU.subtract))
                    dve.drain().then_inc(shifted, 1)
                    dve.wait_ge(expd, 1)
                    V(dve.tensor_reduce(tot[:, :, :], best[:, :, :, :], AX_X, ALU.add))
                    V(dve.reciprocal(tot[:, :, :], tot[:, :, :]))
                    for tt in range(TT):
                        dve.tensor_tensor(picks[:, 2, tt, :].rearrange("p (h k) -> p h k", k=TOPK), best[:, tt, :, :],
                                          spread(tot[:, tt, :], TOPK), ALU.mult)
                    dve.drain().then_inc(ready, 1)
                    for dst in (i1T, i2T, gateT):
                        bank = m.to_dve.get(dve)
                        m.to_dve.free(dve.tensor_copy(dst[:, :], bank[:, 0:T]))

                @block.scalar
                def _(act):
                    act.wait_ge(shifted, 1)
                    act.activation(best[:, :, :, :], best[:, :, :, :], ACT.Exp).then_inc(expd, 1)

                @block.tensor
                def _(pe):
                    pe.wait_ge(ready, 1)
                    for i in range(3):
                        bank = m.to_dve.take(pe)
                        for tt in range(TT):
                            mm = pe.transpose(bank[:, tt * P:(tt + 1) * P], picks[:, i, tt, :], st.ident[:, :])
                        m.to_dve.put(mm)


def stage_experts(nc, m, io, st, acts):
    STEP = 4
    STEPS = EXPERTS_SIDE // STEP
    TOK = 8
    TB = 32
    GROUPS = TB // TOK
    gates_dram = m.dram("expert_gates", [T // TB, P, EXPERTS_SIDE, TB])
    y = st.x
    x_dram = m.dram("x_aside", [P, TT, D])
    x_aside = m.sem("x_aside")
    with ExitStack() as c1:
        i1T, i2T, gateT = (m.sb(c1, n, [P, T]) for n in ("i1_cols", "i2_cols", "gate_cols"))
        with ExitStack() as c2:
            m.weights.memory(c2)
            norm_to_columns(nc, m, st, "norm2", st.x, D, acts, lambda j: st.gain2[:, j:j + 1],
                            lambda j: st.mod_cols[:, 48 + j:49 + j], ahead=first_chunks(io["peer_wq"][0]))
            stage_choose(nc, m, io, st, acts, i1T, i2T, gateT)
        hot2 = m.sb(c1, "onehot_i2", [P, 2, TOK, P])
        hot1 = m.sb(c1, "onehot_i1", [P, 2, TOK, P])
        block_gates = m.sb(c1, "block_gates", [P, 2, EXPERTS_SIDE, TB])
        mod = ModulationParts(m, io, st, c1, "mod_last", (5,))
        hot_ready, hot_used = m.sem("onehots_ready"), [m.sem(f"onehots_used{b}") for b in range(2)]
        gates_ready, stored = m.sem("block_gates_ready"), [m.sem(f"block_gates_stored{b}") for b in range(2)]
        with nc.Block() as block:
            @block.sync
            def _(sp):
                sp.dma_start(x_dram, st.x[:, :, :]).then_inc(x_aside, 16)
                with sp.Fori(0, T // TB // 2) as i:
                    for b in range(2):
                        sp.wait_ge(gates_ready, 2 * i + b + 1)
                        sp.dma_start(gates_dram[bass.ds(2 * i + b, 1)].rearrange("b p e t -> p (b e) t"),
                                     block_gates[:, b, :, :]).then_inc(stored[b], 16)
                for b in range(2):
                    sp.wait_ge(stored[b], 16 * (T // TB // 2 + 1))
                mod.row_store(sp, 5)

            @block.gpsimd
            def _(pool):
                mod.on_pool(pool)

            @block.vector
            def _(dve):
                V = m.dve_chain.on(dve)
                with dve.Fori(0, T // TB // 2) as i:
                    V.enter(i, 4 * GROUPS)
                    for q in range(2 * GROUPS):
                        b = q % 2
                        tok = i * 2 * TB + q * TOK
                        dve.wait_ge(hot_used[b], i * GROUPS + q // 2 + 1)
                        V(dve.tensor_tensor(hot1[:, b, :, :], view(st.iota_row[:, 0:1], [[0, TOK], [1, P]]),
                                            spread(i1T[:, bass.ds(tok, TOK)], P), ALU.is_equal))
                        V(dve.tensor_tensor(hot1[:, b, :, :], hot1[:, b, :, :],
                                            spread(gateT[:, bass.ds(tok, TOK)], P), ALU.mult))
                        dve.tensor_tensor(hot2[:, b, :, :], view(st.iota_row[:, 0:1], [[0, TOK], [1, P]]),
                                          spread(i2T[:, bass.ds(tok, TOK)], P), ALU.is_equal).then_inc(hot_ready, 1)
                V.leave(T // TB // 2)
                dve.wait_ge(x_aside, 16)
                V(dve.memset(y[:, :, :], 0.0))
                for _n in range(mod.tiles):
                    mod.add_tile(dve)
                mod.add_bias(dve)
                mod.row_dve(dve)

            @block.tensor
            def _(pe):
                with pe.Fori(0, T // TB // 2) as i:
                    m.to_act.enter_fill(i, 4 * GROUPS)
                    for q in range(2 * GROUPS):
                        pe.wait_ge(hot_ready, i * 2 * GROUPS + q + 1)
                        for half in range(2):
                            bank = m.to_act.take(pe)
                            for e in range(TOK // 2):
                                t = half * TOK // 2 + e
                                mm = pe.matmul(bank[:, e * P:(e + 1) * P], hot2[:, q % 2, t, :], hot1[:, q % 2, t, :],
                                               start=True, stop=True)
                            m.to_act.put(mm)
                m.to_act.leave_fill(T // TB // 2, 4 * GROUPS)
                mod.on_pe(pe)
                mod.on_pe(pe)
                mod.row_pe(pe, 5)

            @block.scalar
            def _(act):
                for b in range(2):
                    act.drain().then_inc(hot_used[b], 1)
                    act.drain().then_inc(stored[b], 16)
                with act.Fori(0, T // TB // 2) as i:
                    m.to_act.enter_empty(i, 4 * GROUPS)
                    for b in range(2):
                        act.wait_ge(stored[b], 16 * (i + 1))
                        for q in range(GROUPS):
                            for half in range(2):
                                bank = m.to_act.get(act)
                                t0 = q * TOK + half * TOK // 2
                                m.to_act.free(act.activation(block_gates[:, b, :, t0:t0 + TOK // 2].rearrange("p e t -> p t e"),
                                                             bank[:, :].rearrange("p (t e) -> p t e", e=P), ACT.Copy))
                            act.drain().then_inc(hot_used[q % 2], 1)
                        act.drain().then_inc(gates_ready, 1)
                m.to_act.leave_empty(T // TB // 2, 4 * GROUPS)
                mod.on_act(act)
                mod.on_act(act)
    with ExitStack() as c2:
        act_sb = m.sb(c2, "expert_act", [P, STEP, T])
        ah, al = (m.sb(c2, f"expert_act_{s}", [P, STEP, T], F32R) for s in ("high", "low"))
        g_sb = m.sb(c2, "step_gates", [P, T // TB, STEP * TB])
        u_sb, v_sb = m.sb(c2, "expert_u", [P, 2, D]), m.sb(c2, "expert_v", [P, 2, D])
        uh, ul = (m.sb(c2, f"expert_u_T_{s}", [P, 2, KD, P], F32R) for s in ("high", "low"))
        vh, vl = (m.sb(c2, f"expert_v_{s}", [P, STEP, D], F32R) for s in ("high", "low"))
        u_loaded, v_loaded = ([m.sem(f"{s}_loaded{b}") for b in range(2)] for s in "uv")
        g_loaded, uh_ready, vh_ready, act_ready = (m.sem("expert_" + s) for s in ("gates_loaded", "u_high_ready", "v_high_ready", "act_ready"))
        u_split, v_split, g_used, gated, y_added = (m.sem("expert_" + s) for s in ("u_split", "v_split", "gates_used", "gated", "sum_added"))
        START = {u_split: 2, v_split: 2, g_used: 1, gated: STEP, y_added: 2}
        fill0 = m.to_act.of + m.to_act.nf
        with nc.Block() as block:
            @block.sync
            def _(sp):
                with sp.Fori(0, STEPS) as i:
                    for t in range(STEP):
                        n = i * STEP + t
                        sp.wait_ge(u_split, n - 2 + 1 + START[u_split])
                        sp.dma_start(u_sb[:, t % 2, :], io["peer_u"][0, bass.ds(n * P, P), :]).then_inc(u_loaded[t % 2], 16)
                        if t == 1:
                            sp.wait_ge(g_used, i + START[g_used])
                            sp.dma_start(g_sb[:, :, :], gates_dram[:, :, bass.ds(i * STEP, STEP), :].rearrange("b p e t -> p b (e t)"))\
                              .then_inc(g_loaded, 16)

            @block.gpsimd
            def _(pool):
                with pool.Fori(0, STEPS) as i:
                    for t in range(STEP):
                        n = i * STEP + t
                        pool.wait_ge(v_split, n - 2 + 1 + START[v_split])
                        pool.dma_start(v_sb[:, t % 2, :], io["peer_v"][0, bass.ds(n * P, P), :]).then_inc(v_loaded[t % 2], 16)

            @block.tensor
            def _(pe):
                def turn(i, t):
                    pe.wait_ge(u_loaded[t % 2], 16 * (2 * i + t // 2 + 1))
                    for j in range(4):
                        bank = m.to_act.take(pe)
                        for e in range(4):
                            k = 4 * j + e
                            mm = pe.transpose(bank[:, e * P:(e + 1) * P], u_sb[:, t % 2, k * P:(k + 1) * P], st.ident[:, :])
                        m.to_act.put(mm)

                def scores(i, t):
                    pe.wait_ge(u_split, i * STEP + t + 1 + START[u_split])
                    bank = m.to_act.take(pe)
                    for k in range(KD):
                        o = bank[:, 0:T]
                        pe.matmul(o, uh[:, t % 2, k, :], acts.h[:, k, :], start=(k == 0), stop=False)
                        pe.matmul(o, uh[:, t % 2, k, :], acts.l[:, k, :], start=False, stop=False)
                        mm = pe.matmul(o, ul[:, t % 2, k, :], acts.h[:, k, :], start=False, stop=(k == KD - 1))
                    m.to_act.put(mm)

                def sums(i, pair):
                    pe.wait_ge(v_split, i * STEP + 2 * pair + 2 + START[v_split])
                    pe.wait_ge(gated, i * STEP + 2 * pair + 2 + START[gated])
                    for tt in range(TT):
                        tok = slice(tt * P, (tt + 1) * P)
                        for c in range(4):
                            bank = m.to_dve.take(pe)
                            cs = slice(c * CHUNK, (c + 1) * CHUNK)
                            for t in (2 * pair, 2 * pair + 1):
                                pe.matmul(bank[:, :], ah[:, t, tok], vh[:, t, cs], start=(t % 2 == 0), stop=False)
                                pe.matmul(bank[:, :], ah[:, t, tok], vl[:, t, cs], start=False, stop=False)
                                mm = pe.matmul(bank[:, :], al[:, t, tok], vh[:, t, cs], start=False, stop=(t % 2 == 1))
                            m.to_dve.put(mm)

                with pe.Fori(0, STEPS) as i:
                    m.to_act.enter_fill(i, 20)
                    m.to_dve.enter_fill(i, 16)
                    turn(i, 0)
                    turn(i, 1)
                    scores(i, 0)
                    turn(i, 2)
                    scores(i, 1)
                    turn(i, 3)
                    scores(i, 2)
                    scores(i, 3)
                    sums(i, 0)
                    sums(i, 1)
                m.to_act.leave_fill(STEPS, 20)
                m.to_dve.leave_fill(STEPS, 16)

            @block.scalar
            def _(act):
                def u_high(i, t):
                    for j in range(4):
                        bank = m.to_act.get(act)
                        act.activation(uh[:, t % 2, 4 * j:4 * j + 4, :], bank[:, :], ACT.Copy).then_inc(uh_ready, 1)
                        m.to_act.passed_on()

                def v_high(i, t):
                    act.wait_ge(v_loaded[t % 2], 16 * (2 * i + t // 2 + 1))
                    act.wait_ge(y_added, 2 * (i - 1) + t // 2 + 1 + START[y_added])
                    act.activation(vh[:, t, :], v_sb[:, t % 2, :], ACT.Copy).then_inc(vh_ready, 1)

                def gelu(i, t):
                    act.wait_ge(u_split, i * STEP + min(t + 2, STEP) + START[u_split])
                    act.wait_ge(gated, (i - 1) * STEP + t + 1 + START[gated])
                    bank = m.to_act.get(act)
                    m.to_act.free(act.activation(act_sb[:, t, :], bank[:, 0:T], ACT.Gelu_apprx_tanh))
                    act.drain().then_inc(act_ready, 1)

                A = m.act_chain.on(act)
                A(act.activation(act_sb[:, 0, 0:1], st.ident[:, 0:1], ACT.Gelu_apprx_tanh))
                with act.Fori(0, STEPS) as i:
                    m.to_act.enter_empty(i, 20)
                    u_high(i, 0)
                    u_high(i, 1)
                    gelu(i, 0)
                    u_high(i, 2)
                    v_high(i, 0)
                    gelu(i, 1)
                    u_high(i, 3)
                    v_high(i, 1)
                    gelu(i, 2)
                    v_high(i, 2)
                    v_high(i, 3)
                    gelu(i, 3)
                m.to_act.leave_empty(STEPS, 20)

            @block.vector
            def _(dve):
                V = m.dve_chain.on(dve)

                def u_low(i, t):
                    for j in range(4):
                        dve.wait_ge(uh_ready, 4 * (i * STEP + t) + j + 1)
                        bank = m.to_act.banks[(fill0 + 4 * t + j + max(t - 1, 0)) % 4]
                        o = slice(4 * j, 4 * j + 4)
                        dve.tensor_tensor(ul[:, t % 2, o, :], bank[:, :].rearrange("p (k e) -> p k e", e=P),
                                          uh[:, t % 2, o, :], ALU.subtract).then_inc(m.to_act.emptied, 1)
                    dve.drain().then_inc(u_split, 1)

                def v_low(i, t):
                    dve.wait_ge(vh_ready, i * STEP + t + 1)
                    dve.tensor_tensor(vl[:, t, :], v_sb[:, t % 2, :], vh[:, t, :], ALU.subtract).then_inc(v_split, 1)

                def gate(i, t):
                    dve.wait_ge(act_ready, i * STEP + t + 1)
                    if t == 0:
                        dve.wait_ge(g_loaded, 16 * (i + 1))
                    a = act_sb[:, t, :]
                    V(dve.tensor_tensor(a.rearrange("p (b k) -> p b k", k=TB), a.rearrange("p (b k) -> p b k", k=TB),
                                        g_sb[:, :, t * TB:(t + 1) * TB], ALU.mult))
                    V(dve.tensor_copy(ah[:, t, :], a))
                    dve.tensor_tensor(al[:, t, :], a, ah[:, t, :], ALU.subtract).then_inc(gated, 1)
                    if t == STEP - 1:
                        dve.drain().then_inc(g_used, 1)

                def add(i, pair):
                    dve.wait_ge(y_added, 2 * i + pair + START[y_added])
                    for tt in range(TT):
                        for c in range(4):
                            bank = m.to_dve.get(dve)
                            part = y[:, tt, c * CHUNK:(c + 1) * CHUNK]
                            m.to_dve.free(dve.tensor_tensor(part, bank[:, :], part, ALU.add))
                    dve.drain().then_inc(y_added, 1)

                for sem, ahead in START.items():
                    dve.drain().then_inc(sem, ahead)
                with dve.Fori(0, STEPS) as i:
                    V.enter(i, 2 * STEP)
                    m.to_dve.enter_empty(i, 16)
                    u_low(i, 0)
                    u_low(i, 1)
                    u_low(i, 2)
                    gate(i, 0)
                    v_low(i, 0)
                    gate(i, 1)
                    u_low(i, 3)
                    v_low(i, 1)
                    gate(i, 2)
                    v_low(i, 2)
                    v_low(i, 3)
                    gate(i, 3)
                    add(i, 0)
                    add(i, 1)
                V.leave(STEPS)
                m.to_dve.leave_empty(STEPS, 16)
    with ExitStack() as c3:
        row = m.sb(c3, "g2_row", [P, D])
        x_back = m.sb(c3, "x_back", [P, TT, D])
        loaded = m.sem("g2_loaded")
        with nc.Block() as block:
            @block.sync
            def _(sp):
                sp.dma_start(row[:, :], everywhere(st.mod_dram[5 * D:6 * D], D)).then_inc(loaded, 16)
                sp.dma_start(x_back[:, :, :], x_dram).then_inc(loaded, 16)

            @block.vector
            def _(dve):
                V = m.dve_chain.on(dve)
                dve.wait_ge(loaded, 32)
                for tt in range(TT):
                    V(dve.tensor_tensor(y[:, tt, :], y[:, tt, :], row[:, :], ALU.mult))
                    V(dve.tensor_tensor(y[:, tt, :], x_back[:, tt, :], y[:, tt, :], ALU.add))



UNITS = 8


class Inverse:

    def __init__(self, m, st, name, levels, AT, Tm, TT_, X, M):
        self.m, self.st, self.levels = m, st, levels
        self.AT, self.T, self.TT, self.X, self.M = AT, Tm, TT_, X, M
        self.first, self.mask, self.x = m.sem(f"{name}_first_ready"), m.sem(f"{name}_level_masked"), m.sem(f"{name}_x_ready")
        self.t, self.ready = m.sem(f"{name}_t_updated"), m.sem(f"{name}_a_ready")
        self.n = 0

    @staticmethod
    def h(a, half):
        return a[:, 4 * half:4 * half + 4, :]

    def bank3(self, bank):
        return bank[:, :].rearrange("p (u t) -> p u t", t=P)

    def level(self, lv):
        return view(self.st.level[:, lv, 0:1], [[0, 4], [1, P]])

    def on_pool(self, pool):
        pool.wait_ge(self.ready, self.n + 1)
        for lv in range(1, self.levels):
            for half in range(2):
                pool.wait_ge(self.x, 2 * ((self.levels - 1) * self.n + lv - 1) + half)
                pool.tensor_tensor(self.h(self.M, half), self.h(self.AT, half), self.level(lv), ALU.mult)\
                    .then_inc(self.mask, 1)

    def on_pe(self, pe):
        m, base = self.m, 2 * (self.levels - 1) * self.n
        pe.wait_ge(self.first, self.n + 1)
        for half in range(2):
            bank = m.to_dve.take(pe)
            for u in range(4):
                mm = pe.transpose(bank[:, u * P:(u + 1) * P], self.TT[:, 4 * half + u, :], self.st.ident[:, :])
            m.to_dve.put(mm)
        for lv in range(1, self.levels):
            last = lv == self.levels - 1
            for half in range(2):
                n = base + 2 * (lv - 1) + half
                pe.wait_ge(self.mask, n + 1)
                pe.wait_ge(self.t, n + 2 * self.n + 1)
                bank = m.to_act.take(pe)
                for u in range(4 * half, 4 * half + 4):
                    mm = pe.matmul(bank[:, (u % 4) * P:(u % 4 + 1) * P], self.M[:, u, :], self.T[:, u, :], start=True, stop=True)
                m.to_act.put(mm)
            for half in range(2):
                n = base + 2 * (lv - 1) + half
                pe.wait_ge(self.x, n + 1)
                if not last:
                    bank = m.to_dve.take(pe)
                    for u in range(4 * half, 4 * half + 4):
                        mm = pe.matmul(bank[:, (u % 4) * P:(u % 4 + 1) * P], self.TT[:, u, :], self.X[:, u, :], start=True, stop=True)
                    m.to_dve.put(mm)
                bank = m.to_dve.take(pe)
                for u in range(4 * half, 4 * half + 4):
                    mm = pe.matmul(bank[:, (u % 4) * P:(u % 4 + 1) * P], self.X[:, u, :], self.TT[:, u, :], start=True, stop=True)
                m.to_dve.put(mm)

    def on_act(self, act):
        for lv in range(1, self.levels):
            for half in range(2):
                bank = self.m.to_act.get(act)
                self.m.to_act.free(act.activation(self.h(self.X, half), self.bank3(bank), ACT.Copy))
                act.drain().then_inc(self.x, 1)

    def on_dve(self, dve, V):
        m = self.m
        dve.drain().then_inc(self.ready, 1)
        for half in range(2):
            V(dve.tensor_tensor(self.h(self.TT, half), self.h(self.AT, half), self.level(0), ALU.mult))
            V(dve.tensor_tensor(self.h(self.TT, half), view(self.st.ident[:, 0:1], [[0, 4], [1, P]]),
                                self.h(self.TT, half), ALU.subtract))
        dve.drain().then_inc(self.first, 1)
        for half in range(2):
            bank = m.to_dve.get(dve)
            m.to_dve.free(dve.tensor_copy(self.h(self.T, half), self.bank3(bank)))
            dve.drain().then_inc(self.t, 1)
        for lv in range(1, self.levels):
            last = lv == self.levels - 1
            for half in range(2):
                for dst in ((self.TT,) if last else (self.T, self.TT)):
                    bank = m.to_dve.get(dve)
                    if dst is self.T:
                        ins = dve.tensor_tensor(self.h(self.T, half), self.h(self.T, half), self.bank3(bank), ALU.subtract)
                    else:
                        ins = dve.tensor_tensor(self.h(self.TT, half), self.h(self.TT, half), self.bank3(bank), ALU.subtract)
                    m.to_dve.free(ins)
                dve.drain().then_inc(self.t, 1)
        dve.wait_ge(self.t, 2 * self.levels * (self.n + 1))


def arrays_of(buf, n, shape):
    size = int(np.prod(shape))
    flat_buf = buf[:, :, :].rearrange("p k n -> p (k n)")
    names = "abcd"[:len(shape)]
    out = []
    for i in range(n):
        a = flat_buf[:, i * size:(i + 1) * size]
        if len(shape) > 1:
            a = a.rearrange(f"p ({' '.join(names)}) -> p {' '.join(names)}", **{c: s for c, s in zip(names[1:], shape[1:])})
        out.append(a)
    return out



GH, GD = 8, 128


def stage_gdn(nc, m, io, st, acts, cols):
    with ExitStack() as ctx:
        NP_ = RF0
        pr = m.sb(ctx, "gdn_rows", [P, TT, NP_])
        project(nc, m, st, acts, KD, io["w_in_2"][0], GQKV0, NP_, lambda tt, c, n: pr[:, tt, c:c + n],
                loaded=2)
        beta = m.sb(ctx, "gdn_beta", [P, TT, GH])
        gcum = m.sb(ctx, "gdn_gcum", [GH, T])
        gcol = m.sb(ctx, "gdn_gcol", [P, TT, GH])
        egcol = m.sb(ctx, "gdn_exp_gcol", [P, TT, GH])
        gl = m.sb(ctx, "gdn_g_last", [P, GH])
        nw = m.sb(ctx, "gdn_norm_row", [P, GD])
        ss = m.sb(ctx, "gdn_square_sums", [P, TT, 2 * GH])
        with ExitStack() as c1:
            u = m.sb(c1, "gdn_padded", [P, GH, T + CONV_TAPS - 1])
            cv = m.sb(c1, "gdn_conv", [P, GH, T])
            sp_ = Softplus(m, c1, "gdn", GH)
            g = m.sb(c1, "gdn_g", [GH, T])
            ones = m.sb(c1, "gdn_ones", [GH, T])
            bias, alog = m.sb(c1, "gdn_bias_col", [GH, 1]), m.sb(c1, "gdn_a_log_col", [GH, 1])
            loaded, exp_a, summed, silu = m.sem("gdn_small_loaded"), m.sem("gdn_exp_a"), m.sem("gdn_conv_summed"), m.sem("gdn_conv_done")
            gready, col_ready = m.sem("gdn_gcum_ready"), m.sem("gdn_gcol_ready")
            squared, ss_ready, root = m.sem("gdn_squared"), m.sem("gdn_ss_ready"), m.sem("gdn_root_ready")
            sq = arrays_of(m.weights.buf[0], 2, [2 * GH, GD])
            with nc.Block() as block:
                @block.sync
                def _(sp):
                    sp.dma_start(bias[:, :], io["gdn_dt_bias_2"].rearrange("a h -> h a")).then_inc(loaded, 16)
                    sp.dma_start(alog[:, :], io["gdn_a_log_2"].rearrange("a h -> h a")).then_inc(loaded, 16)
                    sp.dma_start(nw[:, :], everywhere(io["gdn_norm_w_2"], GD)).then_inc(loaded, 16)
                    sp.wait_ge(loaded, 48)

                @block.tensor
                def _(pe):
                    bank = m.to_dve.take(pe)
                    for tt in range(TT):
                        mm = pe.transpose(bank[0:GH, tt * P:(tt + 1) * P], pr[:, tt, GA0:GA0 + GH], st.ident[:, :])
                    m.to_dve.put(mm)
                    for part in range(3):
                        turn_to_columns(pe, m.to_dve, st.ident[:, :],
                                        lambda k, tt: pr[:, tt, (part * GH + k) * P:(part * GH + k + 1) * P], GH)
                        pe.wait_ge(silu, part + 1)
                        turn_to_rows(pe, m.to_dve, st.ident[:, :], lambda k, tt: cv[:, k, tt * P:(tt + 1) * P], GH)
                    pe.wait_ge(gready, 1)
                    bank = m.to_dve.take(pe)
                    for tt in range(TT):
                        mm = pe.transpose(bank[:, tt * GH:(tt + 1) * GH], gcum[:, tt * P:(tt + 1) * P], st.ident[0:GH, 0:GH])
                    m.to_dve.put(mm)

                @block.scalar
                def _(act):
                    sp_.on_act(act)
                    act.wait_ge(loaded, 48)
                    act.activation(alog[:, :], alog[:, :], ACT.Exp).then_inc(exp_a, 1)
                    act.activation(beta[:, :, :], pr[:, :, GB0:GB0 + GH], ACT.Sigmoid)
                    act.activation(pr[:, :, GZ0:GZ0 + HALF], pr[:, :, GZ0:GZ0 + HALF], ACT.Silu)
                    for part in range(3):
                        act.wait_ge(summed, part + 1)
                        act.activation(cv[:, :, :], cv[:, :, :], ACT.Silu).then_inc(silu, 1)
                    act.wait_ge(col_ready, 1)
                    act.activation(egcol[:, :, :], gcol[:, :, :], ACT.Exp)
                    for tt in range(TT):
                        act.activation(sq[tt], pr[:, tt, 0:2 * HALF].rearrange("p (h d) -> p h d", d=GD), ACT.Square)
                    act.drain().then_inc(squared, 1)
                    act.wait_ge(ss_ready, 1)
                    act.activation(ss[:, :, :], ss[:, :, :], ACT.Sqrt).then_inc(root, 1)

                @block.vector
                def _(dve):
                    V = m.dve_chain.on(dve)
                    V(dve.memset(u[:, :, 0:CONV_TAPS - 1], 0.0))
                    V(dve.memset(ones[:, :], 1.0))
                    dve.wait_ge(loaded, 48)
                    bank = m.to_dve.get(dve)
                    m.to_dve.free(dve.tensor_scalar(sp_.x[:, :], bank[0:GH, 0:T], bias[:, 0:1], None, ALU.add))
                    V(dve.engine_nop())
                    sp_.on_dve(dve, V, g[:, :])
                    dve.wait_ge(exp_a, 1)
                    V(dve.tensor_scalar(g[:, :], g[:, :], alog[:, 0:1], -1.0, ALU.mult, ALU.mult))
                    for tt in range(TT):
                        V(dve.tensor_tensor_scan(gcum[:, tt * P:(tt + 1) * P], ones[:, 0:P], g[:, tt * P:(tt + 1) * P],
                                                 0.0, ALU.mult, ALU.add))
                    dve.drain().then_inc(gready, 1)
                    for part in range(3):
                        for j in range(GH // 2):
                            bank = m.to_dve.get(dve)
                            m.to_dve.free(dve.tensor_copy(u[:, 2 * j:2 * j + 2, CONV_TAPS - 1:], view(bank[:, 0:1], [[T, 2], [1, T]])))
                        V(dve.engine_nop())
                        nt = 3 * GH
                        causal_conv(dve, V, u, cv, GH, lambda j, k: st.vec.col("gdn_conv_w_2", j * nt + part * GH + k),
                                    lambda k, src: dve.tensor_scalar(cv[:, k, :], src,
                                                                     st.vec.col("gdn_conv_w_2", (CONV_TAPS - 1) * nt + part * GH + k),
                                                                     None, ALU.mult))
                        dve.drain().then_inc(summed, 1)
                        for tt in range(TT):
                            for k in range(2):
                                bank = m.to_dve.get(dve)
                                c = part * HALF + k * CHUNK
                                m.to_dve.free(dve.tensor_copy(pr[:, tt, c:c + CHUNK], bank[:, :]))
                    bank = m.to_dve.get(dve)
                    m.to_dve.free(dve.tensor_copy(gcol[:, :, :], bank[:, 0:TT * GH]))
                    dve.drain().then_inc(col_ready, 1)
                    dve.wait_ge(squared, 1)
                    for tt in range(TT):
                        V(dve.tensor_reduce(ss[:, tt, :], sq[tt], AX_X, ALU.add))
                    V(dve.tensor_scalar(ss[:, :, :], ss[:, :, :], EPS, None, ALU.add))
                    dve.drain().then_inc(ss_ready, 1)
                    dve.wait_ge(root, 1)
                    V(dve.reciprocal(ss[:, :, :], ss[:, :, :]))
                    V(dve.tensor_scalar(ss[:, :, 0:GH], ss[:, :, 0:GH], GD ** -0.5, None, ALU.mult))
                    for tt in range(TT):
                        qk = pr[:, tt, 0:2 * HALF].rearrange("p (h d) -> p h d", d=GD)
                        V(dve.tensor_tensor(qk, qk, spread(ss[:, tt, :], GD), ALU.mult))

        def part_rows(i, tt):
            return pr[:, tt, i * HALF:(i + 1) * HALF].rearrange("p (h d) -> p h d", d=GD)

        with ExitStack() as c2:
            kb = m.sb(c2, "gdn_k_beta", [P, TT, GH, GD])
            kbg = m.sb(c2, "gdn_k_beta_decayed", [P, GH, GD])
            qd = m.sb(c2, "gdn_q_decayed", [P, GH, GD])
            kd = m.sb(c2, "gdn_k_decayed", [P, GH, GD])
            S = m.sb(c2, "gdn_state", [P, GH, GD])
            kT, kbT, qT, qdT, E, AT, QT, Tm = arrays_of(m.weights.buf[0], 8, [GH, GD])
            TT_, X, M, wT, un, sq2 = arrays_of(m.weights.buf[1], 6, [GH, GD])
            inv = Inverse(m, st, "gdn", 7, AT, Tm, TT_, X, M)
            rows_ready, seg, dec, cols_ready = m.sem("gdn_rows_ready"), m.sem("gdn_seg_ready"), m.sem("gdn_dec_ready"), m.sem("gdn_cols_ready")
            kq_ready, kd_sub, kd_exp, kd_ready = m.sem("gdn_kq_masked"), m.sem("gdn_kd_sub"), m.sem("gdn_kd_exp"), m.sem("gdn_kd_ready")
            tt_ready, u_ready, vn_ready, s_ready, w_ready = (m.sem("gdn_" + s) for s in ("tt_ready", "u_ready", "vn_ready", "s_ready", "w_ready"))
            o_ready, o_sq, o_ms, o_root, o_done = (m.sem("gdn_o_" + s) for s in ("ready", "squared", "ms", "root", "done"))
            with nc.Block() as block:
                @block.gpsimd
                def _(pool):
                    for c in range(TT):
                        inv.n = c
                        inv.on_pool(pool)

                @block.scalar
                def _(act):
                    for c in range(TT):
                        inv.n = c
                        act.wait_ge(seg, c + 1)
                        act.activation(E, E, ACT.Exp).then_inc(dec, 1)
                        if c == 0:
                            act.wait_ge(kd_sub, 1)
                            act.activation(gl[:, :], gl[:, :], ACT.Exp).then_inc(kd_exp, 1)
                        inv.on_act(act)
                    for tt in range(TT):
                        act.wait_ge(o_ready, tt + 1)
                        act.activation(sq2, part_rows(2, tt), ACT.Square).then_inc(o_sq, 1)
                        act.wait_ge(o_ms, tt + 1)
                        act.activation(ss[:, tt, 0:GH], ss[:, tt, 0:GH], ACT.Sqrt).then_inc(o_root, 1)

                @block.tensor
                def _(pe):
                    pe.wait_ge(rows_ready, 1)
                    for c in range(TT):
                        inv.n = c
                        srcs = [part_rows(1, c), kb[:, c, :, :], part_rows(0, c)] + ([qd[:, :, :]] if c else [])
                        for half in range(2):
                            for src in srcs:
                                bank = m.to_dve.take(pe)
                                for e in range(4):
                                    mm = pe.transpose(bank[:, e * P:(e + 1) * P], src[:, 4 * half + e, :], st.ident[:, :])
                                m.to_dve.put(mm)
                            bank = m.to_dve.take(pe)
                            for e in range(4):
                                h = 4 * half + e
                                mm = pe.matmul(bank[:, e * P:(e + 1) * P], view(st.ident[0:GH, h:h + 1], [[0, P]]),
                                               gcum[:, c * P:(c + 1) * P], start=True, stop=True)
                            m.to_dve.put(mm)
                        pe.wait_ge(cols_ready, c + 1)
                        for rhs in (kbT, qT):
                            for half in range(2):
                                bank = m.to_dve.take(pe)
                                for e in range(4):
                                    h = 4 * half + e
                                    mm = pe.matmul(bank[:, e * P:(e + 1) * P], kT[:, h, :], rhs[:, h, :], start=True, stop=True)
                                m.to_dve.put(mm)
                        inv.on_pe(pe)
                        pe.wait_ge(tt_ready, c + 1)

                        def per_head(fn):
                            for half in range(2):
                                bank = m.to_dve.take(pe)
                                for e in range(4):
                                    ins = fn(4 * half + e, bank[:, e * P:(e + 1) * P])
                                m.to_dve.put(ins)

                        v = part_rows(2, c)
                        per_head(lambda h, o: pe.matmul(o, TT_[:, h, :], v[:, h, :], start=True, stop=True))
                        if c:
                            per_head(lambda h, o: pe.matmul(o, kbg[:, h, :], TT_[:, h, :], start=True, stop=True))
                            pe.wait_ge(w_ready, 1)
                            per_head(lambda h, o: pe.matmul(o, wT[:, h, :], S[:, h, :], start=True, stop=True))
                        pe.wait_ge(vn_ready, c + 1)
                        if c == 0:
                            per_head(lambda h, o: pe.matmul(o, QT[:, h, :], un[:, h, :], start=True, stop=True))
                            pe.wait_ge(kd_ready, 1)
                            per_head(lambda h, o: pe.matmul(o, kd[:, h, :], un[:, h, :], start=True, stop=True))
                        else:
                            def out(h, o):
                                pe.matmul(o, qdT[:, h, :], S[:, h, :], start=True, stop=False)
                                return pe.matmul(o, QT[:, h, :], un[:, h, :], start=False, stop=True)
                            per_head(out)
                    pe.wait_ge(o_done, 1)
                    turn_to_columns(pe, m.to_dve, st.ident[:, :], lambda k, tt: part_rows(2, tt)[:, k, :], GH)

                @block.vector
                def _(dve):
                    V = m.dve_chain.on(dve)
                    for tt in range(TT):
                        dve.tensor_tensor(kb[:, tt, :, :], part_rows(1, tt), spread(beta[:, tt, :], GD), ALU.mult)
                        V(dve.tensor_tensor(part_rows(2, tt), part_rows(2, tt), spread(beta[:, tt, :], GD), ALU.mult))
                    V(dve.tensor_tensor(kbg[:, :, :], kb[:, 1, :, :], spread(egcol[:, 1, :], GD), ALU.mult))
                    V(dve.tensor_tensor(qd[:, :, :], part_rows(0, 1), spread(egcol[:, 1, :], GD), ALU.mult))
                    dve.drain().then_inc(rows_ready, 1)
                    for c in range(TT):
                        inv.n = c
                        h4 = inv.h
                        for half in range(2):
                            for dst in [kT, kbT, qT] + ([qdT] if c else []):
                                bank = m.to_dve.get(dve)
                                m.to_dve.free(dve.tensor_copy(h4(dst, half), inv.bank3(bank)))
                            bank = m.to_dve.get(dve)
                            if c == 0:
                                dve.tensor_copy(gl[:, 4 * half:4 * half + 4], view(bank[:, 0:1], [[P, 4]], P - 1))
                            for e in range(4):
                                h = 4 * half + e
                                ins = dve.tensor_scalar(E[:, h, :], bank[:, e * P:(e + 1) * P], gcol[:, c, h:h + 1], 0.0,
                                                        ALU.subtract, ALU.min)
                            m.to_dve.free(ins)
                        dve.drain().then_inc(seg, 1)
                        dve.drain().then_inc(cols_ready, 1)
                        dve.wait_ge(dec, c + 1)
                        if c == 0:
                            V(dve.tensor_tensor(gl[:, :], gl[:, :], gcol[:, 0, :], ALU.subtract))
                            dve.drain().then_inc(kd_sub, 1)
                        for dst, mask in ((AT, st.strict), (QT, st.incl)):
                            for half in range(2):
                                bank = m.to_dve.get(dve)
                                m.to_dve.free(dve.tensor_tensor(h4(dst, half), inv.bank3(bank), h4(E, half), ALU.mult))
                                V(dve.engine_nop())
                                V(dve.tensor_tensor(h4(dst, half), h4(dst, half), view(mask[:, 0:1], [[0, 4], [1, P]]), ALU.mult))
                        inv.on_dve(dve, V)
                        dve.drain().then_inc(tt_ready, 1)
                        for half in range(2):
                            bank = m.to_dve.get(dve)
                            m.to_dve.free(dve.tensor_copy(h4(un, half), inv.bank3(bank)))
                        if c:
                            for half in range(2):
                                bank = m.to_dve.get(dve)
                                m.to_dve.free(dve.tensor_copy(h4(wT, half), inv.bank3(bank)))
                            dve.drain().then_inc(w_ready, 1)
                            V(dve.engine_nop())
                            for half in range(2):
                                bank = m.to_dve.get(dve)
                                m.to_dve.free(dve.tensor_tensor(h4(un, half), h4(un, half), inv.bank3(bank), ALU.subtract))
                        dve.drain().then_inc(vn_ready, 1)
                        if c == 0:
                            dve.wait_ge(kd_exp, 1)
                            V(dve.tensor_tensor(kd[:, :, :], part_rows(1, 0), spread(gl[:, :], GD), ALU.mult))
                            dve.drain().then_inc(kd_ready, 1)
                        for half in range(2):
                            bank = m.to_dve.get(dve)
                            m.to_dve.free(dve.tensor_copy(h4(part_rows(2, c), half), inv.bank3(bank)))
                        dve.drain().then_inc(o_ready, 1)
                        if c == 0:
                            for half in range(2):
                                bank = m.to_dve.get(dve)
                                m.to_dve.free(dve.tensor_copy(h4(S, half), inv.bank3(bank)))
                            dve.drain().then_inc(s_ready, 1)
                            dve.wait_ge(s_ready, 1)
                    for tt in range(TT):
                        o = part_rows(2, tt)
                        dve.wait_ge(o_sq, tt + 1)
                        V(dve.tensor_reduce(ss[:, tt, 0:GH], sq2, AX_X, ALU.add))
                        dve.tensor_scalar(ss[:, tt, 0:GH], ss[:, tt, 0:GH], 1.0 / GD, EPS, ALU.mult, ALU.add).then_inc(o_ms, 1)
                        dve.wait_ge(o_root, tt + 1)
                        V(dve.reciprocal(ss[:, tt, 0:GH], ss[:, tt, 0:GH]))
                        V(dve.tensor_tensor(o, o, spread(ss[:, tt, 0:GH], GD), ALU.mult))
                        V(dve.tensor_tensor(o, o, view(nw[:, 0:1], [[0, GH], [1, GD]]), ALU.mult))
                        V(dve.tensor_tensor(o, o, part_rows(3, tt), ALU.mult))
                    dve.drain().then_inc(o_done, 1)
                    for j in range(GH // 2):
                        bank = m.to_dve.get(dve)
                        m.to_dve.free(dve.tensor_copy(cols[:, 2 * j:2 * j + 2, :], view(bank[:, 0:1], [[T, 2], [1, T]])))



RH, RN, RC = 16, 64, 64
LORA = 96
NR = 3 * HALF + 2 * LORA
PAIRS = RH // 2
LN_EPS = 64e-5


def stage_rwkv(nc, m, io, st, acts, cols):
    with ExitStack() as ctx:
        NP_ = NR + HALF
        pr = m.sb(ctx, "rwkv_rows", [P, TT, NP_])
        project(nc, m, st, acts, KD, io["w_in_2"][0], RF0, NP_, lambda tt, c, n: pr[:, tt, c:c + n])
        Kt = m.sb(ctx, "rwkv_K", [P, TT, HALF])
        B = m.sb(ctx, "rwkv_B", [P, TT, HALF])
        pc = m.sb(ctx, "rwkv_chunk_decay", [P, PAIRS, 2 * TT])
        bonus = m.sb(ctx, "rwkv_bonus", [P, TT, RH])
        mask2 = m.sb(ctx, "rwkv_masks", [P, 2, P])
        small = m.sb(ctx, "rwkv_small", [P, TT, RH])
        small2 = m.sb(ctx, "rwkv_small2", [P, TT, RH])
        chunk_ind = m.sb(ctx, "chunk_indicator", [P, 2])

        def part(i, tt):
            return pr[:, tt, i * HALF:(i + 1) * HALF]

        def heads(ap):
            return ap.rearrange("p (h d) -> p h d", d=RN)

        with ExitStack() as c1:
            prev = arrays_of(m.weights.buf[0], 1, [TT, NR])[0]
            mu = arrays_of(m.weights.buf[1], 1, [NR])[0]
            shifted, mu_loaded, first_zero = m.sem("rwkv_prev_loaded"), m.sem("rwkv_mu_loaded"), m.sem("rwkv_first_zeroed")
            ind0 = m.sem("indicator_ones")
            with nc.Block() as block:
                @block.sync
                def _(sp):
                    sp.dma_start(mu, everywhere(io["rwkv_mu_2"], NR)).then_inc(mu_loaded, 16)
                    for tt in range(TT):
                        sp.dma_start(prev[1:P, tt, :], pr[0:P - 1, tt, 0:NR]).then_inc(shifted, 16)
                    sp.dma_start(prev[0:1, 1, :], pr[P - 1:P, 0, 0:NR]).then_inc(shifted, 16)

                @block.gpsimd
                def _(pool):
                    pool.memset(chunk_ind[:, :], 1.0).then_inc(ind0, 1)
                    pool.wait_ge(ind0, 1)
                    L = m.pool_chain.on(pool)
                    L(pool.affine_select(out=chunk_ind[:, 0:1], in_=chunk_ind[:, 0:1], compare_op=ALU.is_ge, fill=0.0,
                                         base=RC - 1, pattern=[[0, 1]], channel_multiplier=-1))
                    L(pool.affine_select(out=chunk_ind[:, 1:2], in_=chunk_ind[:, 1:2], compare_op=ALU.is_ge, fill=0.0,
                                         base=-RC, pattern=[[0, 1]], channel_multiplier=1))

                @block.vector
                def _(dve):
                    V = m.dve_chain.on(dve)
                    V(dve.memset(prev[0:1, 0, :], 0.0))
                    for i, mk in enumerate((st.strict, st.incl)):
                        V(dve.tensor_tensor(mask2[:, i, :], mk[:, :], st.same64[:, :], ALU.mult))
                    dve.wait_ge(shifted, 48)
                    dve.wait_ge(mu_loaded, 16)
                    for tt in range(TT):
                        f = pr[:, tt, 0:NR]
                        V(dve.tensor_tensor(prev[:, tt, :], prev[:, tt, :], f, ALU.subtract))
                        V(dve.tensor_tensor(prev[:, tt, :], prev[:, tt, :], mu, ALU.mult))
                        V(dve.tensor_tensor(f, f, prev[:, tt, :], ALU.add))
        bufs1 = arrays_of(m.weights.buf[0], 4, [TT, HALF]) + arrays_of(m.weights.buf[1], 3, [TT, HALF])
        lw, cum, ea, eb, kk, sq, aa = bufs1
        rows1 = arrays_of(m.weights.buf[1], 8, [HALF])[6:8]
        with ExitStack() as c1:
            wup = m.sb(c1, "rwkv_lora_up", [LORA, 2, HALF])
            lT = m.sb(c1, "rwkv_lora_T", [LORA, 2, T])
            brow = Kt[:, 0:1, :]
            brow2, krow = rows1
            up_loaded, r_loaded, r_used = m.sem("rwkv_up_loaded"), m.sem("rwkv_row_loaded"), m.sem("rwkv_row_used")
            th_ready, l_ready, wp_ready, sg_ready = (m.sem("rwkv_" + s) for s in ("tanh_ready", "lora_T_ready", "pre_ready", "sigmoid_ready"))
            lw_ready, cum_ready, exps_ready, sqd, ssr, rtr = (m.sem("rwkv_" + s) for s in ("lw_ready", "cum_ready", "exps_ready", "kk_squared", "kk_ss_ready", "kk_root"))
            sq_used, ea_used = m.sem("rwkv_sq_used"), m.sem("rwkv_ea_used")
            with nc.Block() as block:
                @block.sync
                def _(sp):
                    sp.dma_start(wup[:, 0, :], io["rwkv_w_up_2"][0]).then_inc(up_loaded, 16)
                    sp.dma_start(wup[:, 1, :], io["rwkv_a_up_2"][0]).then_inc(up_loaded, 16)
                    sp.dma_start(brow[:, 0, :], everywhere(io["rwkv_w0_2"], HALF)).then_inc(r_loaded, 16)
                    sp.wait_ge(r_loaded, 16)
                    sp.dma_start(brow2, everywhere(io["rwkv_a0_2"], HALF)).then_inc(r_loaded, 16)
                    sp.wait_ge(r_loaded, 32)
                    for i, name in enumerate(("rwkv_k_k_2", "rwkv_k_a_2", "rwkv_r_k_2")):
                        if i:
                            sp.wait_ge(r_used, i)
                        sp.dma_start(krow, everywhere(flat(io[name]), HALF)).then_inc(r_loaded, 16)
                        sp.wait_ge(r_loaded, 16 * (i + 3))

                @block.tensor
                def _(pe):
                    pe.wait_ge(th_ready, 1)
                    for i in range(2):
                        bank = m.to_dve.take(pe)
                        for tt in range(TT):
                            c = 3 * HALF + i * LORA
                            mm = pe.transpose(bank[0:LORA, tt * P:(tt + 1) * P], pr[:, tt, c:c + LORA], st.ident[:, :])
                        m.to_dve.put(mm)
                    pe.wait_ge(l_ready, 1)
                    pe.wait_ge(up_loaded, 32)
                    for i in range(2):
                        for tt in range(TT):
                            for c in range(2):
                                bank = m.to_dve.take(pe)
                                m.to_dve.put(pe.matmul(bank[:, :], lT[:, i, tt * P:(tt + 1) * P],
                                                       wup[:, i, c * CHUNK:(c + 1) * CHUNK], start=True, stop=True))
                    pe.wait_ge(lw_ready, 1)
                    for tt in range(TT):
                        for c in range(2):
                            bank = m.to_dve.take(pe)
                            m.to_dve.put(pe.matmul(bank[:, :], mask2[:, 1, :], lw[:, tt, c * CHUNK:(c + 1) * CHUNK],
                                                   start=True, stop=True))
                    bank = m.to_act.take(pe)
                    for q in range(PAIRS):
                        for tt in range(TT):
                            c = (q * TT + tt) * 2
                            mm = pe.matmul(bank[:, c:c + 2], lw[:, tt, q * P:(q + 1) * P], chunk_ind[:, :], start=True, stop=True)
                    m.to_act.put(mm)

                @block.scalar
                def _(act):
                    act.activation(pr[:, :, 3 * HALF:3 * HALF + LORA], pr[:, :, 3 * HALF:3 * HALF + LORA], ACT.Tanh).then_inc(th_ready, 1)
                    act.wait_ge(wp_ready, 1)
                    act.activation(lw, lw, ACT.Sigmoid).then_inc(sg_ready, 1)
                    act.wait_ge(wp_ready, 2)
                    act.activation(aa, aa, ACT.Sigmoid).then_inc(sg_ready, 1)
                    bank = m.to_act.get(act)
                    m.to_act.free(act.activation(pc[:, :, :], bank[:, 0:4 * PAIRS], ACT.Exp))
                    act.wait_ge(sqd, 1)
                    act.activation(sq, kk, ACT.Square).then_inc(ssr, 1)
                    act.wait_ge(cum_ready, 1)
                    act.activation(ea, cum, ACT.Exp)
                    act.activation(eb, cum, ACT.Exp, scale=-1.0).then_inc(exps_ready, 1)
                    act.wait_ge(sqd, 2)
                    act.activation(small[:, :, :], small[:, :, :], ACT.Sqrt).then_inc(rtr, 1)
                    act.wait_ge(ea_used, 1)
                    act.activation(ea, cum, ACT.Exp).then_inc(exps_ready, 1)
                    act.activation(pr[:, :, NR:NR + HALF], pr[:, :, NR:NR + HALF], ACT.Silu)

                @block.vector
                def _(dve):
                    V = m.dve_chain.on(dve)
                    for i in range(2):
                        bank = m.to_dve.get(dve)
                        m.to_dve.free(dve.tensor_copy(lT[:, i, :], bank[0:LORA, 0:T]))
                    dve.drain().then_inc(l_ready, 1)
                    dve.wait_ge(r_loaded, 32)
                    for i, (dst, row) in enumerate(((lw, brow[:, 0, :]), (aa, brow2))):
                        for tt in range(TT):
                            for c in range(2):
                                bank = m.to_dve.get(dve)
                                m.to_dve.free(dve.tensor_tensor(dst[:, tt, c * CHUNK:(c + 1) * CHUNK], bank[:, :],
                                                                row[:, c * CHUNK:(c + 1) * CHUNK], ALU.add))
                        dve.drain().then_inc(wp_ready, 1)
                    dve.wait_ge(sg_ready, 1)
                    V(dve.tensor_scalar(lw, lw, -float(np.exp(np.float32(-0.5))), None, ALU.mult))
                    dve.drain().then_inc(lw_ready, 1)
                    dve.wait_ge(r_loaded, 48)
                    for tt in range(TT):
                        V(dve.tensor_tensor(kk[:, tt, :], part(1, tt), krow, ALU.mult))
                    dve.drain().then_inc(sqd, 1)
                    dve.drain().then_inc(r_used, 1)
                    for tt in range(TT):
                        for c in range(2):
                            bank = m.to_dve.get(dve)
                            m.to_dve.free(dve.tensor_copy(cum[:, tt, c * CHUNK:(c + 1) * CHUNK], bank[:, :]))
                    dve.drain().then_inc(cum_ready, 1)
                    dve.wait_ge(ssr, 1)
                    V(dve.tensor_reduce(small[:, :, :], sq.rearrange("p t (h d) -> p (t h) d", d=RN), AX_X, ALU.add))
                    V(dve.tensor_scalar(small[:, :, :], small[:, :, :], EPS, None, ALU.add))
                    dve.drain().then_inc(sqd, 1)
                    dve.wait_ge(rtr, 1)
                    V(dve.reciprocal(small[:, :, :], small[:, :, :]))
                    for tt in range(TT):
                        V(dve.tensor_tensor(heads(kk[:, tt, :]), heads(kk[:, tt, :]), spread(small[:, tt, :], RN), ALU.mult))
                    dve.wait_ge(sg_ready, 2)
                    dve.wait_ge(r_loaded, 64)
                    for tt in range(TT):
                        V(dve.scalar_tensor_tensor(out=sq[:, tt, :], in0=aa[:, tt, :], scalar=1.0, in1=krow,
                                                   op0=ALU.subtract, op1=ALU.mult))
                        V(dve.scalar_tensor_tensor(out=part(1, tt), in0=sq[:, tt, :], scalar=1.0, in1=part(1, tt),
                                                   op0=ALU.add, op1=ALU.mult))
                    dve.drain().then_inc(r_used, 1)
                    dve.wait_ge(r_loaded, 80)
                    for tt in range(TT):
                        V(dve.tensor_tensor(sq[:, tt, :], part(0, tt), part(1, tt), ALU.mult))
                        V(dve.tensor_tensor(sq[:, tt, :], sq[:, tt, :], krow, ALU.mult))
                    V(dve.tensor_reduce(bonus[:, :, :], sq.rearrange("p t (h d) -> p (t h) d", d=RN), AX_X, ALU.add))
                    dve.wait_ge(exps_ready, 1)
                    for tt in range(TT):
                        V(dve.tensor_tensor(part(0, tt), part(0, tt), ea[:, tt, :], ALU.mult))
                        V(dve.tensor_tensor(part(1, tt), part(1, tt), eb[:, tt, :], ALU.mult))
                        V(dve.tensor_tensor(B[:, tt, :], kk[:, tt, :], aa[:, tt, :], ALU.mult))
                        V(dve.tensor_tensor(B[:, tt, :], B[:, tt, :], eb[:, tt, :], ALU.mult))
                    V(dve.tensor_tensor(cum, cum, lw, ALU.subtract))
                    dve.drain().then_inc(ea_used, 1)
                    dve.wait_ge(exps_ready, 2)
                    for tt in range(TT):
                        V(dve.tensor_tensor(Kt[:, tt, :], kk[:, tt, :], ea[:, tt, :], ALU.mult))
        y = Kt
        S = m.sb(ctx, "rwkv_state", [P, PAIRS, 2, RN])
        flat0 = m.weights.buf[0][:, :, :].rearrange("p k n -> p (k n)")
        KR = flat0[:, 0:4096].rearrange("p (q f t) -> p q f t", q=PAIRS, f=2)
        BT = flat0[:, 4096:6144].rearrange("p (q t) -> p q t", t=T)
        DT = flat0[:, 6144:8192].rearrange("p (q t) -> p q t", t=T)
        flat1 = m.weights.buf[1][:, :, :].rearrange("p k n -> p (k n)")
        ABm = flat1[:, 0:2048].rearrange("p (u f t) -> p u f t", u=UNITS, f=2)
        ADm = flat1[:, 2048:4096].rearrange("p (u f t) -> p u f t", u=UNITS, f=2)
        Tm, TT_, X, M = (flat1[:, 4096 + i * 1024:4096 + (i + 1) * 1024].rearrange("p (u t) -> p u t", t=P) for i in range(4))
        AT = ABm[:, :, 0, :]
        with ExitStack() as c2:
            xu = m.sb(c2, "rwkv_xu", [P, 2, UNITS * RN])
            inv = Inverse(m, st, "rwkv", 6, AT, Tm, TT_, X, M)
            turned, masked, x_ready, u_ready, s_ready, y_ready = (m.sem("rwkv_" + s) for s in ("turned", "masked", "xk_ready", "u_ready", "s_ready", "y_ready"))
            tready = m.sem("rwkv_tt_ready")
            groups = [(hg, tt) for hg in range(2) for tt in range(TT)]
            with nc.Block() as block:
                @block.gpsimd
                def _(pool):
                    for n in range(len(groups)):
                        inv.n = n
                        inv.on_pool(pool)

                @block.scalar
                def _(act):
                    for n in range(len(groups)):
                        inv.n = n
                        inv.on_act(act)

                @block.tensor
                def _(pe):
                    for src in (lambda k, tt: Kt[:, tt, k * P:(k + 1) * P], lambda k, tt: part(0, tt)[:, k * P:(k + 1) * P],
                                lambda k, tt: B[:, tt, k * P:(k + 1) * P], lambda k, tt: part(1, tt)[:, k * P:(k + 1) * P]):
                        turn_to_columns(pe, m.to_dve, st.ident[:, :], src, PAIRS)
                    pe.wait_ge(turned, 1)
                    for n, (hg, tt) in enumerate(groups):
                        inv.n = n
                        tok = slice(tt * P, (tt + 1) * P)
                        hs = [(u, hg * UNITS + u) for u in range(UNITS)]

                        def rng(h):
                            return slice((h % 2) * RN, (h % 2 + 1) * RN)

                        for left in (BT, DT):
                            for j in range(UNITS // 2):
                                bank = m.to_dve.take(pe)
                                u0 = (j // 2) * 4 + j % 2
                                for i, (u, h) in enumerate((hs[u0], hs[u0 + 2])):
                                    mm = pe.matmul(bank[:, i * 2 * P:(i + 1) * 2 * P].rearrange("p (f t) -> p f t", f=2),
                                                   left[rng(h), h // 2, tok], KR[rng(h), h // 2, :, tok], start=True, stop=True)
                                m.to_dve.put(mm)
                        inv.on_pe(pe)
                        pe.wait_ge(tready, n + 1)
                        for c in range(2):
                            step = 2 * n + c
                            ps = slice(c * RC, (c + 1) * RC)
                            ct = slice(tt * P + c * RC, tt * P + (c + 1) * RC)
                            first = tt == 0 and c == 0
                            if not first:
                                pe.wait_ge(s_ready, step - hg)
                            bank = m.to_dve.take(pe)
                            for u, h in hs:
                                o = bank[ps, u * RN:(u + 1) * RN]
                                if not first:
                                    pe.matmul(o, KR[:, h // 2, 0, ct], S[:, h // 2, h % 2, :], start=True, stop=False)
                                mm = pe.matmul(o, ADm[:, u, 0, ps], part(2, tt)[:, h * RN:(h + 1) * RN], start=first, stop=True)
                            m.to_dve.put(mm)
                            pe.wait_ge(x_ready, step + 1)
                            bank = m.to_dve.take(pe)
                            for u, h in hs:
                                mm = pe.matmul(bank[ps, u * RN:(u + 1) * RN], TT_[:, u, ps], xu[:, 0, u * RN:(u + 1) * RN],
                                               start=True, stop=True)
                            m.to_dve.put(mm)
                            pe.wait_ge(u_ready, step + 1)
                            bank = m.to_dve.take(pe)
                            for u, h in hs:
                                o = bank[ps, u * RN:(u + 1) * RN]
                                if not first:
                                    pe.matmul(o, KR[:, h // 2, 1, ct], S[:, h // 2, h % 2, :], start=True, stop=False)
                                pe.matmul(o, ABm[:, u, 1, ps], xu[:, 1, u * RN:(u + 1) * RN], start=first, stop=False)
                                mm = pe.matmul(o, ADm[:, u, 1, ps], part(2, tt)[:, h * RN:(h + 1) * RN], start=False, stop=True)
                            m.to_dve.put(mm)
                            if tt == TT - 1 and c == 1:
                                continue
                            bank = m.to_dve.take(pe)
                            for u, h in hs:
                                o = bank[rng(h), (u // 2) * RN:(u // 2 + 1) * RN]
                                hc = slice(h * RN, (h + 1) * RN)
                                pe.matmul(o, B[ps, tt, hc], xu[ps, 1, u * RN:(u + 1) * RN], start=True, stop=False)
                                mm = pe.matmul(o, part(1, tt)[ps, hc], part(2, tt)[ps, hc], start=False, stop=True)
                            m.to_dve.put(mm)

                @block.vector
                def _(dve):
                    V = m.dve_chain.on(dve)
                    V(dve.memset(S[:, :, :, :], 0.0))
                    V(dve.memset(xu[:, :, :], 0.0))
                    for dst in (KR[:, :, 0, :], KR[:, :, 1, :], BT, DT):
                        for j in range(PAIRS // 2):
                            bank = m.to_dve.get(dve)
                            m.to_dve.free(dve.tensor_copy(dst[:, 2 * j:2 * j + 2, :], view(bank[:, 0:1], [[T, 2], [1, T]])))
                    dve.drain().then_inc(turned, 1)
                    for n, (hg, tt) in enumerate(groups):
                        inv.n = n
                        for dst in (ABm, ADm):
                            for j in range(UNITS // 2):
                                bank = m.to_dve.get(dve)
                                u0 = (j // 2) * 4 + j % 2
                                m.to_dve.free(dve.tensor_tensor(view(dst[:, u0, 0, 0:1], [[4 * P, 2], [1, 2 * P]]),
                                                                view(bank[:, 0:1], [[2 * P, 2], [1, 2 * P]]),
                                                                view(mask2[:, 0, 0:1], [[0, 2], [1, 2 * P]]), ALU.mult))
                        V(dve.engine_nop())
                        inv.on_dve(dve, V)
                        dve.drain().then_inc(tready, 1)
                        for c in range(2):
                            step = 2 * n + c
                            ps = slice(c * RC, (c + 1) * RC)
                            bank = m.to_dve.get(dve)
                            m.to_dve.free(dve.tensor_scalar(xu[ps, 0, :], bank[ps, :], -1.0, None, ALU.mult))
                            dve.drain().then_inc(x_ready, 1)
                            bank = m.to_dve.get(dve)
                            m.to_dve.free(dve.tensor_copy(xu[ps, 1, :], bank[ps, :]))
                            dve.drain().then_inc(u_ready, 1)
                            bank = m.to_dve.get(dve)
                            m.to_dve.free(dve.tensor_copy(y[ps, tt, hg * CHUNK:(hg + 1) * CHUNK], bank[ps, :]))
                            if tt == TT - 1 and c == 1:
                                continue
                            bank = m.to_dve.get(dve)
                            later = tt > 0 or c > 0
                            for e in range(2):
                                er = slice(e * RN, (e + 1) * RN)
                                Se = S[er, hg * 4:hg * 4 + 4, e, :]
                                src = view(bank[er, 0:1], [[RN, 4], [1, RN]])
                                last = dve.tensor_tensor(Se, src, Se, ALU.add) if later else dve.tensor_copy(Se, src)
                            m.to_dve.free(last)
                            V(dve.engine_nop())
                            for e in range(2):
                                er = slice(e * RN, (e + 1) * RN)
                                Se = S[er, hg * 4:hg * 4 + 4, e, :]
                                V(dve.tensor_tensor(Se, Se, spread(pc[er, hg * 4:hg * 4 + 4, 2 * tt + c], RN), ALU.mult))
                            dve.drain().then_inc(s_ready, 1)
        yy, lnw, lnb = arrays_of(m.weights.buf[0], 1, [TT, HALF]) + arrays_of(m.weights.buf[1], 2, [HALF])
        ln_loaded, cent, sqr, msr, rootr, out_ready = (m.sem("rwkv_" + s) for s in ("ln_loaded", "centred", "y_squared", "var_ready", "var_root", "out_ready"))
        with nc.Block() as block:
            @block.sync
            def _(sp):
                sp.dma_start(lnw, everywhere(io["rwkv_lnx_w_2"], HALF)).then_inc(ln_loaded, 16)
                sp.dma_start(lnb, everywhere(io["rwkv_lnx_b_2"], HALF)).then_inc(ln_loaded, 16)

            @block.scalar
            def _(act):
                act.wait_ge(cent, 1)
                act.activation(yy, y[:, :, :], ACT.Square).then_inc(sqr, 1)
                act.wait_ge(msr, 1)
                act.activation(small2[:, :, :], small2[:, :, :], ACT.Sqrt).then_inc(rootr, 1)

            @block.vector
            def _(dve):
                V = m.dve_chain.on(dve)
                V(dve.tensor_reduce(small[:, :, :], y[:, :, :].rearrange("p t (h d) -> p (t h) d", d=RN), AX_X, ALU.add))
                V(dve.tensor_scalar(small[:, :, :], small[:, :, :], 1.0 / RN, None, ALU.mult))
                for tt in range(TT):
                    V(dve.tensor_tensor(heads(y[:, tt, :]), heads(y[:, tt, :]), spread(small[:, tt, :], RN), ALU.subtract))
                dve.drain().then_inc(cent, 1)
                dve.wait_ge(sqr, 1)
                V(dve.tensor_reduce(small2[:, :, :], yy.rearrange("p t (h d) -> p (t h) d", d=RN), AX_X, ALU.add))
                dve.tensor_scalar(small2[:, :, :], small2[:, :, :], 1.0 / RN, LN_EPS, ALU.mult, ALU.add).then_inc(msr, 1)
                dve.wait_ge(rootr, 1)
                V(dve.reciprocal(small2[:, :, :], small2[:, :, :]))
                dve.wait_ge(ln_loaded, 32)
                for tt in range(TT):
                    o = y[:, tt, :]
                    V(dve.tensor_tensor(heads(o), heads(o), spread(small2[:, tt, :], RN), ALU.mult))
                    V(dve.tensor_tensor(o, o, lnw, ALU.mult))
                    V(dve.tensor_tensor(o, o, lnb, ALU.add))
                    V(dve.tensor_tensor(heads(part(2, tt)), heads(part(2, tt)), spread(bonus[:, tt, :], RN), ALU.mult))
                    V(dve.tensor_tensor(o, o, part(2, tt), ALU.add))
                    V(dve.tensor_tensor(o, o, pr[:, tt, NR:NR + HALF], ALU.mult))
                dve.drain().then_inc(out_ready, 1)
                for j in range(PAIRS // 2):
                    bank = m.to_dve.get(dve)
                    m.to_dve.free(dve.tensor_copy(cols[:, 2 * j:2 * j + 2, :], view(bank[:, 0:1], [[T, 2], [1, T]])))

            @block.tensor
            def _(pe):
                pe.wait_ge(out_ready, 1)
                turn_to_columns(pe, m.to_dve, st.ident[:, :], lambda k, tt: y[:, tt, k * P:(k + 1) * P], PAIRS)



S5_TILES, S5_BLOCK = 32, 16
S5_BLOCKS = T // S5_BLOCK
S5_AT_DVE = 22
S5_CARRY_TILES = 2
TWO_PI_PARTS = (6.28125, 0.0019353071693331003, 1.0253131677018246e-11)
ROUND = 1.5 * 2 ** 23


def s5_complex(eng, C, out, x, y, tmp):
    eng.tensor_tensor(out[0], x[0], y[0], ALU.mult)
    eng.tensor_tensor(out[1], x[0], y[1], ALU.mult)
    eng.tensor_tensor(tmp[0], x[1], y[1], ALU.mult)
    C(eng.tensor_tensor(tmp[1], x[1], y[0], ALU.mult))
    eng.tensor_tensor(out[0], out[0], tmp[0], ALU.subtract)
    C(eng.tensor_tensor(out[1], out[1], tmp[1], ALU.add))


def s5_accumulate(eng, C, out, x, y, tmp):
    eng.tensor_tensor(tmp[0], x[0], y[0], ALU.mult)
    eng.tensor_tensor(tmp[1], x[0], y[1], ALU.mult)
    eng.tensor_tensor(tmp[2], x[1], y[1], ALU.mult)
    C(eng.tensor_tensor(tmp[3], x[1], y[0], ALU.mult))
    eng.tensor_tensor(out[0], out[0], tmp[0], ALU.add)
    C(eng.tensor_tensor(out[1], out[1], tmp[1], ALU.add))
    eng.tensor_tensor(out[0], out[0], tmp[2], ALU.subtract)
    C(eng.tensor_tensor(out[1], out[1], tmp[3], ALU.add))


def s5_scan(eng, C, i0, i1, S, a, pw, carry, tmp):
    n = i1 - i0

    def temps(dims):
        names = "abc"[:len(dims)]
        size = int(np.prod(dims))
        spec = {c: s for c, s in zip(names[1:], dims[1:])}
        return [t[:, 0:size].rearrange(f"p ({' '.join(names)}) -> p {' '.join(names)}", **spec) for t in tmp]

    for f in range(2):
        C(eng.tensor_copy(pw[f][:, i0:i1, 0:1], a[f][:, i0:i1].rearrange("p (i o) -> p i o", o=1)))
    m = 1
    while m < S5_BLOCK:
        s5_complex(eng, C, [w[:, i0:i1, m:2 * m] for w in pw], [w[:, i0:i1, 0:m] for w in pw],
                   [spread(w[:, i0:i1, m - 1], m) for w in pw], temps([n, m]))
        m *= 2
    cut = [s[:, i0:i1, :].rearrange("p i (b j) -> p i b j", j=S5_BLOCK) for s in S]
    for j in range(1, S5_BLOCK):
        s5_accumulate(eng, C, [s[:, :, :, j] for s in cut], [spread(x[:, i0:i1], S5_BLOCKS) for x in a],
                      [s[:, :, :, j - 1] for s in cut], temps([n, S5_BLOCKS]))
    for f in range(2):
        C(eng.tensor_copy(carry[f][:, i0:i1, 1:], cut[f][:, :, 0:S5_BLOCKS - 1, S5_BLOCK - 1]))
    for b in range(2, S5_BLOCKS):
        s5_accumulate(eng, C, [x[:, i0:i1, b] for x in carry], [w[:, i0:i1, S5_BLOCK - 1] for w in pw],
                      [x[:, i0:i1, b - 1] for x in carry], temps([n]))
    for i in range(i0, i1, S5_CARRY_TILES):
        q = S5_CARRY_TILES
        powers = [bass.AP(tensor=w.tensor, offset=w[:, i:i + q, :].offset,
                          ap=[list(w.ap[0]), [S5_BLOCK, q], [0, S5_BLOCKS - 1], [1, S5_BLOCK]]) for w in pw]
        s5_accumulate(eng, C, [s[:, i:i + q, S5_BLOCK:].rearrange("p i (b j) -> p i b j", j=S5_BLOCK) for s in S],
                      powers, [spread(x[:, i:i + q, 1:], S5_BLOCK) for x in carry], temps([q, S5_BLOCKS - 1, S5_BLOCK]))
        yield i


def stage_s5(nc, m, io, st, acts, cols):
    with ExitStack() as ctx:
        pr = m.sb(ctx, "s5_rows", [P, TT, 2 * HALF])
        project(nc, m, st, acts, KD, io["w_in_2"][0], SU0, 2 * HALF, lambda tt, c, n: pr[:, tt, c:c + n])
        uT = m.sb(ctx, "s5_u_columns", [P, 8, T])
        BT = m.sb(ctx, "s5_B_T", [P, 8, 2, P])
        CT = m.sb(ctx, "s5_C_T", [P, 8, 2, P])
        consts = m.sb(ctx, "s5_coefs", [P, 4, S5_TILES])
        par = m.sb(ctx, "s5_parity", [P, 2])
        with ExitStack() as c1:
            R = S5_TILES
            rr = m.sb(c1, "s5_row_work", [R, 14, P])
            are, aim, mag, th, n_, rd, sn, sh, den, w0, abr, abi, cr, ci = (rr[:, q, :] for q in range(14))
            ldt = m.sb(c1, "s5_log_dt", [R, 2])
            par8 = m.sb(c1, "s5_parity8", [P, 8])
            dbs = arrays_of(m.weights.buf[0], 2, [R, 2, 16])
            bl = arrays_of(m.weights.buf[0], 8, [R, 16])[4:]
            crows = arrays_of(m.weights.buf[1], 2, [8, 2, 64])
            cl = arrays_of(m.weights.buf[1], 6, [8, 64])[4:]
            loaded, dt_ready, th_ready, trig, rows_ready = (m.sem("s5_" + s) for s in ("loaded", "dt_ready", "theta_ready", "trig_ready", "coefs_ready"))
            c_ready, b_ready = m.sem("s5_c_ready"), m.sem("s5_b_ready")
            with nc.Block() as block:
                @block.sync
                def _(sp):
                    sp.dma_start(are, io["s5_a_re_2"][0].rearrange("(i g) p -> i (g p)", g=2)).then_inc(loaded, 16)
                    sp.dma_start(aim, io["s5_a_im_2"][0].rearrange("(i g) p -> i (g p)", g=2)).then_inc(loaded, 16)
                    sp.dma_start(ldt[:, :], io["s5_log_dt_2"][0].rearrange("(i g) -> i g", g=2)).then_inc(loaded, 16)
                    for f, nm in enumerate(("re", "im")):
                        sp.dma_start(cl[f], io[f"s5_c_{nm}_2"][0].rearrange("(k g) c p -> (g c) k p", g=8)).then_inc(loaded, 16)
                        sp.dma_start(bl[f], io[f"s5_b_{nm}_2"][0].rearrange("(i g) p c -> (g p) i c", g=2)).then_inc(loaded, 16)

                @block.scalar
                def _(act):
                    A = m.act_chain.on(act)
                    act.activation(pr[:, :, HALF:2 * HALF], pr[:, :, HALF:2 * HALF], ACT.Silu)
                    act.wait_ge(loaded, 112)
                    A(act.activation(ldt[:, :], ldt[:, :], ACT.Exp))
                    act.drain().then_inc(dt_ready, 1)
                    act.wait_ge(th_ready, 1)
                    act.activation(mag, mag, ACT.Exp)
                    act.activation(sn, rd, ACT.Sin)
                    act.activation(sh, rd, ACT.Sin, scale=0.5)
                    act.drain().then_inc(trig, 1)

                @block.vector
                def _(dve):
                    V = m.dve_chain.on(dve)
                    V(dve.tensor_reduce(par8[:, :], st.ident[:, :].rearrange("p (b c) -> p b c", c=16), AX_X, ALU.add))
                    V(dve.tensor_reduce(par[:, :], view(par8[:, 0:1], [[1, 2], [2, 4]]), AX_X, ALU.add))
                    V(dve.memset(dbs[0], 0.0))
                    V(dve.memset(dbs[1], 0.0))
                    for j in range(4):
                        bank = m.to_dve.get(dve)
                        m.to_dve.free(dve.tensor_copy(uT[:, 2 * j:2 * j + 2, :], view(bank[:, 0:1], [[T, 2], [1, T]])))
                    dve.wait_ge(dt_ready, 1)
                    dve.tensor_tensor(mag.rearrange("i (g p) -> i g p", g=2), are.rearrange("i (g p) -> i g p", g=2),
                                      spread(ldt[:, :], 64), ALU.mult)
                    V(dve.tensor_tensor(th.rearrange("i (g p) -> i g p", g=2), aim.rearrange("i (g p) -> i g p", g=2),
                                        spread(ldt[:, :], 64), ALU.mult))
                    V(dve.tensor_scalar(n_, th, 1.0 / (2 * np.pi), None, ALU.mult))
                    V(dve.tensor_scalar(n_, n_, ROUND, None, ALU.add))
                    V(dve.tensor_scalar(n_, n_, ROUND, None, ALU.subtract))
                    V(dve.scalar_tensor_tensor(out=rd, in0=n_, scalar=-TWO_PI_PARTS[0], in1=th, op0=ALU.mult, op1=ALU.add))
                    for part in TWO_PI_PARTS[1:]:
                        V(dve.scalar_tensor_tensor(out=rd, in0=n_, scalar=-part, in1=rd, op0=ALU.mult, op1=ALU.add))
                    V(dve.tensor_scalar(rd, rd, 3.1415925, -3.1415925, ALU.min, ALU.max))
                    dve.drain().then_inc(th_ready, 1)
                    for f in range(2):
                        for g in range(2):
                            V(dve.tensor_scalar(crows[f][:, :, g, :], cl[f], par[:, g:g + 1], -1.0 if f else 1.0, ALU.mult, ALU.mult))
                    dve.drain().then_inc(c_ready, 1)
                    for j in range(4):
                        bank = m.to_dve.get(dve)
                        m.to_dve.free(dve.tensor_copy(CT[:, 2 * j:2 * j + 2, :, :].rearrange("p k f s -> p (k f s)"), bank[:, :]))
                    dve.wait_ge(trig, 1)
                    V(dve.tensor_tensor(abr, sh, sh, ALU.mult))
                    V(dve.tensor_scalar(abr, abr, -2.0, 1.0, ALU.mult, ALU.add))
                    V(dve.tensor_tensor(abr, abr, mag, ALU.mult))
                    V(dve.tensor_tensor(abi, sn, mag, ALU.mult))
                    V(dve.tensor_tensor(den, are, are, ALU.mult))
                    V(dve.tensor_tensor(w0, aim, aim, ALU.mult))
                    V(dve.tensor_tensor(den, den, w0, ALU.add))
                    V(dve.reciprocal(den, den))
                    V(dve.tensor_scalar(n_, abr, 1.0, None, ALU.subtract))
                    V(dve.tensor_tensor(cr, n_, are, ALU.mult))
                    V(dve.tensor_tensor(w0, abi, aim, ALU.mult))
                    V(dve.tensor_tensor(cr, cr, w0, ALU.add))
                    V(dve.tensor_tensor(cr, cr, den, ALU.mult))
                    V(dve.tensor_tensor(ci, abi, are, ALU.mult))
                    V(dve.tensor_tensor(w0, n_, aim, ALU.mult))
                    V(dve.tensor_tensor(ci, ci, w0, ALU.subtract))
                    V(dve.tensor_tensor(ci, ci, den, ALU.mult))
                    dve.drain().then_inc(rows_ready, 1)
                    bank = m.to_dve.get(dve)
                    m.to_dve.free(dve.tensor_copy(consts[:, :, :].rearrange("p f i -> p (f i)"), bank[:, 0:4 * R]))
                    V(dve.engine_nop())
                    tmp = bl[2]
                    for g in range(2):
                        hp = slice(g * 64, (g + 1) * 64)
                        cre, cim = (spread(consts[hp, f, :], 16) for f in (2, 3))
                        for f, (x, y, op) in enumerate(((0, 1, ALU.subtract), (1, 0, ALU.add))):
                            o = dbs[f][hp, :, g, :]
                            V(dve.tensor_tensor(o, cre, bl[x][hp], ALU.mult))
                            V(dve.tensor_tensor(tmp[hp], cim, bl[y][hp], ALU.mult))
                            V(dve.tensor_tensor(o, o, tmp[hp], op))
                    dve.drain().then_inc(b_ready, 1)
                    for j in range(4):
                        bank = m.to_dve.get(dve)
                        m.to_dve.free(dve.tensor_copy(BT[:, 2 * j:2 * j + 2, :, :].rearrange("p k f s -> p (k f s)"), bank[:, :]))

                @block.tensor
                def _(pe):
                    turn_to_columns(pe, m.to_dve, st.ident[:, :], lambda k, tt: pr[:, tt, k * P:(k + 1) * P], 8)

                    def turn(src):
                        for j in range(4):
                            bank = m.to_dve.take(pe)
                            for u in range(4):
                                mm = pe.transpose(bank[:, u * P:(u + 1) * P], src(2 * j + u // 2, u % 2), st.ident[:, :])
                            m.to_dve.put(mm)

                    pe.wait_ge(c_ready, 1)
                    turn(lambda k, f: crows[f][:, k, :, :].rearrange("p g s -> p (g s)"))
                    pe.wait_ge(rows_ready, 1)
                    bank = m.to_dve.take(pe)
                    for f in range(4):
                        mm = pe.transpose(bank[:, f * R:(f + 1) * R], rr[:, 10 + f, :], st.ident[0:R, 0:R])
                    m.to_dve.put(mm)
                    pe.wait_ge(b_ready, 1)
                    turn(lambda k, f: dbs[f][:, 4 * k:4 * k + 4, :, :].rearrange("p i g c -> p (i g c)"))
        S = arrays_of(m.weights.buf[0], 1, [S5_TILES, T]) + arrays_of(m.weights.buf[1], 1, [S5_TILES, T])
        with ExitStack() as c2:
            pw = [m.sb(c2, f"s5_powers{f}", [P, S5_TILES, S5_BLOCK])[:, :, :] for f in range(2)]
            carry = [m.sb(c2, f"s5_carry{f}", [P, S5_TILES, S5_BLOCKS])[:, :, :] for f in range(2)]
            size = S5_CARRY_TILES * (S5_BLOCKS - 1) * S5_BLOCK
            tmp_dve = [m.sb(c2, f"s5_tmp_dve{q}", [P, size])[:, :] for q in range(4)]
            tmp_pool = [m.sb(c2, f"s5_tmp_pool{q}", [P, size])[:, :] for q in range(4)]
            a = [consts[:, f, :] for f in range(2)]
            bu_ready, bu_act, s_dve, s_pool, y_ready = (m.sem("s5_" + s) for s in ("bu_by_dve", "bu_by_act", "states_dve", "states_pool", "y_ready"))
            with nc.Block() as block:
                @block.tensor
                def _(pe):
                    for i in range(S5_TILES):
                        ring = m.to_act if i % 2 else m.to_dve
                        bank = ring.take(pe)
                        q = slice((i % 4) * 32, (i % 4 + 1) * 32)
                        for f in range(2):
                            mm = pe.matmul(bank[:, f * T:(f + 1) * T], BT[q, i // 4, f, :], uT[q, i // 4, :], start=True, stop=True)
                        ring.put(mm)
                    for j in range(4):
                        bank = m.to_dve.take(pe)
                        for i in range(8 * j, 8 * j + 8):
                            if i < S5_AT_DVE:
                                pe.wait_ge(s_dve, i // S5_CARRY_TILES + 1)
                            else:
                                pe.wait_ge(s_pool, (i - S5_AT_DVE) // S5_CARRY_TILES + 1)
                            o = bank[(i % 4) * 32:(i % 4 + 1) * 32, (i // 4 % 2) * T:(i // 4 % 2 + 1) * T]
                            for f in range(2):
                                mm = pe.matmul(o, CT[:, i // 4, f, (i % 4) * 32:(i % 4 + 1) * 32], S[f][:, i, :],
                                               start=(f == 0), stop=(f == 1))
                        m.to_dve.put(mm)

                @block.scalar
                def _(act):
                    for i in range(1, S5_TILES, 2):
                        bank = m.to_act.get(act)
                        act.activation(S[0][:, i, :], bank[:, 0:T], ACT.Copy)
                        m.to_act.free(act.activation(S[1][:, i, :], bank[:, T:2 * T], ACT.Copy))
                    act.drain().then_inc(bu_act, 1)
                    act.wait_ge(y_ready, 1)
                    act.activation(cols, cols, ACT.Gelu_apprx_tanh)

                @block.gpsimd
                def _(pool):
                    L = m.pool_chain.on(pool)
                    pool.wait_ge(bu_act, 1)
                    pool.wait_ge(bu_ready, 1)
                    for _i in s5_scan(pool, L, S5_AT_DVE, S5_TILES, S, a, pw, carry, tmp_pool):
                        pool.drain().then_inc(s_pool, 1)

                @block.vector
                def _(dve):
                    V = m.dve_chain.on(dve)
                    for i in range(0, S5_TILES, 2):
                        bank = m.to_dve.get(dve)
                        dve.tensor_copy(S[0][:, i, :], bank[:, 0:T])
                        m.to_dve.free(dve.tensor_copy(S[1][:, i, :], bank[:, T:2 * T]))
                    dve.drain().then_inc(bu_ready, 1)
                    V(dve.engine_nop())
                    dve.wait_ge(bu_act, 1)
                    for _i in s5_scan(dve, V, 0, S5_AT_DVE, S, a, pw, carry, tmp_dve):
                        dve.drain().then_inc(s_dve, 1)
                    for j in range(4):
                        bank = m.to_dve.get(dve)
                        for u in range(2):
                            k = 2 * j + u
                            ins = dve.scalar_tensor_tensor(out=cols[:, k, :], in0=uT[:, k, :], scalar=st.vec.col("s5_d_2", k),
                                                           in1=bank[:, u * T:(u + 1) * T], op0=ALU.mult, op1=ALU.add)
                        m.to_dve.free(ins)
                    dve.drain().then_inc(y_ready, 1)
        project_whole(nc, m, cols, 8, io["s5_glu_w_2"][0], HALF, lambda tt, c, n: pr[:, tt, c:c + n])
        with ExitStack() as c3:
            yr = m.sb(c3, "s5_y_rows", [P, TT, HALF])
            gb = m.sb(c3, "s5_glu_b_row", [P, HALF])
            gb_loaded, added, sig, outr = (m.sem("s5_" + s) for s in ("glu_b_loaded", "glu_b_added", "glu_sigmoid", "out_ready"))
            with nc.Block() as block:
                @block.sync
                def _(sp):
                    sp.dma_start(gb[:, :], everywhere(io["s5_glu_b_2"], HALF)).then_inc(gb_loaded, 16)
                    m.weights.load(sp, io["w_in_2"][0], MG0, CHUNK)
                    m.weights.load(sp, io["w_branch_2"][0, 0], 0, CHUNK)

                @block.tensor
                def _(pe):
                    turn_to_rows(pe, m.to_dve, st.ident[:, :], lambda k, tt: cols[:, k, tt * P:(tt + 1) * P], 8)
                    pe.wait_ge(outr, 1)
                    turn_to_columns(pe, m.to_dve, st.ident[:, :], lambda k, tt: yr[:, tt, k * P:(k + 1) * P], 8)

                @block.scalar
                def _(act):
                    act.wait_ge(added, 1)
                    act.activation(pr[:, :, 0:HALF], pr[:, :, 0:HALF], ACT.Sigmoid).then_inc(sig, 1)

                @block.vector
                def _(dve):
                    V = m.dve_chain.on(dve)
                    dve.wait_ge(gb_loaded, 16)
                    for tt in range(TT):
                        V(dve.tensor_tensor(pr[:, tt, 0:HALF], pr[:, tt, 0:HALF], gb[:, :], ALU.add))
                    dve.drain().then_inc(added, 1)
                    for tt in range(TT):
                        for k in range(2):
                            bank = m.to_dve.get(dve)
                            c = k * CHUNK
                            m.to_dve.free(dve.tensor_tensor(yr[:, tt, c:c + CHUNK], bank[:, :], pr[:, tt, HALF + c:HALF + c + CHUNK], ALU.mult))
                    V(dve.engine_nop())
                    dve.wait_ge(sig, 1)
                    V(dve.tensor_tensor(yr[:, :, :], yr[:, :, :], pr[:, :, 0:HALF], ALU.mult))
                    dve.drain().then_inc(outr, 1)
                    for j in range(4):
                        bank = m.to_dve.get(dve)
                        m.to_dve.free(dve.tensor_copy(cols[:, 2 * j:2 * j + 2, :], view(bank[:, 0:1], [[T, 2], [1, T]])))



BRANCHES = 3


def stage_merge(nc, m, io, st, acts, cols):
    with ExitStack() as ctx:
        m.weights.split_memory(ctx)
        merged = m.sb(ctx, "merged_rows", [P, TT, D])
        gb = m.sb(ctx, "gate_b_rows", [P, 2, CHUNK])
        gate = [m.sb(ctx, f"gates{b}", [P, TT, CHUNK]) for b in range(2)]
        tmp = m.sb(ctx, "merge_tmp", [P, TT, CHUNK])
        gb_loaded = [m.sem(f"merge_gate_b_loaded{b}") for b in range(2)]
        gate_ready, sig, done, high_ready, low_done = (m.sem("merge_" + s) for s in ("logits_ready", "gates_ready", "rows_ready", "high_ready", "low_done"))
        work = [(c, size, br) for c, size in chunks(D) for br in range(BRANCHES)]
        AHEAD = m.weights.UNIT * m.weights.UNITS_HELD
        with nc.Block() as block:
            @block.sync
            def _(sp):
                for i, (c, size, br) in enumerate(work):
                    if i:
                        m.weights.load(sp, io["w_in_2"][0], MG0 + br * D + c, size)
                    if i >= 2:
                        sp.wait_ge(gate_ready, i - 1)
                    sp.dma_start(gb[:, i % 2, 0:size], everywhere(io["gate_b_2"][0, br, c:c + size], size)).then_inc(gb_loaded[i % 2], 16)
                    if i:
                        m.weights.load(sp, io["w_branch_2"][0, br], c, size)
                for w, c0, n in first_chunks(io["w_out_2"][0]):
                    m.weights.load(sp, w, c0, n)

            @block.tensor
            def _(pe):
                for c, size, br in work:
                    m.weights.multiply_split(pe, acts, KD, size, m.to_dve)
                    m.weights.multiply(pe, cols[:, 8 * br:8 * br + 8, :], HALF // P, size, m.to_dve)
                pe.wait_ge(done, 1)
                turn_to_columns(pe, m.to_dve, st.ident[:, :], lambda k, tt: merged[:, tt, k * P:(k + 1) * P], KD)

            @block.scalar
            def _(act):
                for i, (c, size, br) in enumerate(work):
                    m.weights.split_high(act, KD, size)
                    m.weights.seen("act")
                    act.wait_ge(gate_ready, i + 1)
                    g = gate[i % 2]
                    act.activation(g[:, :, :], g[:, :, :], ACT.Sigmoid).then_inc(sig, 1)

            @block.vector
            def _(dve):
                V = m.dve_chain.on(dve)
                for i, (c, size, br) in enumerate(work):
                    m.weights.split_low(dve, KD, size, k0=0 if i == 0 else AHEAD)
                    m.weights.seen("dve")
                    dve.wait_ge(gb_loaded[i % 2], 16 * (i // 2 + 1))
                    g = gate[i % 2]
                    for tt in range(TT):
                        bank = m.to_dve.get(dve)
                        m.to_dve.free(dve.tensor_tensor(g[:, tt, :], bank[:, :], gb[:, i % 2, 0:size], ALU.add))
                    dve.drain().then_inc(gate_ready, 1)
                    if i + 1 < len(work):
                        m.weights.split_low(dve, KD, size, k1=AHEAD)
                    dve.wait_ge(sig, i + 1)
                    for tt in range(TT):
                        bank = m.to_dve.get(dve)
                        o = merged[:, tt, c:c + size]
                        dst = o if br == 0 else tmp[:, tt, :]
                        m.to_dve.free(dve.tensor_tensor(dst, bank[:, :], g[:, tt, :], ALU.mult))
                        V(dve.engine_nop())
                        if br:
                            V(dve.tensor_tensor(o, o, tmp[:, tt, :], ALU.add))
                dve.drain().then_inc(done, 1)
                for j in range(KD // 2):
                    bank = m.to_dve.get(dve)
                    src, two = view(bank[:, 0:1], [[T, 2], [1, T]]), slice(2 * j, 2 * j + 2)
                    V(dve.tensor_copy(acts.h[:, two, :], src))
                    m.to_dve.free(dve.tensor_tensor(acts.l[:, two, :], src, acts.h[:, two, :], ALU.subtract))


def whole_program(nc, io, out):
    with ExitStack() as ctx:
        m = Machine(nc, ctx)
        st = shared_state(m)
        stage_modulation(nc, m, io, st)
        with ExitStack() as c1:
            m.weights.memory(c1)
            proj = m.sb(c1, "projection_rows", [P, TT, N_IN])
            with ExitStack() as c2:
                h1 = Split(m, c2, "h1", KD)
                norm_to_columns(nc, m, st, "norm1", st.x, D, h1, lambda j: st.gain1[:, j:j + 1],
                                lambda j: st.mod_cols[:, j:j + 1], x_sem=(m.sem("x_loaded"), 32),
                                ahead=first_chunks(io["w_in"][0]))
                project_in(nc, m, io, st, h1, lambda tt, c, n: proj[:, tt, c:c + n])
            rows = m.sb(c1, "mixer_rows", [P, TT, HALF])
            stage_attention(nc, m, io, st, proj, rows)
            mixed = Split(m, c1, "mixed", KD)
            norm_to_columns(nc, m, st, "attn_norm", rows, HALF, mixed, lambda j: st.vec.col("attn_out_norm", j), None)
            stage_mamba(nc, m, io, st, proj, rows)
            norm_to_columns(nc, m, st, "ssm_norm", rows, HALF, mixed, lambda j: st.vec.col("ssm_norm", j), None,
                            groups=2, k0=HALF // P, ahead=first_chunks(io["w_out"][0]))
            project_residual(nc, m, st, mixed, io["w_out"][0], st.mod_dram[2 * D:3 * D])
        with ExitStack() as c1:
            h2 = Split(m, c1, "h2", KD)
            stage_experts(nc, m, io, st, h2)
        norm_rows(nc, m, st, "block1_norm", st.x, io["norm_final"])
        m.clear_stage_semaphores()
        with ExitStack() as c1:
            m.weights.memory(c1)
            h3 = Split(m, c1, "h3", KD)
            norm_to_columns(nc, m, st, "norm3", st.x, D, h3, lambda j: st.vec.col("norm_w_2", j), None,
                            ahead=first_chunks(io["w_in_2"][0], GQKV0))
            with ExitStack() as c2:
                cols = m.sb(c2, "branch_columns", [P, BRANCHES * 8, T])
                stage_gdn(nc, m, io, st, h3, cols[:, 0:8, :])
                stage_rwkv(nc, m, io, st, h3, cols[:, 8:16, :])
                stage_s5(nc, m, io, st, h3, cols[:, 16:24, :])
                stage_merge(nc, m, io, st, h3, cols)
            project_residual(nc, m, st, h3, io["w_out_2"][0])
        norm_rows(nc, m, st, "block2_norm", st.x, io["final_norm_w_2"], store=out)


_INS = ["x", "c", "ada_w", "ada_b", "norm_mix", "norm_ffn", "w_in", "cmp_pe", "cmp_w1", "cmp_w2", "rel_bias",
        "attn_out_norm", "conv_w", "conv_b", "dt_bias", "a_log", "d_skip", "ssm_norm", "w_out", "peer_wq",
        "peer_subkeys", "peer_u", "peer_v", "norm_final", "norm_w_2", "w_in_2", "gdn_conv_w_2", "gdn_a_log_2",
        "gdn_dt_bias_2", "gdn_norm_w_2", "rwkv_mu_2", "rwkv_w0_2", "rwkv_w_up_2", "rwkv_a0_2", "rwkv_a_up_2",
        "rwkv_k_k_2", "rwkv_k_a_2", "rwkv_r_k_2", "rwkv_lnx_w_2", "rwkv_lnx_b_2", "s5_a_re_2", "s5_a_im_2",
        "s5_log_dt_2", "s5_b_re_2", "s5_b_im_2", "s5_c_re_2", "s5_c_im_2", "s5_d_2", "s5_glu_w_2", "s5_glu_b_2",
        "gate_b_2", "w_branch_2", "w_out_2", "final_norm_w_2"]


def kernel(**inputs):
    import numpy as _np
    import concourse.bacc as _bacc
    from concourse import mybir as _mybir
    from concourse.bass_utils import run_bass_kernel_spmd as _run

    nc = _bacc.Bacc("TRN2", target_bir_lowering=False, num_devices=1)
    arrays, io = {}, {}
    for name in _INS:
        a = _np.ascontiguousarray(inputs[name])
        arrays[f"in_{name}_dram"] = a
        io[name] = nc.dram_tensor(f"in_{name}_dram", a.shape, _mybir.dt.from_np(a.dtype), kind="ExternalInput").ap()
    out = nc.dram_tensor("out_0_dram", (1, T, D), _mybir.dt.float32, kind="ExternalOutput").ap()
    whole_program(nc, io, out)
    r = _run(nc, [arrays], core_ids=[0])
    return r.results[0]["out_0_dram"]
```
